# Optimizing a Trainium2 kernel written in Bass

```python
import jax, jax.numpy as jnp
from jax import lax
import numpy as np
import math

D_MODEL = 2048
BATCH = 1
SEQ = 256
DEPTH = 1

MIX_WIDTH = D_MODEL
ATTN_WIDTH = MIX_WIDTH // 2
LRU_WIDTH = MIX_WIDTH - ATTN_WIDTH
HEAD_DIM = 64
N_Q_HEADS = ATTN_WIDTH // HEAD_DIM
N_KV_HEADS = 4
Q_PER_KV = N_Q_HEADS // N_KV_HEADS
WINDOW = 128
BLOCK = 128
ROPE_THETA = 10000.0
LRU_BLOCK = 64
N_LRU_BLOCKS = LRU_WIDTH // LRU_BLOCK
CONV_WIDTH = 4
CONV_PAD_LEFT = 2
CONV_PAD_RIGHT = CONV_WIDTH - 1 - CONV_PAD_LEFT
LRU_C = 8.0
PEER_HEADS = 8
PEER_QDIM = 256
PEER_HALF = PEER_QDIM // 2
N_KEYS = 128
N_EXPERTS = N_KEYS * N_KEYS
PEER_TOPK = 16
PEER_CHUNK = 128
EPS = 1e-6
NEG = -1e30

Q_COLS = N_Q_HEADS * HEAD_DIM
KV_COLS = N_KV_HEADS * HEAD_DIM
IN_COLS = Q_COLS + 2 * KV_COLS + 2 * LRU_WIDTH


def rms_norm(x, g):
    xf = x.astype(jnp.float32)
    y = xf * lax.rsqrt(jnp.mean(xf * xf, axis=-1, keepdims=True) + EPS)
    return (y * g.astype(jnp.float32)).astype(x.dtype)

def rope(x, pos):
    half = HEAD_DIM // 2
    inv = ROPE_THETA ** (-jnp.arange(half, dtype=jnp.float32) / half)
    ang = pos.astype(jnp.float32)[:, None] * inv[None, :]
    cos = jnp.cos(ang)[None, :, None, :]
    sin = jnp.sin(ang)[None, :, None, :]
    xf = x.astype(jnp.float32)
    x1, x2 = xf[..., :half], xf[..., half:]
    return jnp.concatenate([x1 * cos - x2 * sin, x2 * cos + x1 * sin], axis=-1).astype(x.dtype)

def windowed_gqa_sink(q, k, v, sink):
    B, S = q.shape[0], q.shape[1]
    nb = S // BLOCK
    qb = q.reshape(B, nb, BLOCK, N_KV_HEADS, Q_PER_KV, HEAD_DIM)

    def band(t):
        tp = jnp.pad(t, ((0, 0), (BLOCK, BLOCK), (0, 0), (0, 0)))
        tp = tp.reshape(B, nb + 2, BLOCK, N_KV_HEADS, HEAD_DIM)
        return jnp.concatenate([tp[:, :-2], tp[:, 1:-1], tp[:, 2:]], axis=2)

    kb, vb = band(k), band(v)
    s = jnp.einsum('bnqgrd,bnkgd->bngrqk', qb, kb,
                   preferred_element_type=jnp.float32) * (HEAD_DIM ** -0.5)
    qpos = jnp.arange(nb)[:, None] * BLOCK + jnp.arange(BLOCK)[None, :]
    kpos = (jnp.arange(nb)[:, None] - 1) * BLOCK + jnp.arange(3 * BLOCK)[None, :]
    rel = kpos[:, None, :] - qpos[:, :, None]
    valid = (jnp.abs(rel) <= WINDOW) & (kpos[:, None, :] >= 0) & (kpos[:, None, :] < S)
    s = jnp.where(valid[None, :, None, None], s, NEG)
    sk = sink.astype(jnp.float32).reshape(1, 1, N_KV_HEADS, Q_PER_KV, 1, 1)
    m = jnp.maximum(jnp.max(s, axis=-1, keepdims=True), sk)
    p = jnp.exp(s - m)
    p = p / (jnp.sum(p, axis=-1, keepdims=True) + jnp.exp(sk - m))
    o = jnp.einsum('bngrqk,bnkgd->bnqgrd', p.astype(v.dtype), vb)
    return o.reshape(B, S, Q_COLS)

def centred_depthwise_conv(x, w, b):
    C = x.shape[-1]
    y = lax.conv_general_dilated(x, w.reshape(CONV_WIDTH, 1, C), window_strides=(1,),
                                 padding=[(CONV_PAD_LEFT, CONV_PAD_RIGHT)],
                                 dimension_numbers=('NWC', 'WIO', 'NWC'),
                                 feature_group_count=C)
    return y + b

def rg_lru(x, w_a, b_a, w_x, b_x, lam, reverse):
    B, S, _ = x.shape
    xb = x.reshape(B, S, N_LRU_BLOCKS, LRU_BLOCK)
    r = jax.nn.sigmoid(jnp.einsum('bshi,hij->bshj', xb, w_a).reshape(B, S, LRU_WIDTH) + b_a)
    i = jax.nn.sigmoid(jnp.einsum('bshi,hij->bshj', xb, w_x).reshape(B, S, LRU_WIDTH) + b_x)
    log_a = (-LRU_C * r.astype(jnp.float32)) * jax.nn.softplus(-lam.astype(jnp.float32))
    a = jnp.exp(log_a)
    u = jnp.sqrt(-jnp.expm1(2.0 * log_a)) * (i * x).astype(jnp.float32)

    def combine(left, right):
        a1, b1 = left
        a2, b2 = right
        return a1 * a2, a2 * b1 + b2

    _, h = lax.associative_scan(combine, (a, u), axis=1, reverse=reverse)
    return h.astype(x.dtype)

def peer(x, w_pq, sub_k1, sub_k2, u_emb, v_emb):
    B, S, D = x.shape
    T = B * S
    xt = x.reshape(T, D)
    q = (xt @ w_pq).reshape(T, PEER_HEADS, 2, PEER_HALF)
    s1 = jnp.einsum('thd,hkd->thk', q[:, :, 0], sub_k1, preferred_element_type=jnp.float32)
    s2 = jnp.einsum('thd,hkd->thk', q[:, :, 1], sub_k2, preferred_element_type=jnp.float32)
    v1, i1 = lax.top_k(s1, PEER_TOPK)
    v2, i2 = lax.top_k(s2, PEER_TOPK)
    cand = (v1[..., :, None] + v2[..., None, :]).reshape(T, PEER_HEADS, PEER_TOPK * PEER_TOPK)
    cidx = (i1[..., :, None] * N_KEYS + i2[..., None, :]).reshape(T, PEER_HEADS, PEER_TOPK * PEER_TOPK)
    sc, sel = lax.top_k(cand, PEER_TOPK)
    eidx = jnp.take_along_axis(cidx, sel, axis=-1)
    gates = jax.nn.softmax(sc, axis=-1)
    nc = T // PEER_CHUNK
    E = PEER_HEADS * PEER_TOPK

    def expert_chunk(args):
        xc, ic, gc = args
        uc = u_emb[ic]
        act = jax.nn.gelu(jnp.einsum('cd,ced->ce', xc, uc))
        vc = v_emb[ic]
        return jnp.einsum('ce,ced->cd', (gc * act).astype(vc.dtype), vc)

    out = lax.map(expert_chunk, (xt.reshape(nc, PEER_CHUNK, D),
                                 eidx.reshape(nc, PEER_CHUNK, E),
                                 gates.reshape(nc, PEER_CHUNK, E)))
    return out.reshape(B, S, D).astype(x.dtype)

def first_inputs(seed: int = 0) -> dict:
    key = jax.random.key(seed)
    ks = jax.random.split(key, 32)
    f32 = jnp.float32
    L = DEPTH

    def nrm(k, shape, scale):
        return jax.random.normal(k, shape, f32) * scale

    def gain(k, n):
        return 1.0 + 0.02 * jax.random.normal(k, (L, n), f32)

    def lam_init(k):
        a_c = jax.random.uniform(k, (L, LRU_WIDTH), f32, 0.9, 0.999)
        a = a_c ** (1.0 / LRU_C)
        return jnp.log(a) - jnp.log1p(-a)

    gs = LRU_BLOCK ** -0.5
    return {
        "x": jax.random.normal(ks[0], (BATCH, SEQ, D_MODEL), f32),
        "g_mix": gain(ks[1], D_MODEL),
        "w_in": nrm(ks[2], (L, D_MODEL, IN_COLS), D_MODEL ** -0.5),
        "sink": nrm(ks[3], (L, N_Q_HEADS), 0.5),
        "conv_w": nrm(ks[4], (L, CONV_WIDTH, LRU_WIDTH), CONV_WIDTH ** -0.5),
        "conv_b": nrm(ks[5], (L, LRU_WIDTH), 0.01),
        "fwd_wa": nrm(ks[6], (L, N_LRU_BLOCKS, LRU_BLOCK, LRU_BLOCK), gs),
        "fwd_ba": nrm(ks[7], (L, LRU_WIDTH), 0.01),
        "fwd_wx": nrm(ks[8], (L, N_LRU_BLOCKS, LRU_BLOCK, LRU_BLOCK), gs),
        "fwd_bx": nrm(ks[9], (L, LRU_WIDTH), 0.01),
        "fwd_lam": lam_init(ks[10]),
        "bwd_wa": nrm(ks[11], (L, N_LRU_BLOCKS, LRU_BLOCK, LRU_BLOCK), gs),
        "bwd_ba": nrm(ks[12], (L, LRU_WIDTH), 0.01),
        "bwd_wx": nrm(ks[13], (L, N_LRU_BLOCKS, LRU_BLOCK, LRU_BLOCK), gs),
        "bwd_bx": nrm(ks[14], (L, LRU_WIDTH), 0.01),
        "bwd_lam": lam_init(ks[15]),
        "g_attn_out": gain(ks[16], ATTN_WIDTH),
        "g_lru_out": gain(ks[17], LRU_WIDTH),
        "w_out": nrm(ks[18], (L, MIX_WIDTH, D_MODEL), MIX_WIDTH ** -0.5),
        "g_ffn": gain(ks[19], D_MODEL),
        "w_pq": nrm(ks[20], (L, D_MODEL, PEER_HEADS * PEER_QDIM), D_MODEL ** -0.5),
        "sub_k1": nrm(ks[21], (L, PEER_HEADS, N_KEYS, PEER_HALF), PEER_HALF ** -0.5),
        "sub_k2": nrm(ks[22], (L, PEER_HEADS, N_KEYS, PEER_HALF), PEER_HALF ** -0.5),
        "u_emb": nrm(ks[23], (L, N_EXPERTS, D_MODEL), D_MODEL ** -0.5),
        "v_emb": nrm(ks[24], (L, N_EXPERTS, D_MODEL), (PEER_HEADS * PEER_TOPK) ** -0.5),
        "g_final": 1.0 + 0.02 * jax.random.normal(ks[25], (D_MODEL,), f32),
    }

def first_block(x, g_mix, w_in, sink, conv_w, conv_b,
              fwd_wa, fwd_ba, fwd_wx, fwd_bx, fwd_lam,
              bwd_wa, bwd_ba, bwd_wx, bwd_bx, bwd_lam,
              g_attn_out, g_lru_out, w_out, g_ffn,
              w_pq, sub_k1, sub_k2, u_emb, v_emb, g_final):
    B, S, D = x.shape
    pos = jnp.arange(S)
    splits = [Q_COLS, Q_COLS + KV_COLS, Q_COLS + 2 * KV_COLS, Q_COLS + 2 * KV_COLS + LRU_WIDTH]
    for l in range(DEPTH):
        h = rms_norm(x, g_mix[l])
        proj = h @ w_in[l]
        q, k, v, x_gate, x_rec = jnp.split(proj, splits, axis=-1)
        q = rope(q.reshape(B, S, N_Q_HEADS, HEAD_DIM), pos)
        k = rope(k.reshape(B, S, N_KV_HEADS, HEAD_DIM), pos)
        v = v.reshape(B, S, N_KV_HEADS, HEAD_DIM)
        y_attn = windowed_gqa_sink(q, k, v, sink[l])

        c = centred_depthwise_conv(x_rec, conv_w[l], conv_b[l])
        h_rec = (rg_lru(c, fwd_wa[l], fwd_ba[l], fwd_wx[l], fwd_bx[l], fwd_lam[l], False)
                 + rg_lru(c, bwd_wa[l], bwd_ba[l], bwd_wx[l], bwd_bx[l], bwd_lam[l], True))
        y_lru = jax.nn.gelu(x_gate) * h_rec

        y = jnp.concatenate([rms_norm(y_attn, g_attn_out[l]), rms_norm(y_lru, g_lru_out[l])], axis=-1)
        x = x + y @ w_out[l]
        x = x + peer(rms_norm(x, g_ffn[l]), w_pq[l], sub_k1[l], sub_k2[l], u_emb[l], v_emb[l])
    return rms_norm(x, g_final)


MLA_HEADS = 8
Q_LORA = 512
KV_LORA = 512
QK_NOPE = 128
QK_ROPE = 64
V_DIM = 128
Q_BLOCK = 128
DIL_HEADS = 8
DIL_DIM = 128
DIL_PATTERNS = ((128, 1), (512, 4), (2048, 16))
DIL_BLOCK = 64
N_BRANCH = 2
D_FF = -(-8 * D_MODEL // (3 * 256)) * 256
RMS_EPS = 1e-6
NEG_INF = -1e30
D_IN = Q_LORA + KV_LORA + QK_ROPE + 3 * DIL_HEADS * DIL_DIM + N_BRANCH * D_MODEL


def rms_norm_2(x, g):
    xf = x.astype(jnp.float32)
    y = xf * lax.rsqrt(jnp.mean(xf * xf, axis=-1, keepdims=True) + RMS_EPS)
    return (y * g.astype(jnp.float32)).astype(x.dtype)

def rope_tables(seq):
    inv = ROPE_THETA ** (-jnp.arange(0, QK_ROPE, 2, dtype=jnp.float32) / QK_ROPE)
    ang = jnp.arange(seq, dtype=jnp.float32)[:, None] * inv[None, :]
    return jnp.cos(ang), jnp.sin(ang)

def apply_rope(x, cos, sin):
    x1, x2 = jnp.split(x, 2, axis=-1)
    c = cos.astype(x.dtype)
    s = sin.astype(x.dtype)
    return jnp.concatenate([x1 * c - x2 * s, x1 * s + x2 * c], axis=-1)

def alibi_slopes(n_heads):
    return jnp.power(2.0, -8.0 * jnp.arange(1, n_heads + 1, dtype=jnp.float32) / n_heads)

def mla_attention(q_nope, q_rope, k_nope, k_rope, v):
    B, S, H, _ = q_nope.shape
    nq = S // Q_BLOCK
    scale = (QK_NOPE + QK_ROPE) ** -0.5

    def to_blocks(t):
        return jnp.moveaxis(t.reshape(B, nq, Q_BLOCK, *t.shape[2:]), 1, 0)

    def attend(blk):
        qn, qr = blk
        s = (jnp.einsum('bqhd,bkhd->bhqk', qn, k_nope, preferred_element_type=jnp.float32)
             + jnp.einsum('bqhd,bkd->bhqk', qr, k_rope, preferred_element_type=jnp.float32)) * scale
        p = jax.nn.softmax(s, axis=-1).astype(v.dtype)
        return jnp.einsum('bhqk,bkhd->bqhd', p, v)

    o = lax.map(attend, (to_blocks(q_nope), to_blocks(q_rope)))
    return jnp.moveaxis(o, 0, 1).reshape(B, S, H, v.shape[-1])

def strided_band_attention(q, k, v, slopes, n_side, dil):
    B, S, H, D = q.shape
    L = S // dil
    nb = -(-L // DIL_BLOCK)
    Lp = nb * DIL_BLOCK

    def to_sub(t):
        return t.reshape(B, L, dil, H, D).transpose(0, 2, 1, 3, 4)

    qs = jnp.pad(to_sub(q), ((0, 0), (0, 0), (0, Lp - L), (0, 0), (0, 0)))
    qs = qs.reshape(B, dil, nb, DIL_BLOCK, H, D)

    def windows(t):
        tp = jnp.pad(to_sub(t), ((0, 0), (0, 0), (DIL_BLOCK, DIL_BLOCK + Lp - L), (0, 0), (0, 0)))
        tb = tp.reshape(B, dil, nb + 2, DIL_BLOCK, H, D)
        return jnp.concatenate([tb[:, :, :-2], tb[:, :, 1:-1], tb[:, :, 2:]], axis=3)

    kw = windows(k)
    vw = windows(v)

    qi = jnp.arange(DIL_BLOCK)[:, None]
    kj = jnp.arange(3 * DIL_BLOCK)[None, :]
    delta = kj - DIL_BLOCK - qi
    kpos = (jnp.arange(nb)[:, None] - 1) * DIL_BLOCK + jnp.arange(3 * DIL_BLOCK)[None, :]
    valid = (jnp.abs(delta) <= n_side)[None] & ((kpos >= 0) & (kpos < L))[:, None, :]
    bias = -slopes[:, None, None] * (dil * jnp.abs(delta)).astype(jnp.float32)[None]

    s = jnp.einsum('bcnqhd,bcnkhd->bcnhqk', qs, kw, preferred_element_type=jnp.float32) * (D ** -0.5)
    s = jnp.where(valid[:, None], s + bias, NEG_INF)
    m = jnp.max(s, axis=-1, keepdims=True)
    p = jnp.exp(s - m)
    l = jnp.sum(p, axis=-1)
    o = jnp.einsum('bcnhqk,bcnkhd->bcnqhd', p.astype(v.dtype), vw).astype(jnp.float32)
    o = o / jnp.swapaxes(l, -1, -2)[..., None]
    lse = jnp.swapaxes(m[..., 0] + jnp.log(l), -1, -2)

    o = o.reshape(B, dil, Lp, H, D)[:, :, :L].transpose(0, 2, 1, 3, 4).reshape(B, S, H, D)
    lse = lse.reshape(B, dil, Lp, H)[:, :, :L].transpose(0, 2, 1, 3).reshape(B, S, H)
    return o, lse

def dilated_attention(q, k, v):
    slopes = alibi_slopes(q.shape[2])
    outs, lses = [], []
    for window, dil in DIL_PATTERNS:
        o, lse = strided_band_attention(q, k, v, slopes, window // (2 * dil), dil)
        outs.append(o)
        lses.append(lse)
    w = jax.nn.softmax(jnp.stack(lses), axis=0)
    o = sum(w[g][..., None] * outs[g] for g in range(len(DIL_PATTERNS)))
    return o.astype(v.dtype)

def hybrid_layer(x, cos, sin, g_mix, w_in, b_gate, g_cq, w_uq, g_ckv, w_ukv,
                 g_q_nope, g_q_rope, g_k_nope, g_k_rope, g_q_dil, g_k_dil,
                 w_o_mla, w_o_dil, w_o, g_ffn, w_gate_up, w_down):
    B, S, _ = x.shape
    h = rms_norm_2(x, g_mix)
    proj = h @ w_in
    dh = DIL_HEADS * DIL_DIM
    cuts = np.cumsum([Q_LORA, KV_LORA, QK_ROPE, dh, dh, dh]).tolist()
    c_q, c_kv, k_r, q_d, k_d, v_d, gate = jnp.split(proj, cuts, axis=-1)

    q = (rms_norm_2(c_q, g_cq) @ w_uq).reshape(B, S, MLA_HEADS, QK_NOPE + QK_ROPE)
    q_nope, q_rope = jnp.split(q, [QK_NOPE], axis=-1)
    q_nope = rms_norm_2(q_nope, g_q_nope)
    q_rope = apply_rope(rms_norm_2(q_rope, g_q_rope), cos[:, None, :], sin[:, None, :])
    kv = (rms_norm_2(c_kv, g_ckv) @ w_ukv).reshape(B, S, MLA_HEADS, QK_NOPE + V_DIM)
    k_nope, v_a = jnp.split(kv, [QK_NOPE], axis=-1)
    k_nope = rms_norm_2(k_nope, g_k_nope)
    k_rope = apply_rope(rms_norm_2(k_r, g_k_rope), cos, sin)
    o_a = mla_attention(q_nope, q_rope, k_nope, k_rope, v_a)
    y_a = o_a.reshape(B, S, MLA_HEADS * V_DIM) @ w_o_mla

    qd = rms_norm_2(q_d.reshape(B, S, DIL_HEADS, DIL_DIM), g_q_dil)
    kd = rms_norm_2(k_d.reshape(B, S, DIL_HEADS, DIL_DIM), g_k_dil)
    vd = v_d.reshape(B, S, DIL_HEADS, DIL_DIM)
    o_b = dilated_attention(qd, kd, vd)
    y_b = o_b.reshape(B, S, dh) @ w_o_dil

    g = jax.nn.sigmoid((gate + b_gate).astype(jnp.float32)).astype(x.dtype)
    g = g.reshape(B, S, N_BRANCH, D_MODEL)
    x = x + (g[:, :, 0] * y_a + g[:, :, 1] * y_b) @ w_o

    gt, up = jnp.split(rms_norm_2(x, g_ffn) @ w_gate_up, 2, axis=-1)
    return x + (jax.nn.silu(gt) * up) @ w_down

def second_inputs(seed: int = 0) -> dict:
    key = jax.random.key(seed)
    ks = jax.random.split(key, 22)

    def dense(k, fan_in, fan_out):
        return jax.random.normal(k, (DEPTH, fan_in, fan_out), jnp.float32) * fan_in ** -0.5

    def gain(k, n):
        return 1.0 + 0.05 * jax.random.normal(k, (DEPTH, n), jnp.float32)

    return {
        "x": jax.random.normal(ks[0], (BATCH, SEQ, D_MODEL), jnp.float32),
        "g_mix": gain(ks[1], D_MODEL),
        "w_in": dense(ks[2], D_MODEL, D_IN),
        "b_gate": 0.02 * jax.random.normal(ks[3], (DEPTH, N_BRANCH * D_MODEL), jnp.float32),
        "g_cq": gain(ks[4], Q_LORA),
        "w_uq": dense(ks[5], Q_LORA, MLA_HEADS * (QK_NOPE + QK_ROPE)),
        "g_ckv": gain(ks[6], KV_LORA),
        "w_ukv": dense(ks[7], KV_LORA, MLA_HEADS * (QK_NOPE + V_DIM)),
        "g_q_nope": gain(ks[8], QK_NOPE),
        "g_q_rope": gain(ks[9], QK_ROPE),
        "g_k_nope": gain(ks[10], QK_NOPE),
        "g_k_rope": gain(ks[11], QK_ROPE),
        "g_q_dil": gain(ks[12], DIL_DIM),
        "g_k_dil": gain(ks[13], DIL_DIM),
        "w_o_mla": dense(ks[14], MLA_HEADS * V_DIM, D_MODEL),
        "w_o_dil": dense(ks[15], DIL_HEADS * DIL_DIM, D_MODEL),
        "w_o": dense(ks[16], D_MODEL, D_MODEL),
        "g_ffn": gain(ks[17], D_MODEL),
        "w_gate_up": dense(ks[18], D_MODEL, 2 * D_FF),
        "w_down": dense(ks[19], D_FF, D_MODEL),
    }

def second_block(x, g_mix, w_in, b_gate, g_cq, w_uq, g_ckv, w_ukv,
              g_q_nope, g_q_rope, g_k_nope, g_k_rope, g_q_dil, g_k_dil,
              w_o_mla, w_o_dil, w_o, g_ffn, w_gate_up, w_down):
    cos, sin = rope_tables(x.shape[1])
    for i in range(DEPTH):
        x = hybrid_layer(x, cos, sin, g_mix[i], w_in[i], b_gate[i], g_cq[i], w_uq[i],
                         g_ckv[i], w_ukv[i], g_q_nope[i], g_q_rope[i], g_k_nope[i],
                         g_k_rope[i], g_q_dil[i], g_k_dil[i], w_o_mla[i], w_o_dil[i],
                         w_o[i], g_ffn[i], w_gate_up[i], w_down[i])
    return x


def setup_inputs(seed=0):
    out = dict(first_inputs(seed))
    for name, value in second_inputs(seed + 1).items():
        if name != "x":
            out[name + "_2"] = value
    return out


def reference(
    x, g_mix, w_in, sink, conv_w, conv_b, fwd_wa, fwd_ba, fwd_wx, fwd_bx, fwd_lam, bwd_wa,
    bwd_ba, bwd_wx, bwd_bx, bwd_lam, g_attn_out, g_lru_out, w_out, g_ffn, w_pq, sub_k1, sub_k2,
    u_emb, v_emb, g_final, g_mix_2, w_in_2, b_gate_2, g_cq_2, w_uq_2, g_ckv_2, w_ukv_2,
    g_q_nope_2, g_q_rope_2, g_k_nope_2, g_k_rope_2, g_q_dil_2, g_k_dil_2, w_o_mla_2, w_o_dil_2,
    w_o_2, g_ffn_2, w_gate_up_2, w_down_2,
):
    x = first_block(
        x, g_mix, w_in, sink, conv_w, conv_b, fwd_wa, fwd_ba, fwd_wx, fwd_bx, fwd_lam, bwd_wa,
        bwd_ba, bwd_wx, bwd_bx, bwd_lam, g_attn_out, g_lru_out, w_out, g_ffn, w_pq, sub_k1,
        sub_k2, u_emb, v_emb, g_final,
    )
    return second_block(
        x, g_mix_2, w_in_2, b_gate_2, g_cq_2, w_uq_2, g_ckv_2, w_ukv_2, g_q_nope_2, g_q_rope_2,
        g_k_nope_2, g_k_rope_2, g_q_dil_2, g_k_dil_2, w_o_mla_2, w_o_dil_2, w_o_2, g_ffn_2,
        w_gate_up_2, w_down_2,
    )


_drawn_inputs = setup_inputs


def setup_inputs(seed=0):
    import zlib

    import numpy as np

    out = dict(_drawn_inputs(seed))
    spreads = {}
    factors = {'sink': 8.0,
     'fwd_ba': 8.0,
     'fwd_bx': 8.0,
     'bwd_ba': 8.0,
     'bwd_bx': 8.0,
     'g_attn_out': 4.418,
     'g_lru_out': 5.018,
     'g_ffn': 8.0,
     'g_mix_2': 2.932,
     'b_gate_2': 8.0,
     'g_cq_2': 8.0,
     'g_ckv_2': 6.142,
     'g_q_nope_2': 8.0,
     'g_q_rope_2': 8.0,
     'g_k_nope_2': 8.0,
     'g_k_rope_2': 8.0,
     'g_q_dil_2': 8.0,
     'g_k_dil_2': 8.0,
     'g_ffn_2': 5.591}
    for name, (base, spread) in spreads.items():
        noise = np.random.default_rng([zlib.crc32(name.encode()), seed]).standard_normal(out[name].shape)
        drawn = base * np.exp(spread * noise) if base else spread * noise
        out[name] = __import__('jax').numpy.asarray(drawn.astype(out[name].dtype))
    for name, factor in factors.items():
        out[name] = (out[name] * factor).astype(out[name].dtype)
    return out
```

```python
from contextlib import ExitStack
import math

import numpy as np
import concourse.bass as bass
from concourse import mybir

F32 = mybir.dt.float32
F32R = mybir.dt.float32r
U32 = mybir.dt.uint32
ALU = mybir.AluOpType
ACT = mybir.ActivationFunctionType
AX = mybir.AxisListType

P = 128
S = 256
NB = S // P
D = 2048
KT = D // P
WCH = 2048
BANK = 512

HD = 64
NQ, NKV = 16, 4
AW = NQ * HD
LW = 1024
LT = LW // P
N_KEYS = 128
PH = 8
TOPK = 16
NE = PH * TOPK
NOPE, ROPE, VD = 128, 64, 128
H2 = 8
QL = 512
QLT = QL // P
FF = 5632
FT = FF // P
FF_PARTS = (24, 20)
EPS = 1e-6
NEG = -1e30

COLS = [("conv_w", 4 * LT), ("conv_b", LT), ("fwd_ba", LT), ("fwd_bx", LT), ("fwd_lam", LT),
        ("bwd_ba", LT), ("bwd_bx", LT), ("bwd_lam", LT), ("g_lru_out", LT), ("b_gate_2", 2 * KT)]
ROWS = [("sink", NQ), ("g_q_nope_2", NOPE), ("g_q_rope_2", ROPE), ("g_k_nope_2", NOPE),
        ("g_k_rope_2", ROPE), ("g_q_dil_2", 128), ("g_k_dil_2", 128), ("iota16", TOPK)]


def offsets(table):
    at, out = 0, {}
    for name, n in table:
        out[name] = (at, n)
        at += n
    return out, at


COL_AT, N_COLS = offsets(COLS)
ROW_AT, N_ROWS = offsets(ROWS)


class Engine:

    def __init__(self, sem, chained=False):
        self.sem, self.count, self.steps, self.met = sem, 0, [], {}
        self.chained = chained

    def wait(self, *marks):
        for m in marks:
            if m is None:
                continue
            if isinstance(m, list):
                self.wait(*m)
                continue
            sem, value = m
            if self.met.get(sem.name, 0) < value:
                self.met[sem.name] = value
                self.steps.append(lambda e, sem=sem, value=value: e.wait_ge(sem, value))

    def do(self, fn, *after):
        self.wait(*after)
        if self.chained and self.count:
            self.wait((self.sem, self.count))
        self.count += 1
        self.steps.append(lambda e: fn(e).then_inc(self.sem, 1))
        return (self.sem, self.count)

    def quiet(self, fn, *after):
        self.wait(*after)
        self.steps.append(fn)

    def mark(self):
        return (self.sem, self.count)

    def dma(self, out, in_, counter, *after):
        self.wait(*after)
        counter[1] += 16
        self.steps.append(lambda e: e.dma_start(out, in_).then_inc(counter[0], 16))
        return (counter[0], counter[1])

    def play(self, e):
        for step in self.steps:
            step(e)


def weave(main, side, every=1):
    n, alive = 0, True
    for _ in main:
        n += 1
        if alive and n % every == 0:
            alive = next(side, "end") != "end"
    for _ in side:
        pass


def build(nc, A, out, dump=None):
    ctx = ExitStack()
    with ctx:
        def sem(name):
            return ctx.enter_context(nc.semaphore(name))

        pe, sp = Engine(sem("pe_done")), Engine(None)
        act, dve, pool = (Engine(sem(n), chained=True) for n in ("act_done", "dve_done", "pool_done"))

        base = (nc.sbuf_base + 63) // 64 * 64
        used = {}

        def at(name, offset, shape, dt=F32):
            size = 4 * int(np.prod(shape[1:]))
            used[name] = (offset, offset + size)
            assert base + offset + size <= nc.sbuf_usable_end, (name, offset, size)
            return nc.alloc_sbuf_tensor_at(name, shape, dt, offset=base + offset)

        KB = 1024
        x = at("x", 0, [P, NB, D])
        o = 16 * KB
        ident = at("ident", o, [P, P]); o += 4 * P
        cols = at("cols", o, [P, N_COLS]); o += 4 * N_COLS
        rows = at("rows", o, [P, N_ROWS]); o += 4 * N_ROWS
        rope_t = at("rope_t", o, [P, NB, 2, 64]); o += 4 * NB * 128
        small = at("small", o, [P, 640]); o += 4 * 640
        SCR = (o + 63) // 64 * 64
        HHL = SCR + 24 * KB
        WR = HHL + 32 * KB
        PH0 = WR + 64 * KB
        xn = at("xn", SCR, [P, NB, D])
        g_row = at("g_row", SCR + 16 * KB, [P, D])
        h_hi = at("h_hi", HHL, [P, KT, S], F32R)
        h_lo = at("h_lo", HHL + 16 * KB, [P, KT, S], F32R)
        N_RAW, N_SPLIT = 2, 3
        w_raw = [at(f"w_raw{i}", WR + 8 * KB * i, [P, WCH]) for i in range(N_RAW)]
        w_hi = [at(f"w_hi{i}", WR + 8 * KB * (N_RAW + i), [P, WCH], F32R) for i in range(N_SPLIT)]
        w_lo = [at(f"w_lo{i}", WR + 8 * KB * (N_RAW + N_SPLIT + i), [P, WCH], F32R) for i in range(N_SPLIT)]

        def col(name, i=0):
            a = COL_AT[name][0] + i
            return cols[:, a:a + 1]

        def row(name):
            a, n = ROW_AT[name]
            return rows[:, a:a + n]

        small_at = [0]

        def columns(n):
            a = small_at[0]
            small_at[0] += n
            assert small_at[0] <= 640, small_at
            return small[:, a:a + n]

        psum = [ctx.enter_context(nc.psum_tensor(f"bank{i}", [P, BANK], F32)) for i in range(8)]
        bank_free = [[] for _ in range(8)]
        turn = {"main": 0, "side": 0}

        def take(kind, n=None):
            i = turn[kind] % 4 + (0 if kind == "main" else 4)
            turn[kind] += 1
            return i

        def pe_wait_bank(i):
            pe.wait(bank_free[i])
            bank_free[i] = []

        const_sem = [sem("consts"), 0]
        for t, name in ((ident, "ident"), (cols, "cols"), (rows, "rows"), (rope_t, "rope1")):
            sp.dma(t[:], A[name], const_sem)
        x_sem = [sem("x_in"), 0]
        gain_sem = [sem("gains"), 0]
        x_in = sp.dma(x[:], A["x"], x_sem)
        consts_in = (const_sem[0], const_sem[1])

        def load_gain(name, *after):
            return sp.dma(g_row[:], A[name], gain_sem, *after)

        class Weights:
            raw_sem = [[sem(f"w_raw_in{i}"), 0] for i in range(N_RAW)]

            def __init__(self, chunks):
                self.chunks, self.n_load, self.n_split, self.n_used = chunks, 0, 0, 0
                self.raw_free = [[] for _ in range(N_RAW)]
                self.split_free = [[] for _ in range(N_SPLIT)]
                self.loaded, self.ready = {}, {}

            def load(self):
                i = self.n_load
                if i >= len(self.chunks):
                    return
                self.n_load += 1
                s = i % N_RAW
                src = self.chunks[i]
                n = src.shape[-1]
                self.loaded[i] = sp.dma(w_raw[s][:, 0:n], src, self.raw_sem[s], self.raw_free[s])

            def split(self):
                i = self.n_split
                if i >= len(self.chunks):
                    return
                while self.n_load <= i:
                    self.load()
                self.n_split += 1
                s, r, n = i % N_SPLIT, i % N_RAW, self.chunks[i].shape[-1]
                hi, lo, raw = w_hi[s][:, 0:n], w_lo[s][:, 0:n], w_raw[r][:, 0:n]
                a = act.do(lambda e: e.activation(hi, raw, ACT.Copy), self.loaded[i], self.split_free[s])
                b = dve.do(lambda e: e.tensor_tensor(lo, raw, hi.bitcast(F32), ALU.subtract),
                           self.loaded[i], a, self.split_free[s])
                self.raw_free[r] = [a, b]
                self.ready[i] = b
                self.load()

            def next(self, ahead=N_SPLIT - 1):
                i = self.n_used
                self.n_used += 1
                while self.n_split < min(i + 1 + ahead, len(self.chunks)):
                    self.split()
                self.now = i % N_SPLIT
                return w_hi[self.now], w_lo[self.now], self.ready[i]

            def used(self, mark):
                self.split_free[self.now] = [mark]

        def three(psum_ap, st, mv, first, last):
            pe.quiet(lambda e: e.matmul(psum_ap, st[0], mv[0], start=first, stop=False))
            pe.quiet(lambda e: e.matmul(psum_ap, st[0], mv[1], start=False, stop=False))
            return lambda e: e.matmul(psum_ap, st[1], mv[0], start=False, stop=last)

        def gemm_rows(ws, a_hi, a_lo, ready, tiles, n_out, consume, width=BANK):
            per = WCH // width
            for n in range(n_out):
                banks = [take("main") for _ in range(NB)]
                for b in banks:
                    pe_wait_bank(b)
                c0 = 0
                while c0 < tiles:
                    k_here = min(per, tiles - c0)
                    hi, lo, split = ws.next()
                    pe.wait(ready, split)
                    for b in range(NB):
                        for k in range(k_here):
                            t = c0 + k
                            last = t == tiles - 1
                            cut = slice(k * width, (k + 1) * width)
                            tok = slice(b * P, (b + 1) * P)
                            fin = three(psum[banks[b]][:, 0:width], (a_hi[:, t, tok], a_lo[:, t, tok]),
                                        (hi[:, cut], lo[:, cut]), t == 0, last)
                            if k == k_here - 1 and (b == NB - 1 or last):
                                mark = pe.do(fin)
                            else:
                                pe.quiet(fin)
                            if last:
                                done = mark
                                bank_free[banks[b]] = consume(n, b, psum[banks[b]][:, 0:width], done)
                    ws.used(mark)
                    c0 += k_here
                    yield

        def gemm_cols(ws, a_hi, a_lo, ready, tiles, n_out, consume):
            per = WCH // (P * tiles)
            for n in range(n_out):
                if n % per == 0:
                    hi, lo, split = ws.next()
                b = take("main")
                pe_wait_bank(b)
                pe.wait(ready, split)
                for t in range(tiles):
                    cut = slice(((n % per) * tiles + t) * P, ((n % per) * tiles + t + 1) * P)
                    fin = three(psum[b][:, 0:S], (hi[:, cut], lo[:, cut]), (a_hi[:, t, :], a_lo[:, t, :]),
                                t == 0, t == tiles - 1)
                    if t == tiles - 1:
                        mark = pe.do(fin)
                    else:
                        pe.quiet(fin)
                if n % per == per - 1 or n == n_out - 1:
                    ws.used(mark)
                bank_free[b] = consume(n, psum[b][:, 0:S], mark)
                yield

        def power_mean(ss, n, width, *after):
            v, half, r = columns(n), columns(n), columns(n)
            m = dve.do(lambda e: e.tensor_scalar(v, ss, 1.0 / width, EPS, ALU.mult, ALU.add), *after)
            k = pool.do(lambda e: e.memset(half, -0.5))
            return r, pool.do(lambda e: e.tensor_tensor(r, v, half, ALU.pow), m, k)

        def norm_rows(src, dst, gain, width, *after):
            marks = []
            for b in range(NB):
                ss = columns(1)
                m = act.do(lambda e, b=b, ss=ss: e.activation(dst(b), src(b), ACT.Square, accum_out=ss), *after)
                r, m = power_mean(ss, 1, width, m)
                marks.append(dve.do(lambda e, b=b, r=r: e.scalar_tensor_tensor(
                    out=dst(b), in0=src(b), scalar=r, in1=gain, op0=ALU.mult, op1=ALU.mult), m))
            return marks

        def flip(src, hi, lo, tiles, marks, free=None, plain=None):
            out_marks = []
            for b in range(NB):
                for t0 in range(0, tiles, 4):
                    n = min(4, tiles - t0)
                    i = take("side")
                    pe_wait_bank(i)
                    pe.wait(marks[b])
                    for k in range(n):
                        fn = lambda e, k=k, i=i, t0=t0, b=b: e.transpose(
                            psum[i][:, k * P:(k + 1) * P], src(b, t0 + k), ident[:])
                        m = pe.do(fn) if k == n - 1 else pe.quiet(fn)
                    got = psum[i][:, 0:n * P].rearrange("p (k q) -> p k q", q=P)
                    tok = slice(b * P, (b + 1) * P)
                    if plain is not None:
                        a = act.do(lambda e, got=got, t0=t0, n=n, tok=tok: e.activation(
                            plain[:, t0:t0 + n, tok], got, ACT.Copy), m, free)
                        bank_free[i] = [a]
                        out_marks.append(a)
                        continue
                    a = act.do(lambda e, got=got, t0=t0, n=n, tok=tok: e.activation(
                        hi[:, t0:t0 + n, tok], got, ACT.Copy), m, free)
                    d = dve.do(lambda e, got=got, t0=t0, n=n, tok=tok: e.tensor_tensor(
                        lo[:, t0:t0 + n, tok], got, hi[:, t0:t0 + n, tok].bitcast(F32), ALU.subtract), a)
                    bank_free[i] = [a, d]
                    out_marks.append(d)
            return out_marks

        def flip_steps(result, *args, **kw):
            result.extend(flip(*args, **kw))
            yield

        def attention(score, scale, bias, sink, value, dv, dst, sbuf_s, sbuf_pt, state, ready):
            pe.wait(ready)
            halves = []
            for pair in range(2):
                i = take("side")
                pe_wait_bank(i)
                for j in (pair, pair + 2):
                    fn = score(j, psum[i][:, (j // 2) * S:(j // 2 + 1) * S])
                    m = pe.do(fn) if j > 1 else pe.quiet(fn)
                halves.append((i, m))
            got = []
            for pair, (i, m) in enumerate(halves):
                d = bias(sbuf_s, pair, psum[i], m, state["s_free"])
                bank_free[i] = [d]
                got.append(d)
            yield
            top, neg, tot, rec = columns(4), columns(4), columns(4), columns(4)
            m = dve.do(lambda e: e.tensor_reduce(top, sbuf_s[:], AX.X, ALU.max), got)
            if sink is not None:
                top2 = columns(4)
                m = dve.do(lambda e: e.tensor_tensor(top2, top, sink, ALU.max), m)
            else:
                top2 = top
            m = dve.do(lambda e: e.tensor_scalar(neg, top2, -1.0, None, ALU.mult), m)
            es = None
            for j in range(4):
                es = act.do(lambda e, j=j: e.activation(sbuf_s[:, j, :], sbuf_s[:, j, :], ACT.Exp,
                                                        bias=neg[:, j:j + 1], accum_out=tot[:, j:j + 1]), m)
            if sink is not None:
                away, ex, tot2 = columns(4), columns(4), columns(4)
                m = dve.do(lambda e: e.tensor_tensor(away, sink, neg, ALU.add), m)
                m = act.do(lambda e: e.activation(ex, away, ACT.Exp), m)
                m = dve.do(lambda e: e.tensor_tensor(tot2, tot, ex, ALU.add), m, es)
            else:
                tot2, m = tot, es
            inv = dve.do(lambda e: e.reciprocal(rec, tot2), m, es)
            yield
            copies = []
            for pair in range(2):
                i = take("side")
                pe_wait_bank(i)
                pe.wait(es)
                for k in range(4):
                    j, kb = 2 * pair + k // 2, k % 2
                    fn = lambda e, k=k, j=j, kb=kb, i=i: e.transpose(
                        psum[i][:, k * P:(k + 1) * P], sbuf_s[:, j, kb * P:(kb + 1) * P], ident[:])
                    m = pe.do(fn) if k == 3 else pe.quiet(fn)
                dst_pt = sbuf_pt[:, 2 * pair:2 * pair + 2, :, :].rearrange("p j k q -> p (j k q)")
                if pair == 0:
                    c = act.do(lambda e, i=i, d=dst_pt: e.activation(d, psum[i][:], ACT.Copy), m, state["pt_free"])
                else:
                    c = dve.do(lambda e, i=i, d=dst_pt: e.tensor_copy(d, psum[i][:]), m, state["pt_free"])
                bank_free[i] = [c]
                copies.append(c)
            state["s_free"] = [m]
            yield
            i = take("side")
            pe_wait_bank(i)
            pe.wait(copies)
            for j in range(4):
                for kb in range(2):
                    fn = lambda e, j=j, kb=kb: e.matmul(psum[i][:, j * dv:(j + 1) * dv], sbuf_pt[:, j, kb, :],
                                                        value(j, kb), start=kb == 0, stop=kb == 1)
                    m = pe.do(fn) if (j, kb) == (3, 1) else pe.quiet(fn)
            state["pt_free"] = [m]
            o_ps = psum[i][:, 0:4 * dv].rearrange("p (j d) -> p j d", j=4)
            d = dve.do(lambda e: e.tensor_tensor(dst, o_ps, rec.unsqueeze(2).broadcast_to([P, 4, dv]), ALU.mult),
                       m, inv)
            bank_free[i] = [d]
            state["out"].append(d)
            yield

        def rope_rows(src, dst, heads, b, tmp, ready, bank_mark=None):
            cos = rope_now[:, b, 0, :].unsqueeze(1).broadcast_to([P, heads, 64])
            sin = rope_now[:, b, 1, :].unsqueeze(1).broadcast_to([P, heads, 64])
            t0, t1 = tmp
            a = dve.do(lambda e: e.tensor_tensor(t0, src, cos, ALU.mult), ready)
            dve.do(lambda e: e.tensor_tensor(t1[:, :, 0:32], src[:, :, 32:64], sin[:, :, 0:32], ALU.mult), ready)
            c = dve.do(lambda e: e.tensor_tensor(t1[:, :, 32:64], src[:, :, 0:32], sin[:, :, 32:64], ALU.mult))
            return c, dve.do(lambda e: e.tensor_tensor(dst, t0, t1, ALU.add), a, c)

        rope_now = rope_t

        def show(name, ap, mark):
            if dump is not None:
                dump(nc, sp, name, ap, [pe.mark(), act.mark(), dve.mark(), pool.mark(), mark])

        gain = load_gain("g_mix")
        marks = norm_rows(lambda b: x[:, b, :], lambda b: xn[:, b, :], g_row[:], D, x_in, gain, consts_in)
        h_ready = flip(lambda b, t: xn[:, b, t * P:(t + 1) * P], h_hi, h_lo, KT, marks)

        o = PH0
        q_rows = at("q_rows", o, [P, NB, AW])
        k_rows = at("k_rows", o + 8 * KB, [P, NB, NKV, 2, HD])
        v_rows = at("v_rows", o + 12 * KB, [P, NB, NKV, HD])
        q_cols = at("q_cols", o + 14 * KB, [P, NQ // 2, S])
        k_cols = at("k_cols", o + 22 * KB, [P, NKV, S])
        s_buf = at("s_buf", o + 26 * KB, [P, 4, S])
        pt_buf = at("pt_buf", o + 30 * KB, [P, 4, 2, P])
        c_cols = at("c_cols", o + 34 * KB, [P, LT, S])
        h_sum = at("h_sum", o + 42 * KB, [P, LT, S])
        gate_c = at("gate_c", o + 50 * KB, [P, LT, S])
        window = at("window", o + 58 * KB, [P, 384])
        lru_w = [at(f"lru_w{i}", o + 59 * KB + 512 + 2 * KB * i, [P, 4, P]) for i in range(2)]
        half = [at(f"lru_half{i}", SCR + 4 * KB * i, [P, LT // 2, S]) for i in range(4)]
        rope_tmp = [at(f"rope_tmp{i}", o + 34 * KB + 2 * KB * i, [P, 8, 64]) for i in range(2)]
        sp_sm = at("softplus", o + 63 * KB + 512, [P, 8, LT])

        win_sem = [sem("window_in"), 0]
        win_in = sp.dma(window[:], A["window"], win_sem)
        ws = Weights([A["w1_qkv"][i] for i in range(12)] + [A["w1_rec"][i] for i in range(8)]
                     + [A["w1_gate"][i] for i in range(8)] + [A["w1_out"][i] for i in range(16)]
                     + [A["w1_pq"][i] for i in range(16)])
        for _ in range(N_RAW):
            ws.load()

        qkv_marks = {"q": [[], []], "k": [[], []], "v": []}

        def take_qkv(n, b, ps, m):
            if n < 2:
                src = ps.rearrange("p (h d) -> p h d", d=HD)
                dst = q_rows[:, b, n * 512:(n + 1) * 512].rearrange("p (h d) -> p h d", d=HD)
                c, r = rope_rows(src, dst, 8, b, [t[:] for t in rope_tmp], m)
                qkv_marks["q"][b].append(r)
                return [c]
            src = ps[:, 0:256].rearrange("p (h d) -> p h d", d=HD)
            c, r = rope_rows(src, k_rows[:, b, :, 0, :], NKV, b, [t[:, 0:NKV, :] for t in rope_tmp], m)
            r2 = dve.do(lambda e: e.tensor_copy(k_rows[:, b, :, 1, :], k_rows[:, b, :, 0, :]), r)
            qkv_marks["k"][b].append(r2)
            v = dve.do(lambda e: e.tensor_copy(v_rows[:, b, :, :].rearrange("p h d -> p (h d)"), ps[:, 256:512]))
            qkv_marks["v"].append(v)
            return [c, v]

        for _ in gemm_rows(ws, h_hi, h_lo, h_ready, KT, 3, take_qkv):
            pass

        att = {"s_free": [], "pt_free": [], "out": []}

        def attention_1():
            ready = flip(lambda b, t: q_rows[:, b, t * P:(t + 1) * P], None, None, NQ // 2,
                         qkv_marks["q"], plain=q_cols)
            yield
            ready += flip(lambda b, t: k_rows[:, b, t, :, :].rearrange("p a d -> p (a d)"), None, None, NKV,
                          qkv_marks["k"], plain=k_cols)
            ready += qkv_marks["v"] + [win_in]
            yield
            for b in range(NB):
                for g in range(NKV):
                    def score(j, ps, g=g, b=b):
                        hh = 4 * g + j
                        at_p = slice(HD * (hh % 2), HD * (hh % 2) + HD)
                        return lambda e: e.matmul(ps, q_cols[at_p, hh // 2, b * P:(b + 1) * P],
                                                  k_cols[at_p, g, :], start=True, stop=True)

                    def bias(sb, pair, ps, m, free, b=b):
                        mask = window[:, (1 - b) * P:(1 - b) * P + S].unsqueeze(1).broadcast_to([P, 2, S])
                        return dve.do(lambda e: e.scalar_tensor_tensor(
                            out=sb[:, pair::2, :], in0=ps[:].rearrange("p (j s) -> p j s", j=2),
                            scalar=HD ** -0.5, in1=mask, op0=ALU.mult, op1=ALU.add), m, free, win_in)

                    yield from attention(
                        score, 1.0, bias, row("sink")[:, 4 * g:4 * g + 4],
                        lambda j, kb, g=g: v_rows[:, kb, g, :], HD,
                        q_rows[:, b, 256 * g:256 * g + 256].rearrange("p (j d) -> p j d", j=4),
                        s_buf, pt_buf, att, ready)

        rec_marks = []

        def take_rec(n, ps, m):
            def tap(w):
                return col("conv_w", w * LT + n)
            c = c_cols[:, n, :]
            m = act.do(lambda e: e.activation(c, ps, ACT.Identity, bias=col("conv_b", n), scale=tap(2)),
                       m, rope_done)
            for w, out_at, in_at in ((0, slice(2, S), slice(0, S - 2)), (1, slice(1, S), slice(0, S - 1)),
                                     (3, slice(0, S - 1), slice(1, S))):
                m = dve.do(lambda e, w=w, o_=out_at, i_=in_at: e.scalar_tensor_tensor(
                    out=c[:, o_], in0=ps[:, i_], scalar=tap(w), in1=c[:, o_], op0=ALU.mult, op1=ALU.add), m)
            rec_marks.append(m)
            return [m]

        rope_done = dve.mark()

        def take_gate(n, ps, m):
            m = act.do(lambda e: e.activation(gate_c[:, n, :], ps, ACT.Gelu_apprx_tanh), m)
            gate_marks.append(m)
            return [m]

        gate_marks, lru_marks = [], []
        lru_w_sem = [[sem(f"lru_w_in{i}"), 0] for i in range(2)]

        def softplus(d):
            lam = cols[:, COL_AT[("fwd_lam", "bwd_lam")[d]][0]:][:, 0:LT]
            t = [sp_sm[:, 4 * d + i, :] for i in range(4)]
            m = act.do(lambda e: e.activation(t[0], lam, ACT.Abs), consts_in)
            m = act.do(lambda e: e.activation(t[0], t[0], ACT.Exp, scale=-1.0), m)
            m = dve.do(lambda e: e.tensor_scalar(t[0], t[0], 1.0, None, ALU.add), m)
            m = act.do(lambda e: e.activation(t[0], t[0], ACT.Ln), m)
            n = dve.do(lambda e: e.tensor_scalar(t[1], lam, -1.0, 0.0, ALU.mult, ALU.max), consts_in)
            m = dve.do(lambda e: e.tensor_tensor(t[1], t[1], t[0], ALU.add), m, n)
            k = dve.do(lambda e: e.tensor_scalar(t[2], t[1], 8.0, None, ALU.mult), m)
            m = dve.do(lambda e: e.tensor_scalar(t[3], t[1], -8.0, None, ALU.mult), m)
            return t[2], t[3], [k, m]

        lru_out = {}

        def recurrence():
            R, I, T, Q = [h[:] for h in half]
            free = h_ready
            free = free + [dve.mark(), act.mark()]
            w_free = [[], []]
            done = []
            for d in range(2):
                s_pos, s_neg, sp_done = softplus(d)
                yield
                for part in range(2):
                    tiles = range(part * LT // 2, (part + 1) * LT // 2)
                    sig = []
                    for n in tiles:
                        s = n % 2
                        w_in = sp.dma(lru_w[s][:], A["lru_w"][n], lru_w_sem[s], w_free[s])
                        i = take("side")
                        pe_wait_bank(i)
                        pe.wait(w_in, rec_marks[n])
                        for k in range(2):
                            fn = lambda e, k=k, s=s, n=n, i=i, w=2 * d + k: e.matmul(
                                psum[i][:, k * S:(k + 1) * S], lru_w[s][:, w, :], c_cols[:, n, :],
                                start=True, stop=True)
                            m = pe.do(fn) if k else pe.quiet(fn)
                        w_free[s] = [m]
                        k = n - tiles[0]
                        ba, bx = (("fwd_ba", "fwd_bx"), ("bwd_ba", "bwd_bx"))[d]
                        a1 = act.do(lambda e, k=k, n=n, i=i, ba=ba: e.activation(
                            R[:, k, :], psum[i][:, 0:S], ACT.Sigmoid, bias=col(ba, n)), m, free)
                        a2 = act.do(lambda e, k=k, n=n, i=i, bx=bx: e.activation(
                            I[:, k, :], psum[i][:, S:2 * S], ACT.Sigmoid, bias=col(bx, n)), m)
                        bank_free[i] = [a2]
                        yield
                    m_i = act.mark()
                    for n in tiles:
                        k = n - tiles[0]
                        m_t = act.do(lambda e, k=k, s=s_pos[:, n:n + 1]: e.activation(
                            T[:, k, :], R[:, k, :], ACT.Tanh, scale=s), sp_done, m_i)
                    for n in tiles:
                        k = n - tiles[0]
                        m_a = act.do(lambda e, k=k, s=s_neg[:, n:n + 1]: e.activation(
                            R[:, k, :], R[:, k, :], ACT.Exp, scale=s), m_t)
                    yield
                    m = dve.do(lambda e: e.tensor_scalar(Q, T, 1.0, None, ALU.add), m_t, free)
                    m = dve.do(lambda e: e.reciprocal(Q, Q), m)
                    m = dve.do(lambda e: e.tensor_tensor(T, T, Q, ALU.mult), m)
                    m_s = act.do(lambda e: e.activation(T, T, ACT.Sqrt, scale=2.0), m)
                    m = dve.do(lambda e, t0=tiles[0]: e.tensor_tensor(
                        I, I, c_cols[:, t0:t0 + LT // 2, :], ALU.mult), m_i)
                    m = dve.do(lambda e: e.tensor_tensor(I, I, T, ALU.mult), m, m_s)
                    yield
                    for n in tiles:
                        k = n - tiles[0]
                        if d == 0:
                            f = dve.do(lambda e, k=k, n=n: e.tensor_tensor_scan(
                                h_sum[:, n, :], R[:, k, :], I[:, k, :], 0.0, ALU.mult, ALU.add), m, m_a)
                        else:
                            f = dve.do(lambda e, k=k: e.tensor_tensor_scan(
                                Q[:, k, ::-1], R[:, k, ::-1], I[:, k, ::-1], 0.0, ALU.mult, ALU.add), m, m_a)
                    if d == 1:
                        f = dve.do(lambda e, t0=tiles[0]: e.tensor_tensor(
                            h_sum[:, t0:t0 + LT // 2, :], h_sum[:, t0:t0 + LT // 2, :], Q, ALU.add), f)
                    free = [f]
                    done.append(f)
                    yield
            lru_out["done"] = done

        for _ in gemm_cols(ws, h_hi, h_lo, h_ready, KT, LT, take_rec):
            pass
        show("c_cols", c_cols, None)

        def both(a, b):
            live = [a, b]
            while live:
                for g in list(live):
                    if next(g, "end") == "end":
                        live.remove(g)
                    else:
                        yield

        side = both(attention_1(), recurrence())
        n_side = 6

        def several(g, n):
            while True:
                for _ in range(n):
                    if next(g, "end") == "end":
                        return
                yield

        weave(gemm_cols(ws, h_hi, h_lo, h_ready, KT, LT, take_gate), several(side, n_side))
        show("q_rows", q_rows, None)
        show("h_sum", h_sum, None)
        h_free = [pe.mark()]

        gain = load_gain("g_attn_out", dve.mark(), act.mark())
        ga = g_row[:, 0:AW]
        y_tmp = xn[:, 1, :]
        sq = half[0]
        m0 = [att["out"][-1], dve.mark(), act.mark(), gain]
        y_rows = at("y_rows", SCR, [P, NB, AW])
        marks = norm_rows(lambda b: q_rows[:, b, :], lambda b: y_rows[:, b, :], ga, AW, *m0)
        y_ready = flip(lambda b, t: y_rows[:, b, t * P:(t + 1) * P], h_hi, h_lo, AW // P, marks, free=h_free)
        ylru = gate_c
        m = dve.do(lambda e: e.tensor_tensor(ylru[:], gate_c[:], h_sum[:], ALU.mult), lru_out["done"], gate_marks)
        m2 = act.do(lambda e: e.activation(h_sum[:], ylru[:], ACT.Square), m)
        ones = at("ones", o + 26 * KB, [P, P])
        k = pool.do(lambda e: e.memset(ones[:], 1.0), att["out"][-1], act.mark(), pe.mark())
        i = take("side")
        pe_wait_bank(i)
        pe.wait(m2, k)
        for t in range(LT):
            fn = lambda e, t=t, i=i: e.matmul(psum[i][:, 0:S], ones[:], h_sum[:, t, :], start=t == 0, stop=t == LT - 1)
            m3 = pe.do(fn) if t == LT - 1 else pe.quiet(fn)
        rs_bc = at("rs_bc", o + 27 * KB, [P, S])
        m = dve.do(lambda e, i=i: e.tensor_scalar(rs_bc[:], psum[i][:, 0:S], 1.0 / LW, EPS, ALU.mult, ALU.add), m3, k)
        bank_free[i] = [m]
        m = act.do(lambda e: e.activation(rs_bc[:], rs_bc[:], ACT.Sqrt), m)
        m = dve.do(lambda e: e.reciprocal(rs_bc[:], rs_bc[:]), m)
        for t in range(LT):
            m1 = dve.do(lambda e, t=t: e.scalar_tensor_tensor(
                out=ylru[:, t, :], in0=ylru[:, t, :], scalar=col("g_lru_out", t), in1=rs_bc[:],
                op0=ALU.mult, op1=ALU.mult), m, m2)
        T0 = AW // P
        a = act.do(lambda e: e.activation(h_hi[:, T0:KT, :], ylru[:], ACT.Copy), m1, h_free)
        d = dve.do(lambda e: e.tensor_tensor(h_lo[:, T0:KT, :], ylru[:], h_hi[:, T0:KT, :].bitcast(F32),
                                             ALU.subtract), a, h_free)
        y_ready = y_ready + [d]

        def add_to_x(scale=None):
            def f(n, b, ps, m):
                m = dve.do(lambda e: e.tensor_tensor(x[:, b, n * 512:(n + 1) * 512], ps,
                                                     x[:, b, n * 512:(n + 1) * 512], ALU.add), m)
                x_marks.append(m)
                return [m]
            return f

        x_marks = []
        for _ in gemm_rows(ws, h_hi, h_lo, y_ready, KT, D // BANK, add_to_x()):
            pass
        show("x1", x, None)

        h_free = [pe.mark()]
        gain = load_gain("g_ffn", dve.mark(), act.mark(), pe.mark())
        m_free = [dve.mark(), act.mark(), pe.mark()]
        marks = norm_rows(lambda b: x[:, b, :], lambda b: xn[:, b, :], g_row[:], D, x_marks, gain, m_free)
        f_ready = flip(lambda b, t: xn[:, b, t * P:(t + 1) * P], h_hi, h_lo, KT, marks, free=h_free)
        xn_rows = marks

        o = PH0
        qp = at("qp", o, [P, 2 * PH, S])
        sub_k = at("sub_k", o + 16 * KB, [P, 2 * PH, N_KEYS])
        scores = at("scores", o + 24 * KB, [P, NB, 2 * PH, N_KEYS])
        subk_sem = [sem("sub_k_in"), 0]
        before = [dve.mark(), act.mark(), pe.mark(), pool.mark()]
        subk_in = sp.dma(sub_k[:], A["sub_k"], subk_sem, before)
        qp_marks, sc_marks = [], [[], []]

        def take_pq(n, ps, m):
            m = act.do(lambda e: e.activation(qp[:, n, :], ps, ACT.Copy), m, before)
            i = take("side")
            pe_wait_bank(i)
            pe.wait(m, subk_in)
            for b in range(NB):
                fn = lambda e, b=b, i=i: e.matmul(psum[i][:, b * P:(b + 1) * P], qp[:, n, b * P:(b + 1) * P],
                                                  sub_k[:, n, :], start=True, stop=True)
                k = pe.do(fn) if b else pe.quiet(fn)
            c = dve.do(lambda e, i=i: e.tensor_copy(scores[:, :, n, :],
                                                    psum[i][:, 0:2 * P].rearrange("p (b k) -> p b k", b=NB)), k, before)
            bank_free[i] = [c]
            for b in range(NB):
                sc_marks[b].append(c)
            return [m]

        for _ in gemm_cols(ws, h_hi, h_lo, f_ready, KT, 2 * PH, take_pq):
            pass
        show("scores", scores, None)

        gone = [pe.mark(), dve.mark(), act.mark()]
        o = HHL
        val = at("val", o, [P, NB, 2 * PH, TOPK])
        idx = at("idx", o + 2 * KB, [P, NB, 2 * PH, TOPK], U32)
        cand = [at(f"cand{i}", o + 4 * KB + KB * i, [P, TOPK, TOPK]) for i in range(2)]
        best = at("best", o + 6 * KB, [P, NB, PH, TOPK])
        pos = at("pos", o + 7 * KB, [P, NB, PH, TOPK], U32)
        half_u = [at(f"half_u{i}", o + 8 * KB + 512 * i, [P, NE], U32) for i in range(2)]
        half_f = [at(f"half_f{i}", o + 9 * KB + 512 * i, [P, NE]) for i in range(2)]
        idx_f = at("idx_f", o + 10 * KB, [P, 2 * PH, TOPK])
        pick = [at(f"pick{i}", o + 11 * KB + 512 * i, [P, NE]) for i in range(2)]
        expert_f = at("expert_f", o + 12 * KB, [P, NE])
        expert = at("expert", o + 12 * KB + 512, [P, NB, NE], U32)
        gates = at("gates", o + 13 * KB + 512, [P, NB, NE])
        dots = at("dots", o + 14 * KB + 512, [P, NB, NE])
        wts = at("wts", o + 15 * KB + 512, [P, NB, NE])
        diag = [at(f"diag{i}", o + 16 * KB + 512 + 512 * i, [P, P]) for i in range(4)]
        eq = at("eq", o + 19 * KB, [P, NE, TOPK])
        N_U, N_V = 5, 5
        ring_at = o + 27 * KB
        u_rows = [at(f"u_rows{i}", ring_at + 8 * KB * i, [P, D]) for i in range(N_U)]
        v_rows2 = [at(f"v_rows{i}", ring_at + 8 * KB * (N_U + i), [P, D]) for i in range(N_V)]
        assert ring_at + 8 * KB * (N_U + N_V) <= PH0 + 24 * KB

        def top16(values, src, indices, after):
            m = dve.do(lambda e: e.max(values[:, 0:8], src), after)
            m = dve.do(lambda e: e.max_index(indices[:, 0:8], values[:, 0:8], src), m)
            m = dve.do(lambda e: e.match_replace(src, values[:, 0:8], src, NEG * 3e8), m)
            m = dve.do(lambda e: e.max(values[:, 8:16], src), m)
            return dve.do(lambda e: e.max_index(indices[:, 8:16], values[:, 8:16], src), m)

        def route(b):
            for n in range(2 * PH):
                m = top16(val[:, b, n, :], scores[:, b, n, :], idx[:, b, n, :], [sc_marks[b], gone])
            for h in range(PH):
                c = cand[h % 2]
                m = dve.do(lambda e, h=h, c=c: e.tensor_tensor(
                    c[:], val[:, b, 2 * h, :].unsqueeze(2).broadcast_to([P, TOPK, TOPK]),
                    val[:, b, 2 * h + 1, :].unsqueeze(1).broadcast_to([P, TOPK, TOPK]), ALU.add), m)
                m = top16(best[:, b, h, :], c[:].rearrange("p a b -> p (a b)"), pos[:, b, h, :], [m])
            p2 = pos[:, b, :, :].rearrange("p h k -> p (h k)")
            m1 = dve.do(lambda e: e.tensor_scalar(half_u[0][:], p2, 4, None, ALU.logical_shift_right), m)
            m2 = dve.do(lambda e: e.tensor_scalar(half_u[1][:], p2, 15, None, ALU.bitwise_and), m)
            m1 = dve.do(lambda e: e.tensor_copy(half_f[0][:], half_u[0][:]), m1)
            m2 = dve.do(lambda e: e.tensor_copy(half_f[1][:], half_u[1][:]), m2)
            m = dve.do(lambda e: e.tensor_copy(idx_f[:], idx[:, b, :, :]), m)
            by_half = idx_f[:].rearrange("p (h two) a -> p two h a", two=2)
            iota = row("iota16").unsqueeze(1).broadcast_to([P, NE, TOPK])
            eq4 = eq[:].rearrange("p (h k) a -> p h k a", h=PH)
            for i in range(2):
                m = dve.do(lambda e, i=i: e.tensor_tensor(
                    eq[:], half_f[i][:].unsqueeze(2).broadcast_to([P, NE, TOPK]), iota, ALU.is_equal), m, m1, m2)
                m = dve.do(lambda e, i=i: e.tensor_tensor(
                    eq4, eq4, by_half[:, i].unsqueeze(2).broadcast_to([P, PH, TOPK, TOPK]), ALU.mult), m)
                m = dve.do(lambda e, i=i: e.tensor_reduce(pick[i][:], eq[:], AX.X, ALU.add), m)
            m = dve.do(lambda e: e.scalar_tensor_tensor(out=expert_f[:], in0=pick[0][:], scalar=float(N_KEYS),
                                                        in1=pick[1][:], op0=ALU.mult, op1=ALU.add), m)
            e_mark = dve.do(lambda e: e.tensor_copy(expert[:, b, :], expert_f[:]), m)
            g3 = gates[:, b, :].rearrange("p (h k) -> p h k", h=PH)
            tot, rec = columns(PH), columns(PH)
            m = dve.do(lambda e: e.tensor_tensor(g3, best[:, b, :, :],
                                                 best[:, b, :, 0:1].broadcast_to([P, PH, TOPK]), ALU.subtract))
            m = act.do(lambda e: e.activation(gates[:, b, :], gates[:, b, :], ACT.Exp), m)
            m = dve.do(lambda e: e.tensor_reduce(tot, g3, AX.X, ALU.add), m)
            m = dve.do(lambda e: e.reciprocal(rec, tot), m)
            m = dve.do(lambda e: e.tensor_tensor(g3, g3, rec.unsqueeze(2).broadcast_to([P, PH, TOPK]), ALU.mult), m)
            return e_mark, m

        routed = [route(0)]
        routed.append(None)

        u_sem = [[sem(f"u_in{i}"), 0] for i in range(N_U)]
        v_sem = [[sem(f"v_in{i}"), 0] for i in range(N_V)]
        u_free, v_free = [[gone] for _ in range(N_U)], [[gone] for _ in range(N_V)]
        u_got, v_got = {}, {}
        GROUP, LAG = 8, 10
        steps = NB * NE
        ready_w, peer_marks = {}, []
        diag_free = [[] for _ in diag]
        n_diag = [0]

        def gather(table, dst, which, counter, *after):
            pool.wait(*after)
            counter[1] += 16
            pool.steps.append(lambda e: e.indirect_dma_start(
                dst, None, table, bass.IndirectOffsetOnAxis(ap=which, axis=0)).then_inc(counter[0], 16))
            return (counter[0], counter[1])

        def u_step(j):
            b, k = j // NE, j % NE
            s = j % N_U
            got = gather(A["u_emb"], u_rows[s][:], expert[:, b, k:k + 1], u_sem[s], u_free[s], routed[b][0])
            m = dve.do(lambda e: e.tensor_tensor_reduce(
                out=u_rows[s][:], in0=u_rows[s][:], in1=xn[:, b, :], scale=1.0, scalar=0.0,
                op0=ALU.mult, op1=ALU.add, accum_out=dots[:, b, k:k + 1]), got, xn_rows, gone)
            u_free[s] = [m]
            if k % GROUP == GROUP - 1:
                g = slice(k - GROUP + 1, k + 1)
                m = act.do(lambda e: e.activation(dots[:, b, g], dots[:, b, g], ACT.Gelu_apprx_tanh), m)
                ready_w[j // GROUP] = dve.do(lambda e: e.tensor_tensor(
                    wts[:, b, g], dots[:, b, g], gates[:, b, g], ALU.mult), m, routed[b][1])

        def v_load(j):
            b, k, s = j // NE, j % NE, j % N_V
            v_got[j] = gather(A["v_emb"], v_rows2[s][:], expert[:, b, k:k + 1], v_sem[s], v_free[s], routed[b][0])

        def v_use(j):
            b, k, s = j // NE, j % NE, j % N_V
            q = n_diag[0] % len(diag)
            n_diag[0] += 1
            m = act.do(lambda e: e.activation(diag[q][:], ident[:], ACT.Copy, scale=wts[:, b, k:k + 1]),
                       ready_w[j // GROUP], diag_free[q])
            if k == 0:
                for i in range(4):
                    pe_wait_bank(4 * b + i)
            pe.wait(m, v_got[j])
            for i in range(4):
                fn = lambda e, i=i: e.matmul(psum[4 * b + i][:], diag[q][:], v_rows2[s][:, i * BANK:(i + 1) * BANK],
                                             start=k == 0, stop=k == NE - 1)
                m = pe.do(fn) if i == 3 else pe.quiet(fn)
            v_free[s] = [m]
            diag_free[q] = [m]
            if k == NE - 1:
                for i in range(4):
                    cut = slice(i * BANK, (i + 1) * BANK)
                    d = dve.do(lambda e, i=i, cut=cut: e.tensor_tensor(
                        x[:, b, cut], psum[4 * b + i][:], x[:, b, cut], ALU.add), m)
                    bank_free[4 * b + i] = [d]
                    peer_marks.append(d)

        for j in range(steps + LAG + GROUP):
            if j == 24:
                routed[1] = route(1)
            if j < steps:
                u_step(j)
            if 0 <= j - LAG < steps:
                v_load(j - LAG)
                v_use(j - LAG)
        show("x2", x, None)

        everything = [pe.mark(), dve.mark(), act.mark(), pool.mark()]
        for e in (act, dve, pool):
            e.wait(everything)
        small_at[0] = 0
        gain = load_gain("g_final", everything)
        marks = norm_rows(lambda b: x[:, b, :], lambda b: xn[:, b, :], g_row[:], D, peer_marks, gain, everything)
        for b in range(NB):
            m = act.do(lambda e, b=b: e.activation(x[:, b, :], xn[:, b, :], ACT.Copy), marks[b])
        x_now = [m]
        gain = load_gain("g_mix_2", marks)
        marks = norm_rows(lambda b: x[:, b, :], lambda b: xn[:, b, :], g_row[:], D, x_now, gain)
        h_ready = flip(lambda b, t: xn[:, b, t * P:(t + 1) * P], h_hi, h_lo, KT, marks, free=everything)
        rope_in = sp.dma(rope_t[:], A["rope2"], const_sem, everything)

        ws = Weights([A["w2_lat"][i] for i in range(8)] + [A["w2_kr"][0]]
                     + [A["w2_uq"][i] for i in range(3)] + [A["w2_ukv"][i] for i in range(4)]
                     + [A["w2_dil"][i] for i in range(24)]
                     + [A["w2_gate"][i] for i in range(16)] + [A["w2_omla"][i] for i in range(8)]
                     + [c for n in range(KT) for c in
                        ([A["w2_gate"][16 + n]] + ([A["w2_odil"][n // 2]] if n % 2 == 0 else []))]
                     + [A["w2_o"][i] for i in range(16)]
                     + [c for p0, np_ in ((0, FF_PARTS[0]), (FF_PARTS[0], FF_PARTS[1]))
                        for c in ([A["w2_gu"][2 * (p0 + i) + g] for i in range(np_) for g in range(2)]
                                  + [A["w2_down"][n * (FT // 4) + p0 // 4 + i]
                                     for n in range(4) for i in range(np_ // 4)])])
        ws.raw_free = [[everything] for _ in range(N_RAW)]
        ws.split_free = [[everything] for _ in range(N_SPLIT)]

        PA = PH0
        lat_hi = at("lat_hi", PA, [P, 2 * QLT, S], F32R)
        lat_lo = at("lat_lo", PA + 8 * KB, [P, 2 * QLT, S], F32R)
        q2_rows = at("q2_rows", PA + 16 * KB, [P, NB, H2, NOPE])
        kn_rows = at("kn_rows", PA + 24 * KB, [P, NB, H2, NOPE])
        v2_rows = at("v2_rows", PA + 32 * KB, [P, NB, H2, VD])
        qr_rows = at("qr_rows", PA + 40 * KB, [P, NB, H2, ROPE])
        kr_cols = at("kr_cols", PA + 44 * KB, [P, S])
        kr_rows = at("kr_rows", PA + 45 * KB, [P, NB, 2, ROPE])
        qr_cols = at("qr_cols", PA + 46 * KB, [P, H2 // 2, S])
        lat_rows = at("lat_rows", SCR, [P, NB, 2, QL])
        sq_tmp = at("sq_tmp", SCR + 8 * KB, [P, BANK])
        nt_tmp = at("nt_tmp", SCR + 10 * KB, [P, BANK])
        rt_tmp = [at(f"rt_tmp{i}", SCR + 12 * KB + 2 * KB * i, [P, 8, 64]) for i in range(2)]

        tmp_free = [h_ready]

        def head_norm(src, heads, width, gain_name, dst, ready):
            n = heads * width
            ss = columns(heads)
            sq = sq_tmp[:, 0:n].rearrange("p (h w) -> p h w", h=heads)
            nt = nt_tmp[:, 0:n].rearrange("p (h w) -> p h w", h=heads)
            a = act.do(lambda e: e.activation(sq, src, ACT.Square), ready, tmp_free[0])
            m = dve.do(lambda e: e.tensor_reduce(ss, sq, AX.X, ALU.add), a)
            c = dve.do(lambda e: e.tensor_tensor(nt, src, row(gain_name).unsqueeze(1).broadcast_to(
                [P, heads, width]), ALU.mult), a, consts_in)
            r, m = power_mean(ss, heads, width, m)
            d = dve.do(lambda e: e.tensor_tensor(dst, nt, r.unsqueeze(2).broadcast_to([P, heads, width]),
                                                 ALU.mult), m, c)
            tmp_free[0] = [d]
            return c, d

        lat_marks = [[], []]

        def take_lat(n, b, ps, m):
            ss = columns(1)
            a = act.do(lambda e: e.activation(sq_tmp[:], ps, ACT.Square, accum_out=ss), m, tmp_free[0])
            r, k = power_mean(ss, 1, QL, a)
            d = dve.do(lambda e: e.scalar_tensor_tensor(
                out=lat_rows[:, b, n, :], in0=ps, scalar=r, in1=g_row[:, n * QL:(n + 1) * QL],
                op0=ALU.mult, op1=ALU.mult), k, lat_gain)
            lat_marks[b].append(d)
            return [a, d]

        lat_gain = load_gain("g_lat", marks)
        for _ in gemm_rows(ws, h_hi, h_lo, h_ready, KT, 2, take_lat):
            pass

        kr_marks = [[], []]

        def take_kr(n, b, ps, m):
            c, d = head_norm(ps.rearrange("p (h w) -> p h w", h=1), 1, ROPE, "g_k_rope_2",
                             kr_rows[:, b, 0:1, :], m)
            _, r = rope_rows(kr_rows[:, b, 0:1, :], kr_rows[:, b, 1:2, :], 1, b, [t[:, 0:1, :] for t in rt_tmp],
                             [d, rope_in])
            r = dve.do(lambda e: e.tensor_copy(kr_rows[:, b, 0:1, :], kr_rows[:, b, 1:2, :]), r)
            kr_marks[b].append(r)
            return [c]

        for _ in gemm_rows(ws, h_hi, h_lo, h_ready, KT, 1, take_kr, width=ROPE):
            pass
        lat_ready = flip(lambda b, t: lat_rows[:, b, t // QLT, (t % QLT) * P:(t % QLT + 1) * P],
                         lat_hi, lat_lo, 2 * QLT, lat_marks)
        kr_ready = flip(lambda b, t: kr_rows[:, b, :, :].rearrange("p a d -> p (a d)"), None, None, 1, kr_marks,
                        plain=kr_cols[:].unsqueeze(1))

        mla_marks = {"qn": [[], []], "qr": [[], []], "kn": [[], []], "v": []}

        def take_uq(n, b, ps, m):
            if n < 2:
                c, d = head_norm(ps.rearrange("p (h w) -> p h w", h=4), 4, NOPE, "g_q_nope_2",
                                 q2_rows[:, b, 4 * n:4 * n + 4, :], m)
                mla_marks["qn"][b].append(d)
                return [c]
            c, d = head_norm(ps.rearrange("p (h w) -> p h w", h=8), 8, ROPE, "g_q_rope_2", qr_rows[:, b, :, :], m)
            _, r = rope_rows(qr_rows[:, b, :, :], qr_rows[:, b, :, :], 8, b, [t[:] for t in rt_tmp], [d, rope_in])
            mla_marks["qr"][b].append(r)
            return [c]

        for _ in gemm_rows(ws, lat_hi[:, 0:QLT, :], lat_lo[:, 0:QLT, :], lat_ready, QLT, 3, take_uq):
            pass

        def take_ukv(n, b, ps, m):
            if n < 2:
                c, d = head_norm(ps.rearrange("p (h w) -> p h w", h=4), 4, NOPE, "g_k_nope_2",
                                 kn_rows[:, b, 4 * n:4 * n + 4, :], m)
                mla_marks["kn"][b].append(d)
                return [c]
            d = act.do(lambda e: e.activation(
                v2_rows[:, b, 4 * (n - 2):4 * (n - 2) + 4, :].rearrange("p h w -> p (h w)"), ps, ACT.Copy), m)
            mla_marks["v"].append(d)
            return [d]

        for _ in gemm_rows(ws, lat_hi[:, QLT:2 * QLT, :], lat_lo[:, QLT:2 * QLT, :], lat_ready, QLT, 4, take_ukv):
            pass
        show("q2_rows", q2_rows, None)
        show("kn_rows", kn_rows, None)
        show("v2_rows", v2_rows, None)

        lat_gone = [pe.mark()]
        qn_cols = at("qn_cols", PA, [P, H2, S])
        kn_cols = at("kn_cols", PA + 8 * KB, [P, H2, S])
        mla_ready = flip(lambda b, t: q2_rows[:, b, t, :], None, None, H2, mla_marks["qn"], free=lat_gone, plain=qn_cols)
        mla_ready += flip(lambda b, t: kn_rows[:, b, t, :], None, None, H2, mla_marks["kn"], free=lat_gone, plain=kn_cols)
        mla_ready += flip(lambda b, t: qr_rows[:, b, 2 * t:2 * t + 2, :].rearrange("p a d -> p (a d)"), None, None,
                          H2 // 2, mla_marks["qr"], plain=qr_cols)
        mla_ready += kr_ready + mla_marks["v"]

        rows_gone = [pe.mark()]
        dq_rows = at("dq_rows", PA + 16 * KB, [P, NB, H2, 128])
        dk_rows = at("dk_rows", PA + 24 * KB, [P, NB, H2, 128])
        dv_rows = at("dv_rows", SCR + 16 * KB, [P, NB, H2, 128])
        o2_rows = at("o2_rows", SCR, [P, NB, H2, VD])
        s2_buf = at("s2_buf", PA + 50 * KB, [P, 4, S])
        pt2_buf = at("pt2_buf", PA + 54 * KB, [P, 4, 2, P])

        mla = {"s_free": [], "pt_free": [], "out": []}

        def attention_mla():
            scale = (NOPE + ROPE) ** -0.5
            for b in range(NB):
                for g in range(H2 // 4):
                    def score(j, ps, g=g, b=b):
                        hh = 4 * g + j
                        at_p = slice(ROPE * (hh % 2), ROPE * (hh % 2) + ROPE)
                        tok = slice(b * P, (b + 1) * P)
                        pe.quiet(lambda e: e.matmul(ps, qn_cols[:, hh, tok], kn_cols[:, hh, :], start=True, stop=False))
                        return lambda e: e.matmul(ps, qr_cols[at_p, hh // 2, tok], kr_cols[at_p, :],
                                                  start=False, stop=True)

                    def bias(sb, pair, ps, m, free):
                        return dve.do(lambda e: e.tensor_scalar(
                            sb[:, pair::2, :], ps[:].rearrange("p (j s) -> p j s", j=2),
                            scale, None, ALU.mult), m, free)

                    yield from attention(score, 1.0, bias, None,
                                         lambda j, kb, g=g: v2_rows[:, kb, 4 * g + j, :], VD,
                                         o2_rows[:, b, 4 * g:4 * g + 4, :], s2_buf, pt2_buf, mla, mla_ready)

        dil_marks = {"q": [[], []], "k": [[], []], "v": []}

        def take_dil(n, b, ps, m):
            which, part = n // 2, n % 2
            if which < 2:
                dst = (dq_rows, dk_rows)[which][:, b, 4 * part:4 * part + 4, :]
                c, d = head_norm(ps.rearrange("p (h w) -> p h w", h=4), 4, 128, ("g_q_dil_2", "g_k_dil_2")[which],
                                 dst, [m, rows_gone])
                dil_marks["qk"[which]][b].append(d)
                return [c]
            d = act.do(lambda e: e.activation(dv_rows[:, b, 4 * part:4 * part + 4, :].rearrange("p h w -> p (h w)"),
                                              ps, ACT.Copy), m, lat_marks[0] + lat_marks[1])
            dil_marks["v"].append(d)
            return [d]

        weave(gemm_rows(ws, h_hi, h_lo, h_ready, KT, 6, take_dil), attention_mla())
        show("o_mla", o2_rows, None)

        om_hi = at("om_hi", PA, [P, H2, S], F32R)
        om_lo = at("om_lo", PA + 8 * KB, [P, H2, S], F32R)
        mla_gone = [pe.mark()]
        om_ready = flip(lambda b, t: o2_rows[:, b, t, :], om_hi, om_lo, H2, [mla["out"], mla["out"]], free=mla_gone)
        o2_gone = [pe.mark()]
        dk_cols = at("dk_cols", PA + 32 * KB, [P, H2, S])
        dq_cols = at("dq_cols", PA + 40 * KB, [P, H2, S])
        g_cols = at("g_cols", PA + 16 * KB, [P, KT, S])
        dil_ready = flip(lambda b, t: dk_rows[:, b, t, :], None, None, H2, dil_marks["k"], free=mla_gone, plain=dk_cols)
        dil_ready += flip(lambda b, t: dq_rows[:, b, t, :], None, None, H2, dil_marks["q"], free=mla_gone, plain=dq_cols)
        dil_ready += dil_marks["v"]
        dist = at("dist", SCR + 8 * KB, [P, 2, 384])
        dist_sem = [sem("dist_in"), 0]
        dist_in = sp.dma(dist[:], A["dist"], dist_sem, dve.mark(), act.mark(), pe.mark())
        dil_gone = [pe.mark()]
        dil = {"s_free": mla["s_free"], "pt_free": mla["pt_free"], "out": []}

        def attention_dil():
            for b in range(NB):
                for g in range(H2 // 4):
                    def score(j, ps, g=g, b=b):
                        hh = 4 * g + j
                        return lambda e: e.matmul(ps, dq_cols[:, hh, b * P:(b + 1) * P], dk_cols[:, hh, :],
                                                  start=True, stop=True)

                    def bias(sb, pair, ps, m, free, g=g, b=b):
                        cut = slice((1 - b) * P, (1 - b) * P + S)
                        for j in (pair, pair + 2):
                            slope = 2.0 ** (-8.0 * (4 * g + j + 1) / H2)
                            k = dve.do(lambda e, j=j, slope=slope: e.scalar_tensor_tensor(
                                out=sb[:, j, :], in0=dist[:, 0, cut], scalar=-slope, in1=dist[:, 1, cut],
                                op0=ALU.mult, op1=ALU.add), free, dist_in)
                        return dve.do(lambda e: e.scalar_tensor_tensor(
                            out=sb[:, pair::2, :], in0=ps[:].rearrange("p (j s) -> p j s", j=2),
                            scalar=128 ** -0.5, in1=sb[:, pair::2, :], op0=ALU.mult, op1=ALU.add), m, k)

                    yield from attention(score, 1.0, bias, None,
                                         lambda j, kb, g=g: dv_rows[:, kb, 4 * g + j, :], 128,
                                         o2_rows[:, b, 4 * g:4 * g + 4, :], s2_buf, pt2_buf, dil, [dil_ready, o2_gone])

        def take_g0(n, ps, m):
            m = act.do(lambda e: e.activation(g_cols[:, n, :], ps, ACT.Sigmoid, bias=col("b_gate_2", n)), m, dil_gone)
            g0_marks.append(m)
            return [m]

        def take_ya(n, ps, m):
            m = dve.do(lambda e: e.tensor_tensor(g_cols[:, n, :], ps, g_cols[:, n, :], ALU.mult), m, g0_marks[n])
            z_marks[n] = m
            return [m]

        g0_marks, z_marks = [], {}

        def g0_and_ya():
            yield from gemm_cols(ws, h_hi, h_lo, h_ready, KT, KT, take_g0)
            yield from gemm_cols(ws, om_hi, om_lo, om_ready, H2, KT, take_ya)

        weave(g0_and_ya(), attention_dil())
        show("o_dil", o2_rows, None)

        od_hi = at("od_hi", PA + 32 * KB, [P, H2, S], F32R)
        od_lo = at("od_lo", PA + 40 * KB, [P, H2, S], F32R)
        att_gone = [pe.mark()]
        od_ready = flip(lambda b, t: o2_rows[:, b, t, :], od_hi, od_lo, H2, [dil["out"], dil["out"]], free=att_gone)
        g1_tmp = [at(f"g1_tmp{i}", PA + 50 * KB + KB * i, [P, S]) for i in range(2)]
        g1_marks, g1_free = {}, [[att_gone], [att_gone]]

        def take_g1(n, ps, m):
            s = n % 2
            g1_marks[n] = act.do(lambda e: e.activation(g1_tmp[s][:], ps, ACT.Sigmoid, bias=col("b_gate_2", KT + n)),
                                 m, g1_free[s])
            return [g1_marks[n]]

        def take_yb(n, ps, m):
            s = n % 2
            m = dve.do(lambda e: e.tensor_tensor(g1_tmp[s][:], ps, g1_tmp[s][:], ALU.mult), m, g1_marks[n])
            k = dve.do(lambda e: e.tensor_tensor(g_cols[:, n, :], g_cols[:, n, :], g1_tmp[s][:], ALU.add),
                       m, z_marks[n])
            g1_free[s] = [k]
            z_marks[n] = k
            return [m]

        for n in range(KT):
            hi, lo, split = ws.next(ahead=1)
            b = take("main")
            pe_wait_bank(b)
            pe.wait(h_ready, split)
            for t in range(KT):
                cut = slice(t * P, (t + 1) * P)
                fin = three(psum[b][:, 0:S], (hi[:, cut], lo[:, cut]), (h_hi[:, t, :], h_lo[:, t, :]),
                            t == 0, t == KT - 1)
                m = pe.do(fin) if t == KT - 1 else pe.quiet(fin)
            ws.used(m)
            bank_free[b] = take_g1(n, psum[b][:, 0:S], m)
            if n % 2 == 0:
                hi2, lo2, split2 = ws.next(ahead=1)
                slot2 = ws.now
            b = take("main")
            pe_wait_bank(b)
            pe.wait(od_ready, split2)
            for t in range(H2):
                cut = slice(((n % 2) * H2 + t) * P, ((n % 2) * H2 + t + 1) * P)
                fin = three(psum[b][:, 0:S], (hi2[:, cut], lo2[:, cut]), (od_hi[:, t, :], od_lo[:, t, :]),
                            t == 0, t == H2 - 1)
                m = pe.do(fin) if t == H2 - 1 else pe.quiet(fin)
            ws.split_free[slot2] = [m]
            bank_free[b] = take_yb(n, psum[b][:, 0:S], m)
        h_free = [pe.mark()]
        z_ready = []
        for q in range(4):
            t4 = slice(4 * q, 4 * q + 4)
            a = act.do(lambda e, t4=t4: e.activation(h_hi[:, t4, :], g_cols[:, t4, :], ACT.Copy),
                       [z_marks[n] for n in range(4 * q, 4 * q + 4)], h_free)
            d = dve.do(lambda e, t4=t4: e.tensor_tensor(h_lo[:, t4, :], g_cols[:, t4, :],
                                                        h_hi[:, t4, :].bitcast(F32), ALU.subtract), a, h_free)
            z_ready.append(d)
        show("z", g_cols, None)
        x_marks = []
        for _ in gemm_rows(ws, h_hi, h_lo, z_ready, KT, D // BANK, add_to_x()):
            pass
        show("x3", x, None)

        h_free = [pe.mark()]
        gone = [pe.mark(), dve.mark(), act.mark()]
        gain = load_gain("g_ffn_2", gone)
        marks = norm_rows(lambda b: x[:, b, :], lambda b: xn[:, b, :], g_row[:], D, x_marks, gain, gone)
        f_ready = flip(lambda b, t: xn[:, b, t * P:(t + 1) * P], h_hi, h_lo, KT, marks, free=h_free)
        hid_hi = at("hid_hi", PA, [P, FF_PARTS[0], S], F32R)
        hid_lo = at("hid_lo", PA + 24 * KB, [P, FF_PARTS[0], S], F32R)
        g_tmp = [at(f"silu_tmp{i}", PA + 48 * KB + KB * i, [P, S]) for i in range(4)]
        hid_free = gone
        g_free = [[gone] for _ in g_tmp]
        n_g = [0]
        out_sem = [sem("out_done"), 0]
        for part, tiles in enumerate(FF_PARTS):
            hid_marks, silu_marks = [], {}

            def take_gu(n, ps, m):
                i, s = n // 2, (n // 2) % 4
                if n % 2 == 0:
                    silu_marks[i] = act.do(lambda e: e.activation(g_tmp[s][:], ps, ACT.Silu), m, g_free[s])
                    return [silu_marks[i]]
                d = dve.do(lambda e: e.tensor_tensor(g_tmp[s][:], ps, g_tmp[s][:], ALU.mult), m, silu_marks[i])
                a = act.do(lambda e: e.activation(hid_hi[:, i, :], g_tmp[s][:], ACT.Copy), d, hid_free)
                k = dve.do(lambda e: e.tensor_tensor(hid_lo[:, i, :], g_tmp[s][:], hid_hi[:, i, :].bitcast(F32),
                                                     ALU.subtract), a, hid_free)
                g_free[s] = [a, k]
                hid_marks.append(k)
                return [d]

            for _ in gemm_cols(ws, h_hi, h_lo, f_ready, KT, 2 * tiles, take_gu):
                pass

            def to_x(n, b, ps, m):
                cut = slice(n * BANK, (n + 1) * BANK)
                m = dve.do(lambda e: e.tensor_tensor(x[:, b, cut], ps, x[:, b, cut], ALU.add), m)
                if part == len(FF_PARTS) - 1:
                    sp.dma(out[b * P:(b + 1) * P, cut], x[:, b, cut], out_sem, m)
                return [m]

            for _ in gemm_rows(ws, hid_hi, hid_lo, hid_marks, tiles, D // BANK, to_x):
                pass
            hid_free = [pe.mark()]
        sp.wait((out_sem[0], out_sem[1]))

        block = ctx.enter_context(nc.Block())

        @block.sync
        def _(e):
            sp.play(e)

        @block.scalar
        def _(e):
            act.play(e)

        @block.vector
        def _(e):
            dve.play(e)

        @block.gpsimd
        def _(e):
            pool.play(e)

        @block.tensor
        def _(e):
            pe.play(e)


def chunks_rows(w, width=BANK):
    k, n = w.shape
    per = WCH // width
    kt = k // P
    per = min(per, kt)
    w = w.reshape(kt // per, per, P, n // width, width).transpose(3, 0, 2, 1, 4)
    return np.ascontiguousarray(w).reshape(-1, P, per * width)


def chunks_cols(w):
    k, n = w.shape
    kt = k // P
    per = WCH // (P * kt)
    w = w.reshape(kt, P, n // (P * per), per, P).transpose(2, 1, 3, 0, 4)
    return np.ascontiguousarray(w).reshape(-1, P, WCH)


def columns_of(v):
    return np.ascontiguousarray(v.reshape(-1, P).T)


def layout(i):
    f = np.float32
    c = {}
    x = i["x"].reshape(NB, P, D)
    c["x"] = np.ascontiguousarray(x.transpose(1, 0, 2))
    c["ident"] = np.eye(P, dtype=f)
    col = {n: columns_of(i[n][0]) for n, _ in COLS}
    c["cols"] = np.ascontiguousarray(np.concatenate([col[n] for n, _ in COLS], axis=1))
    row = {n: i[n][0] for n, _ in ROWS if n != "iota16"}
    row["iota16"] = np.arange(TOPK, dtype=f)
    c["rows"] = np.ascontiguousarray(np.broadcast_to(np.concatenate([row[n] for n, _ in ROWS]), (P, N_ROWS)))

    def every_partition(v):
        return np.ascontiguousarray(np.broadcast_to(v, (P, D)))

    for n in ("g_mix", "g_ffn", "g_mix_2", "g_ffn_2"):
        c[n] = every_partition(i[n][0])
    c["g_final"] = every_partition(i["g_final"])
    c["g_attn_out"] = every_partition(np.concatenate([i["g_attn_out"][0]] * 2))
    c["g_lat"] = every_partition(np.concatenate([i["g_cq_2"][0], i["g_ckv_2"][0]] * 2))

    pos = np.arange(S, dtype=f)[:, None]
    def table(inv):
        ang = pos * inv[None, :]
        cos, sin = np.cos(ang).astype(f), np.sin(ang).astype(f)
        t = np.stack([np.concatenate([cos, cos], 1), np.concatenate([-sin, sin], 1)], 1)
        return np.ascontiguousarray(t.reshape(NB, P, 2, 64).transpose(1, 0, 2, 3))
    c["rope1"] = table((f(10000.0) ** (-np.arange(32, dtype=f) / f(32))).astype(f))
    c["rope2"] = table((f(10000.0) ** (-np.arange(0, 64, 2, dtype=f) / f(64))).astype(f))
    delta = np.arange(384)[None, :] - P - np.arange(P)[:, None]
    c["window"] = np.where(np.abs(delta) <= 128, 0.0, NEG).astype(f)
    count = (np.abs(delta) <= 64).astype(int) + (delta % 4 == 0) + (delta % 16 == 0)
    c["dist"] = np.ascontiguousarray(np.stack(
        [np.abs(delta).astype(f), np.where(count > 0, np.log(np.maximum(count, 1)), NEG).astype(f)], 1))

    w = i["w_in"][0]
    c["w1_qkv"] = chunks_rows(w[:, :1536])
    c["w1_gate"] = chunks_cols(w[:, 1536:2560])
    c["w1_rec"] = chunks_cols(w[:, 2560:3584])
    lru = np.zeros((LT, P, 4, P), f)
    for k, n in enumerate(("fwd_wa", "fwd_wx", "bwd_wa", "bwd_wx")):
        a = i[n][0]
        for t in range(LT):
            lru[t, 0:64, k, 0:64] = a[2 * t]
            lru[t, 64:128, k, 64:128] = a[2 * t + 1]
    c["lru_w"] = lru
    c["w1_out"] = chunks_rows(i["w_out"][0])
    c["w1_pq"] = chunks_cols(i["w_pq"][0])
    sk = np.stack([i["sub_k1"][0], i["sub_k2"][0]], 1)
    c["sub_k"] = np.ascontiguousarray(sk.reshape(2 * PH, N_KEYS, P).transpose(2, 0, 1))
    c["u_emb"] = i["u_emb"][0]
    c["v_emb"] = i["v_emb"][0]

    w = i["w_in_2"][0]
    c["w2_lat"] = chunks_rows(w[:, 0:1024])
    kr = w[:, 1024:1088].reshape(KT, P, ROPE).transpose(1, 0, 2)
    c["w2_kr"] = np.ascontiguousarray(kr).reshape(1, P, KT * ROPE)
    c["w2_dil"] = chunks_rows(w[:, 1088:4160])
    c["w2_gate"] = chunks_cols(w[:, 4160:])
    uq = i["w_uq_2"][0].reshape(QL, H2, NOPE + ROPE)
    c["w2_uq"] = chunks_rows(np.concatenate([uq[:, :, :NOPE].reshape(QL, -1), uq[:, :, NOPE:].reshape(QL, -1)], 1))
    ukv = i["w_ukv_2"][0].reshape(QL, H2, NOPE + VD)
    c["w2_ukv"] = chunks_rows(np.concatenate([ukv[:, :, :NOPE].reshape(QL, -1), ukv[:, :, NOPE:].reshape(QL, -1)], 1))
    c["w2_omla"] = chunks_cols(i["w_o_mla_2"][0])
    c["w2_odil"] = chunks_cols(i["w_o_dil_2"][0])
    c["w2_o"] = chunks_rows(i["w_o_2"][0])
    gu = i["w_gate_up_2"][0].reshape(D, 2, FT, P).transpose(0, 2, 1, 3).reshape(D, 2 * FF)
    c["w2_gu"] = chunks_cols(gu)
    c["w2_down"] = chunks_rows(i["w_down_2"][0])
    return {k: np.ascontiguousarray(v) for k, v in c.items()}


def program(nc, arrays, dump=None):
    A = {n: nc.dram_tensor(f"in_{n}", a.shape, F32, kind="ExternalInput").ap() for n, a in arrays.items()}
    out = nc.dram_tensor("out", (S, D), F32, kind="ExternalOutput").ap()
    build(nc, A, out, dump)


def kernel(**inputs):
    import concourse.bacc as bacc
    from concourse.bass_utils import run_bass_kernel_spmd

    arrays = layout({k: np.asarray(v) for k, v in inputs.items()})
    nc = bacc.Bacc("TRN2", target_bir_lowering=False, num_devices=1)
    program(nc, arrays)
    r = run_bass_kernel_spmd(nc, [{f"in_{n}": a for n, a in arrays.items()}], core_ids=[0])
    return r.results[0]["out"].reshape(1, S, D)
```

```python
from contextlib import ExitStack
import math

import numpy as np
import concourse.bass as bass
from concourse import mybir

F32 = mybir.dt.float32
F32R = mybir.dt.float32r
U32 = mybir.dt.uint32
ALU = mybir.AluOpType
ACT = mybir.ActivationFunctionType
AX = mybir.AxisListType

P = 128
S = 256
NB = S // P
D = 2048
KT = D // P
WCH = 2048
BANK = 512

HD = 64
NQ, NKV = 16, 4
AW = NQ * HD
LW = 1024
LT = LW // P
N_KEYS = 128
PH = 8
TOPK = 16
NE = PH * TOPK
NOPE, ROPE, VD = 128, 64, 128
H2 = 8
QL = 512
QLT = QL // P
FF = 5632
FT = FF // P
FF_PARTS = (24, 20)
EPS = 1e-6
NEG = -1e30

COLS = [("conv_w", 4 * LT), ("conv_b", LT), ("fwd_ba", LT), ("fwd_bx", LT), ("fwd_lam", LT),
        ("bwd_ba", LT), ("bwd_bx", LT), ("bwd_lam", LT), ("g_lru_out", LT), ("b_gate_2", 2 * KT)]
ROWS = [("sink", NQ), ("g_q_nope_2", NOPE), ("g_q_rope_2", ROPE), ("g_k_nope_2", NOPE),
        ("g_k_rope_2", ROPE), ("g_q_dil_2", 128), ("g_k_dil_2", 128), ("iota16", TOPK)]


def offsets(table):
    at, out = 0, {}
    for name, n in table:
        out[name] = (at, n)
        at += n
    return out, at


COL_AT, N_COLS = offsets(COLS)
ROW_AT, N_ROWS = offsets(ROWS)


class Engine:

    def __init__(self, sem, chained=False):
        self.sem, self.count, self.steps, self.met = sem, 0, [], {}
        self.chained = chained

    def wait(self, *marks):
        for m in marks:
            if m is None:
                continue
            if isinstance(m, list):
                self.wait(*m)
                continue
            sem, value = m
            if self.met.get(sem.name, 0) < value:
                self.met[sem.name] = value
                self.steps.append(lambda e, sem=sem, value=value: e.wait_ge(sem, value))

    def do(self, fn, *after):
        self.wait(*after)
        if self.chained and self.count:
            self.wait((self.sem, self.count))
        self.count += 1
        self.steps.append(lambda e: fn(e).then_inc(self.sem, 1))
        return (self.sem, self.count)

    def quiet(self, fn, *after):
        self.wait(*after)
        self.steps.append(fn)

    def mark(self):
        return (self.sem, self.count)

    def dma(self, out, in_, counter, *after):
        self.wait(*after)
        counter[1] += 16
        self.steps.append(lambda e: e.dma_start(out, in_).then_inc(counter[0], 16))
        return (counter[0], counter[1])

    def play(self, e):
        for step in self.steps:
            step(e)


class Side:

    def __init__(self):
        self.live = []

    def add(self, stage, rate=1, delay=0):
        self.live.append([stage, rate, delay])

    def step(self):
        for entry in list(self.live):
            if entry[2]:
                entry[2] -= 1
                continue
            for _ in range(entry[1]):
                if next(entry[0], "end") == "end":
                    self.live.remove(entry)
                    break

    def beside(self, main):
        for _ in main:
            self.step()

    def finish(self):
        while self.live:
            self.step()


class Ready(list):

    def __init__(self):
        self.groups = {}

    def put(self, group, mark):
        self.append(mark)
        self.groups.setdefault(group, []).append(mark)

    def of(self, tile):
        return self.groups[tile // 4]


def build(nc, A, out):
    ctx = ExitStack()
    with ctx:
        def sem(name):
            return ctx.enter_context(nc.semaphore(name))

        pe, sp = Engine(sem("pe_done")), Engine(None)
        act, dve, pool = (Engine(sem(n), chained=True) for n in ("act_done", "dve_done", "pool_done"))

        base = (nc.sbuf_base + 63) // 64 * 64
        used = {}

        def at(name, offset, shape, dt=F32):
            size = 4 * int(np.prod(shape[1:]))
            used[name] = (offset, offset + size)
            assert base + offset + size <= nc.sbuf_usable_end, (name, offset, size)
            return nc.alloc_sbuf_tensor_at(name, shape, dt, offset=base + offset)

        KB = 1024
        x = at("x", 0, [P, NB, D])
        o = 16 * KB
        ident = at("ident", o, [P, P]); o += 4 * P
        cols = at("cols", o, [P, N_COLS]); o += 4 * N_COLS
        rows = at("rows", o, [P, N_ROWS]); o += 4 * N_ROWS
        rope_t = at("rope_t", o, [P, NB, 2, 64]); o += 4 * NB * 128
        small = at("small", o, [P, 640]); o += 4 * 640
        SCR = (o + 63) // 64 * 64
        HHL = SCR + 24 * KB
        WR = HHL + 32 * KB
        PH0 = WR + 64 * KB
        xn = at("xn", SCR, [P, NB, D])
        g_row = at("g_row", SCR + 16 * KB, [P, D])
        h_hi = at("h_hi", HHL, [P, KT, S], F32R)
        h_lo = at("h_lo", HHL + 16 * KB, [P, KT, S], F32R)
        N_RAW, N_SPLIT = 2, 3
        w_raw = [at(f"w_raw{i}", WR + 8 * KB * i, [P, WCH]) for i in range(N_RAW)]
        w_hi = [at(f"w_hi{i}", WR + 8 * KB * (N_RAW + i), [P, WCH], F32R) for i in range(N_SPLIT)]
        w_lo = [at(f"w_lo{i}", WR + 8 * KB * (N_RAW + N_SPLIT + i), [P, WCH], F32R) for i in range(N_SPLIT)]

        def col(name, i=0):
            a = COL_AT[name][0] + i
            return cols[:, a:a + 1]

        def row(name):
            a, n = ROW_AT[name]
            return rows[:, a:a + n]

        small_at = [0]

        def columns(n):
            a = small_at[0]
            small_at[0] += n
            assert small_at[0] <= 640, small_at
            return small[:, a:a + n]

        psum = [ctx.enter_context(nc.psum_tensor(f"bank{i}", [P, BANK], F32)) for i in range(8)]
        bank_free = [[] for _ in range(8)]
        turn = {"main": 0, "side": 0}

        def take(kind, n=None):
            for _ in range(4):
                i = turn[kind] % 4 + (0 if kind == "main" else 4)
                turn[kind] += 1
                if bank_free[i] is not None:
                    return i
            assert False, "all banks are held"

        def pe_wait_bank(i):
            assert bank_free[i] is not None
            pe.wait(bank_free[i])
            bank_free[i] = None

        const_sem = [sem("consts"), 0]
        x_sem = [[sem(f"x_in{b}"), 0] for b in range(NB)]
        gain_sem = [sem("gains"), 0]
        x_in = [sp.dma(x[:, b, :], A["x"][:, b, :], x_sem[b]) for b in range(NB)]

        def load_gain(name, *after):
            return sp.dma(g_row[:], A[name], gain_sem, *after)

        class Weights:
            raw_sem = [[sem(f"w_raw_in{i}"), 0] for i in range(N_RAW)]

            def __init__(self, chunks):
                self.chunks, self.n_load, self.n_split, self.n_used = chunks, 0, 0, 0
                self.raw_free = [[] for _ in range(N_RAW)]
                self.split_free = [[] for _ in range(N_SPLIT)]
                self.loaded, self.ready = {}, {}

            def load(self):
                i = self.n_load
                if i >= len(self.chunks):
                    return
                self.n_load += 1
                s = i % N_RAW
                src = self.chunks[i]
                n = src.shape[-1]
                self.loaded[i] = sp.dma(w_raw[s][:, 0:n], src, self.raw_sem[s], self.raw_free[s])

            def split(self):
                i = self.n_split
                if i >= len(self.chunks):
                    return
                while self.n_load <= i:
                    self.load()
                self.n_split += 1
                s, r, n = i % N_SPLIT, i % N_RAW, self.chunks[i].shape[-1]
                hi, lo, raw = w_hi[s][:, 0:n], w_lo[s][:, 0:n], w_raw[r][:, 0:n]
                a = act.do(lambda e: e.activation(hi, raw, ACT.Copy), self.loaded[i], self.split_free[s])
                b = dve.do(lambda e: e.tensor_tensor(lo, raw, hi.bitcast(F32), ALU.subtract),
                           self.loaded[i], a, self.split_free[s])
                self.raw_free[r] = [a, b]
                self.ready[i] = b
                self.load()

            def next(self):
                i = self.n_used
                self.n_used += 1
                while self.n_split < min(i + N_SPLIT, len(self.chunks)):
                    self.split()
                self.now = i % N_SPLIT
                return w_hi[self.now], w_lo[self.now], self.ready[i]

            def used(self, mark):
                self.split_free[self.now] = [mark]

        def three(psum_ap, st, mv, first, last):
            pe.quiet(lambda e: e.matmul(psum_ap, st[0], mv[0], start=first, stop=False))
            pe.quiet(lambda e: e.matmul(psum_ap, st[0], mv[1], start=False, stop=False))
            return lambda e: e.matmul(psum_ap, st[1], mv[0], start=False, stop=last)

        def gemm_rows(ws, a_hi, a_lo, ready, tiles, n_out, consume, width=BANK):
            per = WCH // width
            for n in range(n_out):
                banks = [take("main") for _ in range(NB)]
                for b in banks:
                    pe_wait_bank(b)
                c0 = 0
                while c0 < tiles:
                    k_here = min(per, tiles - c0)
                    hi, lo, split = ws.next()
                    pe.wait(split)
                    for b in range(NB):
                        for k in range(k_here):
                            t = c0 + k
                            pe.wait(ready.of(t))
                            last = t == tiles - 1
                            cut = slice(k * width, (k + 1) * width)
                            tok = slice(b * P, (b + 1) * P)
                            fin = three(psum[banks[b]][:, 0:width], (a_hi[:, t, tok], a_lo[:, t, tok]),
                                        (hi[:, cut], lo[:, cut]), t == 0, last)
                            if k == k_here - 1 and (b == NB - 1 or last):
                                mark = pe.do(fin)
                            else:
                                pe.quiet(fin)
                            if last:
                                done = mark
                                bank_free[banks[b]] = consume(n, b, psum[banks[b]][:, 0:width], done)
                    ws.used(mark)
                    c0 += k_here
                    yield

        def gemm_cols(ws, a_hi, a_lo, ready, tiles, n_out, consume):
            per = WCH // (P * tiles)
            for n in range(n_out):
                if n % per == 0:
                    hi, lo, split = ws.next()
                b = take("main")
                pe_wait_bank(b)
                pe.wait(split)
                for t in range(tiles):
                    pe.wait(ready.of(t))
                    cut = slice(((n % per) * tiles + t) * P, ((n % per) * tiles + t + 1) * P)
                    fin = three(psum[b][:, 0:S], (hi[:, cut], lo[:, cut]), (a_hi[:, t, :], a_lo[:, t, :]),
                                t == 0, t == tiles - 1)
                    if t == tiles - 1:
                        mark = pe.do(fin)
                    else:
                        pe.quiet(fin)
                if n % per == per - 1 or n == n_out - 1:
                    ws.used(mark)
                bank_free[b] = consume(n, psum[b][:, 0:S], mark)
                yield

        def power_mean(ss, n, width, *after):
            v, half, r = columns(n), columns(n), columns(n)
            m = dve.do(lambda e: e.tensor_scalar(v, ss, 1.0 / width, EPS, ALU.mult, ALU.add), *after)
            k = pool.do(lambda e: e.memset(half, -0.5))
            return r, pool.do(lambda e: e.tensor_tensor(r, v, half, ALU.pow), m, k)

        def norm_rows(src, dst, gain, width, *after, blocks=range(NB)):
            marks = []
            for b in blocks:
                ss = columns(1)
                m = act.do(lambda e, b=b, ss=ss: e.activation(dst(b), src(b), ACT.Square, accum_out=ss), *after)
                r, m = power_mean(ss, 1, width, m)
                marks.append(dve.do(lambda e, b=b, r=r: e.scalar_tensor_tensor(
                    out=dst(b), in0=src(b), scalar=r, in1=gain, op0=ALU.mult, op1=ALU.mult), m))
            return marks

        QUARTERS = [slice(q * BANK, (q + 1) * BANK) for q in range(D // BANK)]

        def square_of(b, q, sums, *after):
            cut = QUARTERS[q]
            return act.do(lambda e: e.activation(xn[:, b, cut], x[:, b, cut], ACT.Square,
                                                 accum_out=sums[:, q:q + 1]), *after)

        def norm_to_columns(sums, squared, gain_in, out_marks, hi, lo, *after, free=None):
            scale, rows_of = {}, [{}, {}]
            for b in range(NB):
                ss = columns(1)
                m = dve.do(lambda e, ss=ss, b=b: e.tensor_reduce(ss, sums[b], AX.X, ALU.add), squared[b])
                scale[b] = power_mean(ss, 1, D, m)

            def make_rows(q):
                cut = QUARTERS[q]
                for b in range(NB):
                    r, m = scale[b]
                    rows_of[b][q] = dve.do(lambda e, b=b, r=r: e.scalar_tensor_tensor(
                        out=xn[:, b, cut], in0=x[:, b, cut], scalar=r, in1=g_row[:, cut],
                        op0=ALU.mult, op1=ALU.mult), m, gain_in, *after)

            flips = flip_steps(out_marks, lambda b, t: xn[:, b, t * P:(t + 1) * P], hi, lo, KT, rows_of, free=free)
            make_rows(0)
            for q in range(len(QUARTERS)):
                if q + 1 < len(QUARTERS):
                    make_rows(q + 1)
                for _ in range(NB):
                    next(flips)
            next(flips, None)
            return [rows_of[b][q] for b in range(NB) for q in rows_of[b]]

        def flip_steps(out_marks, src, hi, lo, tiles, marks, free=None, plain=None, blocks=range(NB), kind="side",
                       first=0, last=None):
            for t0 in range(first, tiles if last is None else last, 4):
                for b in blocks:
                    n = min(4, tiles - t0)
                    i = take(kind)
                    pe_wait_bank(i)
                    pe.wait(marks[b][t0 // 4] if isinstance(marks[b], dict) else marks[b])
                    for k in range(n):
                        fn = lambda e, k=k, i=i, t0=t0, b=b: e.transpose(
                            psum[i][:, k * P:(k + 1) * P], src(b, t0 + k), ident[:])
                        m = pe.do(fn) if k == n - 1 else pe.quiet(fn)
                    got = psum[i][:, 0:n * P].rearrange("p (k q) -> p k q", q=P)
                    tok = slice(b * P, (b + 1) * P)
                    if plain is not None:
                        a = act.do(lambda e, got=got, t0=t0, n=n, tok=tok: e.activation(
                            plain[:, t0:t0 + n, tok], got, ACT.Copy), m, free)
                        bank_free[i] = [a]
                        out_marks.put(t0 // 4, a)
                        yield
                        continue
                    a = act.do(lambda e, got=got, t0=t0, n=n, tok=tok: e.activation(
                        hi[:, t0:t0 + n, tok], got, ACT.Copy), m, free)
                    d = dve.do(lambda e, got=got, t0=t0, n=n, tok=tok: e.tensor_tensor(
                        lo[:, t0:t0 + n, tok], got, hi[:, t0:t0 + n, tok].bitcast(F32), ALU.subtract), a)
                    bank_free[i] = [a, d]
                    out_marks.put(t0 // 4, d)
                    yield

        def attention(score, bias, sink, value, dv, dst, sbuf_s, sbuf_pt, state, ready):
            pe.wait(ready)
            halves = []
            for pair in range(2):
                i = take("side")
                pe_wait_bank(i)
                for j in (pair, pair + 2):
                    fn = score(j, psum[i][:, (j // 2) * S:(j // 2 + 1) * S])
                    m = pe.do(fn) if j > 1 else pe.quiet(fn)
                halves.append((i, m))
            got = []
            for pair, (i, m) in enumerate(halves):
                d = bias(sbuf_s, pair, psum[i], m, state["s_free"])
                bank_free[i] = [d]
                got.append(d)
            top, neg, tot, rec = columns(4), columns(4), columns(4), columns(4)
            m = dve.do(lambda e: e.tensor_reduce(top, sbuf_s[:], AX.X, ALU.max), got)
            if sink is not None:
                top2 = columns(4)
                m = dve.do(lambda e: e.tensor_tensor(top2, top, sink, ALU.max), m)
            else:
                top2 = top
            m = dve.do(lambda e: e.tensor_scalar(neg, top2, -1.0, None, ALU.mult), m)
            if sink is not None:
                away, ex, tot2 = columns(4), columns(4), columns(4)
                m = dve.do(lambda e: e.tensor_tensor(away, sink, neg, ALU.add), m)
            yield
            es = None
            for j in range(4):
                es = act.do(lambda e, j=j: e.activation(sbuf_s[:, j, :], sbuf_s[:, j, :], ACT.Exp,
                                                        bias=neg[:, j:j + 1], accum_out=tot[:, j:j + 1]), m)
            if sink is not None:
                es2 = act.do(lambda e: e.activation(ex, away, ACT.Exp), m)
            yield
            copies = []
            for pair in range(2):
                i = take("side")
                pe_wait_bank(i)
                pe.wait(es)
                for k in range(4):
                    j, kb = 2 * pair + k // 2, k % 2
                    fn = lambda e, k=k, j=j, kb=kb, i=i: e.transpose(
                        psum[i][:, k * P:(k + 1) * P], sbuf_s[:, j, kb * P:(kb + 1) * P], ident[:])
                    m = pe.do(fn) if k == 3 else pe.quiet(fn)
                dst_pt = sbuf_pt[:, 2 * pair:2 * pair + 2, :, :].rearrange("p j k q -> p (j k q)")
                if pair == 0:
                    c = act.do(lambda e, i=i, d=dst_pt: e.activation(d, psum[i][:], ACT.Copy), m, state["pt_free"])
                else:
                    c = dve.do(lambda e, i=i, d=dst_pt: e.tensor_copy(d, psum[i][:]), m, state["pt_free"])
                bank_free[i] = [c]
                copies.append(c)
            state["s_free"] = [m]
            yield
            if sink is not None:
                inv = dve.do(lambda e: e.tensor_tensor(tot2, tot, ex, ALU.add), es2, es)
            else:
                tot2, inv = tot, es
            inv = dve.do(lambda e: e.reciprocal(rec, tot2), inv)
            i = take("side")
            pe_wait_bank(i)
            pe.wait(copies)
            for j in range(4):
                for kb in range(2):
                    fn = lambda e, j=j, kb=kb, i=i: e.matmul(psum[i][:, j * dv:(j + 1) * dv], sbuf_pt[:, j, kb, :],
                                                        value(j, kb), start=kb == 0, stop=kb == 1)
                    m = pe.do(fn) if (j, kb) == (3, 1) else pe.quiet(fn)
            state["pt_free"] = [m]
            o_ps = psum[i][:, 0:4 * dv].rearrange("p (j d) -> p j d", j=4)
            d = dve.do(lambda e: e.tensor_tensor(dst, o_ps, rec.unsqueeze(2).broadcast_to([P, 4, dv]), ALU.mult),
                       m, inv, state.get("out_free"))
            bank_free[i] = [d]
            state["out"].append(d)
            yield

        def rope_rows(src, dst, heads, b, tmp, ready, bank_mark=None):
            cos = rope_t[:, b, 0, :].unsqueeze(1).broadcast_to([P, heads, 64])
            sin = rope_t[:, b, 1, :].unsqueeze(1).broadcast_to([P, heads, 64])
            t0, t1 = tmp
            a = dve.do(lambda e: e.tensor_tensor(t0, src, cos, ALU.mult), ready)
            dve.do(lambda e: e.tensor_tensor(t1[:, :, 0:32], src[:, :, 32:64], sin[:, :, 0:32], ALU.mult), ready)
            c = dve.do(lambda e: e.tensor_tensor(t1[:, :, 32:64], src[:, :, 0:32], sin[:, :, 32:64], ALU.mult))
            return c, dve.do(lambda e: e.tensor_tensor(dst, t0, t1, ALU.add), a, c)

        o = PH0
        q_rows = at("q_rows", o, [P, NB, AW])
        k_rows = at("k_rows", o + 8 * KB, [P, NB, NKV, 2, HD])
        v_rows = at("v_rows", o + 12 * KB, [P, NB, NKV, HD])
        q_cols = at("q_cols", o + 14 * KB, [P, NQ // 2, S])
        k_cols = at("k_cols", o + 22 * KB, [P, NKV, S])
        s_buf = [at(f"s_buf{b}", a, [P, 4, S]) for b, a in enumerate((o + 26 * KB, SCR + 16 * KB))]
        pt_buf = [at(f"pt_buf{b}", a, [P, 4, 2, P]) for b, a in enumerate((o + 30 * KB, SCR + 20 * KB))]
        rope_tmp = [at(f"rope_tmp{i}", o + 50 * KB + 2 * KB * i, [P, 8, 64]) for i in range(2)]
        c_cols = at("c_cols", o + 34 * KB, [P, LT, S])
        h_sum = at("h_sum", o + 42 * KB, [P, LT, S])
        gate_c = at("gate_c", o + 50 * KB, [P, LT, S])
        window = at("window", o + 58 * KB, [P, 384])
        lru_w = [at(f"lru_w{i}", o + 59 * KB + 512 + 2 * KB * i, [P, 4, P]) for i in range(2)]
        sp_sm = at("softplus", o + 63 * KB + 512, [P, 8, LT])
        half = [at(f"lru_half{i}", SCR + 4 * KB * i, [P, LT // 2, S]) for i in range(4)]

        win_sem = [sem("window_in"), 0]
        out_chunks = [A["w1_out"][4 * n + 2 * part + c] for part in (1, 0) for n in range(4) for c in range(2)]
        ws = Weights([A["w1_rec"][i] for i in range(8)] + [A["w1_qkv"][i] for i in (*range(8, 12), *range(8))]
                     + [A["w1_gate"][i] for i in range(8)] + out_chunks
                     + [A["w1_pq"][i] for i in range(16)])
        gain = load_gain("g_mix")
        ident_sem = [sem("ident_in"), 0]
        ident_in = sp.dma(ident[:], A["ident"], ident_sem)
        for _ in range(N_RAW):
            ws.load()
        for t, name in ((cols, "cols"), (rows, "rows"), (rope_t, "rope1")):
            sp.dma(t[:], A[name], const_sem)
        consts_in = (const_sem[0], const_sem[1])
        win_in = sp.dma(window[:], A["window"], win_sem)
        first_sums, h_ready = [columns(1) for _ in range(NB)], Ready()
        m0 = act.do(lambda e: e.activation(xn[:, 0, :], x[:, 0, :], ACT.Square, accum_out=first_sums[0]), x_in[0])
        m1 = dve.do(lambda e: e.tensor_tensor_reduce(
            out=xn[:, 1, :], in0=x[:, 1, :], in1=x[:, 1, :], scale=1.0, scalar=0.0,
            op0=ALU.mult, op1=ALU.add, accum_out=first_sums[1]), x_in[1])
        norm_to_columns(first_sums, [m0, m1], [gain, ident_in], h_ready, h_hi, h_lo)
        act.wait(consts_in)
        dve.wait(consts_in)

        side = Side()
        rec_marks = []

        def take_rec(n, ps, m):
            def tap(w):
                return col("conv_w", w * LT + n)
            c = c_cols[:, n, :]
            m = act.do(lambda e: e.activation(c, ps, ACT.Identity, bias=col("conv_b", n), scale=tap(2)), m)
            for w, out_at, in_at in ((0, slice(2, S), slice(0, S - 2)), (1, slice(1, S), slice(0, S - 1)),
                                     (3, slice(0, S - 1), slice(1, S))):
                m = dve.do(lambda e, w=w, o_=out_at, i_=in_at: e.scalar_tensor_tensor(
                    out=c[:, o_], in0=ps[:, i_], scalar=tap(w), in1=c[:, o_], op0=ALU.mult, op1=ALU.add), m)
            rec_marks.append(m)
            return [m]

        lru_w_sem = [[sem(f"lru_w_in{i}"), 0] for i in range(2)]
        lru_done = []

        def softplus(d):
            lam = cols[:, COL_AT[("fwd_lam", "bwd_lam")[d]][0]:][:, 0:LT]
            t = [sp_sm[:, 4 * d + i, :] for i in range(4)]
            m = act.do(lambda e: e.activation(t[0], lam, ACT.Abs), consts_in)
            m = act.do(lambda e: e.activation(t[0], t[0], ACT.Exp, scale=-1.0), m)
            m = dve.do(lambda e: e.tensor_scalar(t[0], t[0], 1.0, None, ALU.add), m)
            m = act.do(lambda e: e.activation(t[0], t[0], ACT.Ln), m)
            n = dve.do(lambda e: e.tensor_scalar(t[1], lam, -1.0, 0.0, ALU.mult, ALU.max), consts_in)
            m = dve.do(lambda e: e.tensor_tensor(t[1], t[1], t[0], ALU.add), m, n)
            k = dve.do(lambda e: e.tensor_scalar(t[2], t[1], 8.0, None, ALU.mult), m)
            m = dve.do(lambda e: e.tensor_scalar(t[3], t[1], -8.0, None, ALU.mult), m)
            return t[2], t[3], [k, m]

        def recurrence():
            R, I, T, Q = [h[:] for h in half]
            rounds = [(d, part) for part in range(2) for d in range(2)]
            order = [(d, n) for d, part in rounds for n in range(part * LT // 2, (part + 1) * LT // 2)]
            soft, w_free, w_next, banks = {}, [[], []], {}, {}

            def load_w(k):
                if k < len(order):
                    w_next[k] = sp.dma(lru_w[k % 2][:], A["lru_w"][order[k][1]], lru_w_sem[k % 2], w_free[k % 2])

            def products(k):
                d, n = order[k]
                s, i = k % 2, take("side")
                pe_wait_bank(i)
                pe.wait(w_next[k], rec_marks[n])
                for h in range(2):
                    fn = lambda e, h=h, w=2 * d + h: e.matmul(
                        psum[i][:, h * S:(h + 1) * S], lru_w[s][:, w, :], c_cols[:, n, :], start=True, stop=True)
                    m = pe.do(fn) if h else pe.quiet(fn)
                w_free[s] = [m]
                load_w(k + 2)
                banks[k] = (i, m)

            def gates_of_tile(k, free):
                d, n = order[k]
                i, m = banks[k]
                ba, bx = (("fwd_ba", "fwd_bx"), ("bwd_ba", "bwd_bx"))[d]
                act.do(lambda e: e.activation(R[:, k % 4, :], psum[i][:, 0:S], ACT.Sigmoid, bias=col(ba, n)), m, free)
                a = act.do(lambda e: e.activation(I[:, k % 4, :], psum[i][:, S:2 * S], ACT.Sigmoid, bias=col(bx, n)), m)
                bank_free[i] = [a]
                return a

            load_w(0)
            load_w(1)
            soft = [softplus(d) for d in range(2)]
            for k in range(2):
                products(k)
            yield
            free = h_ready
            for r, (d, part) in enumerate(rounds):
                s_pos, s_neg, sp_done = soft[d]
                k0, t0 = 4 * r, part * LT // 2
                for k in (k0, k0 + 1):
                    gates_of_tile(k, free)
                for k in (k0 + 2, k0 + 3):
                    products(k)
                yield
                for k in (k0 + 2, k0 + 3):
                    m_i = gates_of_tile(k, free)
                for k in range(4):
                    m_t = act.do(lambda e, k=k, s=s_pos[:, t0 + k:t0 + k + 1]: e.activation(
                        T[:, k, :], R[:, k, :], ACT.Tanh, scale=s), sp_done, m_i, free)
                for k in range(4):
                    m_a = act.do(lambda e, k=k, s=s_neg[:, t0 + k:t0 + k + 1]: e.activation(
                        R[:, k, :], R[:, k, :], ACT.Exp, scale=s), m_t)
                yield
                m = dve.do(lambda e: e.tensor_scalar(Q, T, 1.0, None, ALU.add), m_t, free)
                m = dve.do(lambda e: e.reciprocal(Q, Q), m)
                m_q = dve.do(lambda e: e.tensor_tensor(T, T, Q, ALU.mult), m)
                m_c = pool.do(lambda e, t0=t0: e.tensor_tensor(I, I, c_cols[:, t0:t0 + LT // 2, :], ALU.mult), m_i)
                yield
                m_s = act.do(lambda e: e.activation(T, T, ACT.Sqrt, scale=2.0), m_q)
                yield
                m = dve.do(lambda e: e.tensor_tensor(I, I, T, ALU.mult), m_c, m_s)
                for k in range(4):
                    if d == 0:
                        f = dve.do(lambda e, k=k, t0=t0: e.tensor_tensor_scan(
                            h_sum[:, t0 + k, :], R[:, k, :], I[:, k, :], 0.0, ALU.mult, ALU.add), m, m_a)
                    else:
                        f = dve.do(lambda e, k=k: e.tensor_tensor_scan(
                            Q[:, k, ::-1], R[:, k, ::-1], I[:, k, ::-1], 0.0, ALU.mult, ALU.add), m, m_a)
                if d == 1:
                    f = dve.do(lambda e, t0=t0: e.tensor_tensor(
                        h_sum[:, t0:t0 + LT // 2, :], h_sum[:, t0:t0 + LT // 2, :], Q, ALU.add), f)
                free = [f]
                lru_done.append(f)
                if r + 1 < len(rounds):
                    for k in (k0 + 4, k0 + 5):
                        products(k)
                yield

        qkv_marks = {"q": [[], []], "k": [[], []], "v": []}

        def take_qkv(n, b, ps, m):
            n = n - 1
            if n >= 0:
                src = ps.rearrange("p (h d) -> p h d", d=HD)
                dst = q_rows[:, b, n * 512:(n + 1) * 512].rearrange("p (h d) -> p h d", d=HD)
                c, r = rope_rows(src, dst, 8, b, [t[:] for t in rope_tmp], m)
                qkv_marks["q"][b].append(r)
                return [c]
            src = ps[:, 0:256].rearrange("p (h d) -> p h d", d=HD)
            c, r = rope_rows(src, k_rows[:, b, :, 0, :], NKV, b, [t[:, 0:NKV, :] for t in rope_tmp], m)
            r2 = act.do(lambda e: e.activation(k_rows[:, b, :, 1, :], k_rows[:, b, :, 0, :], ACT.Copy), r)
            qkv_marks["k"][b].append(r2)
            v = act.do(lambda e: e.activation(v_rows[:, b, :, :].rearrange("p h d -> p (h d)"), ps[:, 256:512],
                                              ACT.Copy), m)
            qkv_marks["v"].append(v)
            return [c, v]

        att = [{"s_free": h_ready, "pt_free": h_ready, "out": []} for _ in range(NB)]
        k_ready, q_ready = Ready(), Ready()

        def attention_1(b):
            for g in range(NKV):
                att[b]["out_free"] = list(q_ready.of(2 * g))
                def score(j, ps, g=g):
                    hh = 4 * g + j
                    at_p = slice(HD * (hh % 2), HD * (hh % 2) + HD)
                    return lambda e: e.matmul(ps, q_cols[at_p, hh // 2, b * P:(b + 1) * P],
                                              k_cols[at_p, g, :], start=True, stop=True)

                def bias(sb, pair, ps, m, free):
                    mask = window[:, (1 - b) * P:(1 - b) * P + S].unsqueeze(1).broadcast_to([P, 2, S])
                    return dve.do(lambda e: e.scalar_tensor_tensor(
                        out=sb[:, pair::2, :], in0=ps[:].rearrange("p (j s) -> p j s", j=2),
                        scalar=HD ** -0.5, in1=mask, op0=ALU.mult, op1=ALU.add), m, free, win_in)

                yield from attention(
                    score, bias, row("sink")[:, 4 * g:4 * g + 4],
                    lambda j, kb, g=g: v_rows[:, kb, g, :], HD,
                    q_rows[:, b, 256 * g:256 * g + 256].rearrange("p (j d) -> p j d", j=4),
                    s_buf[b], pt_buf[b], att[b], [k_ready, q_ready.of(2 * g), qkv_marks["v"], win_in])

        def take_gate(n, ps, m):
            m = act.do(lambda e: e.activation(gate_c[:, n, :], ps, ACT.Copy), m, rope_gone)
            gate_marks.append(m)
            return [m]

        gate_marks = []
        side.add(recurrence(), delay=4)
        side.beside(gemm_cols(ws, h_hi, h_lo, h_ready, KT, LT, take_rec))

        def flip_k():
            return flip_steps(k_ready, lambda b, t: k_rows[:, b, t, :, :].rearrange("p a d -> p (a d)"), None,
                              None, NKV, qkv_marks["k"], plain=k_cols)

        def flip_q(part):
            marks = [[qkv_marks["q"][b][part]] for b in range(NB)]
            yield from flip_steps(q_ready, lambda b, t: q_rows[:, b, t * P:(t + 1) * P], None, None, NQ // 2,
                                  marks, plain=q_cols, first=4 * part, last=4 * part + 4)

        step = 0
        for _ in gemm_rows(ws, h_hi, h_lo, h_ready, KT, 3, take_qkv):
            step += 1
            if step == 5:
                side.add(flip_k())
            if step == 9:
                side.add(flip_q(0))
            if step == 11:
                side.add(attention_1(0))
                side.add(attention_1(1), delay=2)
            side.step()
        rope_gone = [dve.mark()]
        side.add(flip_q(1), delay=1)
        side.beside(gemm_cols(ws, h_hi, h_lo, h_ready, KT, LT, take_gate))
        h_free = [pe.mark()]
        while len(lru_done) < 4:
            side.step()

        T0 = AW // P
        ylru = gate_c
        m = act.do(lambda e: e.activation(gate_c[:], gate_c[:], ACT.Gelu_apprx_tanh), gate_marks)
        m = dve.do(lambda e: e.tensor_tensor(ylru[:], gate_c[:], h_sum[:], ALU.mult), lru_done, m)
        m2 = act.do(lambda e: e.activation(h_sum[:], ylru[:], ACT.Square), m)
        ones = at("ones", o + 34 * KB, [P, P])
        rs_bc = at("rs_bc", o + 35 * KB, [P, S])
        k = pool.do(lambda e: e.memset(ones[:], 1.0), lru_done)
        i = take("side")
        pe_wait_bank(i)
        pe.wait(m2, k)
        for t in range(LT):
            fn = lambda e, t=t, i=i: e.matmul(psum[i][:, 0:S], ones[:], h_sum[:, t, :], start=t == 0, stop=t == LT - 1)
            m3 = pe.do(fn) if t == LT - 1 else pe.quiet(fn)
        m = dve.do(lambda e, i=i: e.tensor_scalar(rs_bc[:], psum[i][:, 0:S], 1.0 / LW, EPS, ALU.mult, ALU.add), m3, k)
        bank_free[i] = [m]
        m = act.do(lambda e: e.activation(rs_bc[:], rs_bc[:], ACT.Sqrt), m)
        m = dve.do(lambda e: e.reciprocal(rs_bc[:], rs_bc[:]), m)
        side.step()
        ylru_ready = Ready()
        for t4 in (0, 4):
            for t in range(t4, t4 + 4):
                m1 = dve.do(lambda e, t=t: e.scalar_tensor_tensor(
                    out=ylru[:, t, :], in0=ylru[:, t, :], scalar=col("g_lru_out", t), in1=rs_bc[:],
                    op0=ALU.mult, op1=ALU.mult), m, m2)
            part, to = slice(t4, t4 + 4), slice(T0 + t4, T0 + t4 + 4)
            a = act.do(lambda e, part=part, to=to: e.activation(h_hi[:, to, :], ylru[:, part, :], ACT.Copy), m1, h_free)
            d = dve.do(lambda e, part=part, to=to: e.tensor_tensor(
                h_lo[:, to, :], ylru[:, part, :], h_hi[:, to, :].bitcast(F32), ALU.subtract), a, h_free)
            ylru_ready.put(t4 // 4, d)

        def add_to_x(n, b, ps, m):
            return [dve.do(lambda e: e.tensor_tensor(x[:, b, QUARTERS[n]], ps, x[:, b, QUARTERS[n]], ALU.add), m)]

        def add_and_square(sums, squared, *after):
            def consume(n, b, ps, m):
                m = add_to_x(n, b, ps, m)
                squared[b].append(square_of(b, n, sums[b], m, *after))
                return m
            return consume

        g_att = at("g_att", o + 36 * KB, [P, AW])
        y_rows = at("y_rows", SCR, [P, NB, AW])
        g_att_in = sp.dma(g_att[:], A["g_attn_out"], gain_sem, lru_done)
        y_ready = Ready()

        def finish_attention():
            while len(att[0]["out"]) < NKV or len(att[1]["out"]) < NKV:
                yield
            marks = norm_rows(lambda b: q_rows[:, b, :], lambda b: y_rows[:, b, :], g_att[:], AW,
                              att[0]["out"], att[1]["out"], g_att_in, lru_done)
            yield
            yield from flip_steps(y_ready, lambda b, t: y_rows[:, b, t * P:(t + 1) * P], h_hi, h_lo, T0, marks,
                                  free=h_free)

        side.add(finish_attention(), rate=2)
        side.beside(gemm_rows(ws, h_hi[:, T0:KT, :], h_lo[:, T0:KT, :], ylru_ready, LT, D // BANK, add_to_x))
        side.finish()
        gone = [dve.mark(), act.mark(), pe.mark(), pool.mark()]
        gain = load_gain("g_ffn", gone)
        sums, squared = [columns(4) for _ in range(NB)], [[], []]
        for _ in gemm_rows(ws, h_hi, h_lo, y_ready, T0, D // BANK, add_and_square(sums, squared, gone)):
            pass

        h_free = [pe.mark()]
        f_ready = Ready()
        xn_rows = norm_to_columns(sums, squared, gain, f_ready, h_hi, h_lo, free=h_free)
        gone = [gone, h_free]

        N_U, N_V = 5, 5
        u_rows = [at(f"u_rows{i}", a, [P, D]) for i, a in enumerate(
            (PH0, PH0 + 8 * KB, WR, WR + 8 * KB, WR + 24 * KB))]
        v_emb_rows = [at(f"v_rows{i}", a, [P, D]) for i, a in enumerate(
            (WR + 48 * KB, WR + 32 * KB, WR + 56 * KB, WR + 16 * KB, WR + 40 * KB))]
        o = PH0 + 16 * KB
        sub_k = at("sub_k", o, [P, 2 * PH, N_KEYS])
        scores1 = at("scores1", o + 8 * KB, [P, 2 * PH, N_KEYS])
        scores0 = at("scores0", o + 16 * KB, [P, 2, N_KEYS])
        qp = [at(f"qp{i}", o + 17 * KB + KB * i, [P, S]) for i in range(2)]
        o += 19 * KB
        val = at("val", o, [P, NB, 2 * PH, TOPK])
        idx = at("idx", o + 2 * KB, [P, NB, 2 * PH, TOPK], U32)
        cand = at("cand", o + 4 * KB, [P, TOPK, TOPK])
        eq = at("eq", o + 5 * KB, [P, TOPK, TOPK])
        best = at("best", o + 6 * KB, [P, NB, PH, TOPK])
        pos = at("pos", o + 7 * KB, [P, NB, PH, TOPK], U32)
        half_u = [at(f"half_u{i}", o + 8 * KB + 64 * i, [P, TOPK], U32) for i in range(2)]
        pick = [at(f"pick{i}", o + 8 * KB + 384 + 64 * i, [P, TOPK]) for i in range(2)]
        expert = at("expert", o + 9 * KB, [P, NB, NE], U32)
        gates = at("gates", o + 10 * KB, [P, NB, NE])
        dots = at("dots", o + 11 * KB, [P, NB, NE])
        wts = at("wts", o + 12 * KB, [P, NB, NE])
        diag = [at(f"diag{i}", o + 13 * KB + 512 * i, [P, P]) for i in range(4)]
        subk_sem = [sem("sub_k_in"), 0]
        subk_in = sp.dma(sub_k[:], A["sub_k"], subk_sem, gone)
        score_marks = {}

        def top16(values, src, indices, after):
            m = dve.do(lambda e: e.max(values[:, 0:8], src), after)
            m = dve.do(lambda e: e.max_index(indices[:, 0:8], values[:, 0:8], src), m)
            m = dve.do(lambda e: e.match_replace(src, values[:, 0:8], src, -3e38), m)
            m = dve.do(lambda e: e.max(values[:, 8:16], src), m)
            return dve.do(lambda e: e.max_index(indices[:, 8:16], values[:, 8:16], src), m)

        def route_half(b, n):
            src = scores0[:, n % 2, :] if b == 0 else scores1[:, n, :]
            return top16(val[:, b, n, :], src, idx[:, b, n, :], [score_marks[n], gone])

        def route_head(b, h):
            m = dve.do(lambda e: e.tensor_tensor(
                cand[:], val[:, b, 2 * h, :].unsqueeze(2).broadcast_to([P, TOPK, TOPK]),
                val[:, b, 2 * h + 1, :].unsqueeze(1).broadcast_to([P, TOPK, TOPK]), ALU.add))
            m = top16(best[:, b, h, :], cand[:].rearrange("p a b -> p (a b)"), pos[:, b, h, :], [m])
            yield
            g = gates[:, b, h * TOPK:(h + 1) * TOPK]
            tot, rec, neg = columns(1), columns(1), columns(1)
            k = dve.do(lambda e: e.tensor_scalar(neg, best[:, b, h, 0:1], -1.0, None, ALU.mult), m)
            k = act.do(lambda e: e.activation(g, best[:, b, h, :], ACT.Exp, bias=neg, accum_out=tot), k)
            m1 = dve.do(lambda e: e.tensor_scalar(half_u[0][:], pos[:, b, h, :], 4, None, ALU.logical_shift_right), m)
            m2 = dve.do(lambda e: e.tensor_scalar(half_u[1][:], pos[:, b, h, :], 15, None, ALU.bitwise_and), m)
            yield
            iota = row("iota16").unsqueeze(1).broadcast_to([P, TOPK, TOPK])
            for i in range(2):
                m = EQ.do(lambda e, i=i: e.tensor_tensor(
                    eq[:], half_u[i][:].unsqueeze(2).broadcast_to([P, TOPK, TOPK]), iota, ALU.is_equal), m, m1, m2)
                m = EQ.do(lambda e, i=i: e.tensor_tensor(
                    eq[:], eq[:], idx[:, b, 2 * h + i:2 * h + i + 1, :].broadcast_to([P, TOPK, TOPK]), ALU.mult), m)
                m = dve.do(lambda e, i=i: e.tensor_reduce(pick[i][:], eq[:], AX.X, ALU.add), m)
                yield
            experts_of[b, h] = dve.do(lambda e: e.scalar_tensor_tensor(
                out=expert[:, b, h * TOPK:(h + 1) * TOPK], in0=pick[0][:], scalar=float(N_KEYS),
                in1=pick[1][:], op0=ALU.mult, op1=ALU.add), m)
            m = dve.do(lambda e: e.reciprocal(rec, tot), k)
            gates_of[b, h] = dve.do(lambda e: e.tensor_scalar(g, g, rec, None, ALU.mult), m)
            yield

        EQ = dve
        experts_of, gates_of = {}, {}
        qp_free = [[gone], [gone]]

        def take_pq(n, ps, m):
            q = qp[n % 2]
            m = act.do(lambda e: e.activation(q[:], ps, ACT.Copy), m, qp_free[n % 2])
            i = take("side")
            pe_wait_bank(i)
            pe.wait(m, subk_in)
            for b in range(NB):
                fn = lambda e, b=b, i=i: e.matmul(psum[i][:, b * P:(b + 1) * P], q[:, b * P:(b + 1) * P],
                                                  sub_k[:, n, :], start=True, stop=True)
                k = pe.do(fn) if b else pe.quiet(fn)
            qp_free[n % 2] = [k]
            act.do(lambda e, i=i: e.activation(scores0[:, n % 2, :], psum[i][:, 0:P], ACT.Copy), k, gone,
                   routed0.get(n - 2))
            c = act.do(lambda e, i=i: e.activation(scores1[:, n, :], psum[i][:, P:2 * P], ACT.Copy), k, gone)
            bank_free[i] = [c]
            score_marks[n] = c
            return [m]

        def route_block_1():
            for h in range(PH):
                for n in (2 * h, 2 * h + 1):
                    route_half(1, n)
                    yield
                yield from route_head(1, h)

        u_sem = [[sem(f"u_in{i}"), 0] for i in range(N_U)]
        v_sem = [[sem(f"v_in{i}"), 0] for i in range(N_V)]
        u_free, v_free = [[gone] for _ in range(N_U)], [[] for _ in range(N_V)]
        v_got = {}
        GROUP, LAG, EARLY = 8, 10, 10
        steps = NB * NE
        ready_w, peer_done = {}, {}
        diag_free = [[] for _ in diag]

        def gather(table, dst, j, counter, *after):
            b, k = j // NE, j % NE
            pool.wait(*after, experts_of[b, k // TOPK])
            counter[1] += 16
            which = expert[:, b, k:k + 1]
            pool.steps.append(lambda e: e.indirect_dma_start(
                dst, None, table, bass.IndirectOffsetOnAxis(ap=which, axis=0)).then_inc(counter[0], 16))
            return (counter[0], counter[1])

        def u_step(j):
            b, k = j // NE, j % NE
            s = j % 2 if j < EARLY else (j - EARLY + 2) % N_U
            got = gather(A["u_emb"], u_rows[s][:], j, u_sem[s], u_free[s])
            m = dve.do(lambda e: e.tensor_tensor_reduce(
                out=u_rows[s][:], in0=u_rows[s][:], in1=xn[:, b, :], scale=1.0, scalar=0.0,
                op0=ALU.mult, op1=ALU.add, accum_out=dots[:, b, k:k + 1]), got, xn_rows)
            u_free[s] = [m]
            if k % GROUP == GROUP - 1:
                g = slice(k - GROUP + 1, k + 1)
                m = act.do(lambda e: e.activation(dots[:, b, g], dots[:, b, g], ACT.Gelu_apprx_tanh), m)
                ready_w[j // GROUP] = dve.do(lambda e: e.tensor_tensor(
                    wts[:, b, g], dots[:, b, g], gates[:, b, g], ALU.mult), m, gates_of[b, k // TOPK])
            return m

        def v_step(j):
            b, k, s = j // NE, j % NE, j % N_V
            got = gather(A["v_emb"], v_emb_rows[s][:], j, v_sem[s], v_free[s])
            q = j % len(diag)
            m = act.do(lambda e: e.activation(diag[q][:], ident[:], ACT.Copy, scale=wts[:, b, k:k + 1]),
                       ready_w[j // GROUP], diag_free[q])
            if k == 0:
                for i in range(4):
                    pe_wait_bank(4 * b + i)
            pe.wait(m, got)
            for i in range(4):
                fn = lambda e, i=i: e.matmul(psum[4 * b + i][:], diag[q][:], v_emb_rows[s][:, i * BANK:(i + 1) * BANK],
                                             start=k == 0, stop=k == NE - 1)
                m = pe.do(fn) if i == 3 else pe.quiet(fn)
            v_free[s] = [m]
            diag_free[q] = [m]
            if k == NE - 1:
                peer_done[b] = m

        n, routed0, early = 0, {}, 0
        for _ in gemm_cols(ws, h_hi, h_lo, f_ready, KT, 2 * PH, take_pq):
            routed0[n] = route_half(0, n)
            if n % 2:
                for _ in route_head(0, n // 2):
                    pass
            if n >= 2 * PH - EARLY:
                u_step(early)
                early += 1
            n += 1
        for s in (2, 3):
            u_free[s] = [ws.raw_free[s - 2]]
        u_free[4] = v_free[0] = [ws.split_free[1]]
        v_free[1] = v_free[2] = [ws.split_free[2]]
        v_free[3] = v_free[4] = [ws.split_free[0]]

        gf_row = at("gf_row", PH0 + 50 * KB, [P, D])
        junk = at("junk", PH0 + 16 * KB, [P, BANK])
        gf_sem = [sem("g_final_in"), 0]
        h_ready = Ready()
        gain_f, u_last = [], {}
        gf_free = pe.mark()

        def enter_layer_2(b, kind):
            if b == 0:
                gain_f.append(sp.dma(gf_row[:], A["g_final"], gf_sem, gone))
                gain_f.append(load_gain("g_mix_2", xn_rows))
                yield
            sx, sy = columns(4), columns(4)
            for q, cut in enumerate(QUARTERS):
                bank = 4 * b + q
                m = dve.do(lambda e, bank=bank, cut=cut: e.tensor_tensor(
                    x[:, b, cut], psum[bank][:], x[:, b, cut], ALU.add), peer_done[b])
                bank_free[bank] = [m]
                mx = square_of(b, q, sx, m, u_last[b])
                m = dve.do(lambda e, cut=cut: e.tensor_tensor(
                    x[:, b, cut], x[:, b, cut], gf_row[:, cut], ALU.mult), mx, gain_f)
                my = act.do(lambda e, q=q, cut=cut: e.activation(
                    junk[:], x[:, b, cut], ACT.Square, accum_out=sy[:, q:q + 1]), m, gf_free)
                if q % 2:
                    yield
            tx, ty, ty_r, r12 = columns(1), columns(1), columns(1), columns(1)
            m = dve.do(lambda e: e.tensor_reduce(tx, sx, AX.X, ALU.add), mx)
            r1, m1 = power_mean(tx, 1, D, m)
            m = dve.do(lambda e: e.tensor_reduce(ty, sy, AX.X, ALU.add), my)
            m = dve.do(lambda e: e.scalar_tensor_tensor(
                out=ty_r, in0=ty, scalar=r1, in1=r1, op0=ALU.mult, op1=ALU.mult), m, m1)
            r2, m2 = power_mean(ty_r, 1, D, m)
            yield
            rows_of = {}
            for q, cut in enumerate(QUARTERS):
                m = act.do(lambda e, cut=cut: e.activation(x[:, b, cut], x[:, b, cut], ACT.Copy, scale=r1), m1)
                rows_of[q] = dve.do(lambda e, cut=cut: e.scalar_tensor_tensor(
                    out=xn[:, b, cut], in0=x[:, b, cut], scalar=r2, in1=g_row[:, cut],
                    op0=ALU.mult, op1=ALU.mult), m, m2)
                if q % 2:
                    yield
            yield from flip_steps(h_ready, lambda b, t: xn[:, b, t * P:(t + 1) * P], h_hi, h_lo, KT, {b: rows_of},
                                  free=gf_free, blocks=(b,), kind=kind)

        side.add(route_block_1())
        for j in range(EARLY, steps + LAG):
            if j < steps:
                if j % NE == NE - 1:
                    u_last[j // NE] = u_step(j)
                else:
                    u_step(j)
            if 0 <= j - LAG < steps:
                v_step(j - LAG)
            if j - LAG == NE - 1:
                side.add(enter_layer_2(0, "main"))
            side.step()
        side.finish()

        ws = Weights([A["w2_lat"][i] for i in range(8)] + [A["w2_kr"][0]]
                     + [A["w2_dil"][i] for i in range(16, 24)]
                     + [A["w2_uq"][i] for i in range(3)] + [A["w2_ukv"][i] for i in range(4)]
                     + [A["w2_dil"][i] for i in range(16)]
                     + [A["w2_gate"][i] for i in range(16)] + [A["w2_omla"][i] for i in range(8)]
                     + [A["w2_gate"][i] for i in range(16, 32)] + [A["w2_odil"][i] for i in range(8)]
                     + [A["w2_o"][i] for i in range(16)]
                     + [c for p0, np_ in ((0, FF_PARTS[0]), (FF_PARTS[0], FF_PARTS[1]))
                        for c in ([A["w2_gu"][2 * (p0 + i) + g] for i in range(np_) for g in range(2)]
                                  + [A["w2_down"][n * (FT // 4) + p0 // 4 + i]
                                     for n in range(4) for i in range(np_ // 4)])])
        ws.raw_free = [u_free[2], u_free[3]]
        ws.split_free = [[v_free[3], v_free[4]], [u_free[4], v_free[0]], [v_free[1], v_free[2]]]
        for _ in range(N_SPLIT):
            ws.split()
        for _ in enter_layer_2(1, "side"):
            pass
        everything = [pe.mark(), dve.mark(), act.mark()]
        for e in (act, dve, pool):
            e.wait(everything)
        small_at[0] = 0
        rope_in = sp.dma(rope_t[:], A["rope2"], const_sem, everything)

        PA = PH0
        lat_hi = at("lat_hi", PA, [P, 2 * QLT, S], F32R)
        lat_lo = at("lat_lo", PA + 8 * KB, [P, 2 * QLT, S], F32R)
        q2_rows = at("q2_rows", PA + 16 * KB, [P, NB, H2, NOPE])
        kn_rows = at("kn_rows", PA + 24 * KB, [P, NB, H2, NOPE])
        v2_rows = at("v2_rows", PA + 32 * KB, [P, NB, H2, VD])
        qr_rows = at("qr_rows", PA + 40 * KB, [P, NB, H2, ROPE])
        kr_cols = at("kr_cols", PA + 44 * KB, [P, S])
        kr_rows = at("kr_rows", PA + 45 * KB, [P, NB, 2, ROPE])
        qr_cols = at("qr_cols", PA + 46 * KB, [P, H2 // 2, S])
        g_lat = at("g_lat", PA + 58 * KB, [P, 2 * QL])
        lat_rows = at("lat_rows", SCR, [P, NB, 2, QL])
        sq_tmp = at("sq_tmp", SCR + 8 * KB, [P, BANK])
        nt_tmp = at("nt_tmp", SCR + 10 * KB, [P, BANK])
        rt_tmp = [at(f"rt_tmp{i}", SCR + 12 * KB + 2 * KB * i, [P, 8, 64]) for i in range(2)]
        dv_rows = at("dv_rows", SCR + 16 * KB, [P, NB, H2, 128])

        tmp_free = [h_ready]

        def head_norm(src, heads, width, gain_name, dst, ready):
            n = heads * width
            ss = columns(heads)
            sq = sq_tmp[:, 0:n].rearrange("p (h w) -> p h w", h=heads)
            nt = nt_tmp[:, 0:n].rearrange("p (h w) -> p h w", h=heads)
            a = act.do(lambda e: e.activation(sq, src, ACT.Square), ready, tmp_free[0])
            m = dve.do(lambda e: e.tensor_reduce(ss, sq, AX.X, ALU.add), a)
            c = dve.do(lambda e: e.tensor_tensor(nt, src, row(gain_name).unsqueeze(1).broadcast_to(
                [P, heads, width]), ALU.mult), a, consts_in)
            r, m = power_mean(ss, heads, width, m)
            d = dve.do(lambda e: e.tensor_tensor(dst, nt, r.unsqueeze(2).broadcast_to([P, heads, width]),
                                                 ALU.mult), m, c)
            tmp_free[0] = [d]
            return c, d

        lat_marks = [[], []]

        def take_lat(n, b, ps, m):
            ss = columns(1)
            a = act.do(lambda e: e.activation(sq_tmp[:], ps, ACT.Square, accum_out=ss), m, tmp_free[0])
            r, k = power_mean(ss, 1, QL, a)
            d = dve.do(lambda e: e.scalar_tensor_tensor(
                out=lat_rows[:, b, n, :], in0=ps, scalar=r, in1=g_lat[:, n * QL:(n + 1) * QL],
                op0=ALU.mult, op1=ALU.mult), k, lat_gain)
            lat_marks[b].append(d)
            return [a, d]

        lat_gain = sp.dma(g_lat[:], A["g_lat"], gain_sem, everything)
        for _ in gemm_rows(ws, h_hi, h_lo, h_ready, KT, 2, take_lat):
            pass

        kr_marks = [[], []]

        def take_kr(n, b, ps, m):
            c, d = head_norm(ps.rearrange("p (h w) -> p h w", h=1), 1, ROPE, "g_k_rope_2",
                             kr_rows[:, b, 0:1, :], m)
            _, r = rope_rows(kr_rows[:, b, 0:1, :], kr_rows[:, b, 1:2, :], 1, b, [t[:, 0:1, :] for t in rt_tmp],
                             [d, rope_in])
            r = dve.do(lambda e: e.tensor_copy(kr_rows[:, b, 0:1, :], kr_rows[:, b, 1:2, :]), r)
            kr_marks[b].append(r)
            return [c]

        for _ in gemm_rows(ws, h_hi, h_lo, h_ready, KT, 1, take_kr, width=ROPE):
            pass

        dil_marks = {"q": [[], []], "k": [[], []], "v": []}

        def take_dv(n, b, ps, m):
            d = act.do(lambda e: e.activation(dv_rows[:, b, 4 * n:4 * n + 4, :].rearrange("p h w -> p (h w)"),
                                              ps, ACT.Copy), m, everything)
            dil_marks["v"].append(d)
            return [d]

        lat_ready, kr_ready = Ready(), Ready()
        side.add(flip_steps(lat_ready, lambda b, t: lat_rows[:, b, t // QLT, (t % QLT) * P:(t % QLT + 1) * P],
                            lat_hi, lat_lo, 2 * QLT, lat_marks, free=everything))
        side.add(flip_steps(kr_ready, lambda b, t: kr_rows[:, b, :, :].rearrange("p a d -> p (a d)"), None, None, 1,
                            kr_marks, free=everything, plain=kr_cols[:].unsqueeze(1)))
        side.beside(gemm_rows(ws, h_hi, h_lo, h_ready, KT, 2, take_dv))
        side.finish()

        mla_marks = {"qn": [[], []], "qr": [[], []], "kn": [[], []], "v": []}

        def take_uq(n, b, ps, m):
            if n < 2:
                c, d = head_norm(ps.rearrange("p (h w) -> p h w", h=4), 4, NOPE, "g_q_nope_2",
                                 q2_rows[:, b, 4 * n:4 * n + 4, :], m)
                mla_marks["qn"][b].append(d)
                return [c]
            c, d = head_norm(ps.rearrange("p (h w) -> p h w", h=8), 8, ROPE, "g_q_rope_2", qr_rows[:, b, :, :], m)
            _, r = rope_rows(qr_rows[:, b, :, :], qr_rows[:, b, :, :], 8, b, [t[:] for t in rt_tmp], [d, rope_in])
            mla_marks["qr"][b].append(r)
            return [c]

        for _ in gemm_rows(ws, lat_hi[:, 0:QLT, :], lat_lo[:, 0:QLT, :], lat_ready, QLT, 3, take_uq):
            pass

        def take_ukv(n, b, ps, m):
            if n < 2:
                c, d = head_norm(ps.rearrange("p (h w) -> p h w", h=4), 4, NOPE, "g_k_nope_2",
                                 kn_rows[:, b, 4 * n:4 * n + 4, :], m)
                mla_marks["kn"][b].append(d)
                return [c]
            d = act.do(lambda e: e.activation(
                v2_rows[:, b, 4 * (n - 2):4 * (n - 2) + 4, :].rearrange("p h w -> p (h w)"), ps, ACT.Copy), m)
            mla_marks["v"].append(d)
            return [d]

        lat_ready_kv = Ready()
        for m in lat_ready:
            lat_ready_kv.put(0, m)
        for _ in gemm_rows(ws, lat_hi[:, QLT:2 * QLT, :], lat_lo[:, QLT:2 * QLT, :], lat_ready_kv, QLT, 4, take_ukv):
            pass

        lat_gone = [pe.mark()]
        qn_cols = at("qn_cols", PA, [P, H2, S])
        kn_cols = at("kn_cols", PA + 8 * KB, [P, H2, S])
        mla_ready, q2_flipped, kn_flipped = Ready(), Ready(), Ready()

        def mla_flips():
            yield from flip_steps(q2_flipped, lambda b, t: q2_rows[:, b, t, :], None, None, H2, mla_marks["qn"],
                                  free=lat_gone, plain=qn_cols)
            yield from flip_steps(kn_flipped, lambda b, t: kn_rows[:, b, t, :], None, None, H2, mla_marks["kn"],
                                  free=lat_gone, plain=kn_cols)
            yield from flip_steps(mla_ready, lambda b, t: qr_rows[:, b, 2 * t:2 * t + 2, :].rearrange(
                "p a d -> p (a d)"), None, None, H2 // 2, mla_marks["qr"], plain=qr_cols)
            mla_ready.extend([q2_flipped, kn_flipped, kr_ready, mla_marks["v"]])
            side.add(attention_mla(0))
            side.add(attention_mla(1), delay=2)

        dq_rows = at("dq_rows", PA + 16 * KB, [P, NB, H2, 128])
        dk_rows = at("dk_rows", PA + 24 * KB, [P, NB, H2, 128])
        o2_rows = at("o2_rows", SCR, [P, NB, H2, VD])
        s2_buf = [at(f"s2_buf{b}", a, [P, 4, S]) for b, a in enumerate((PA + 50 * KB, PA + 58 * KB))]
        pt2_buf = [at(f"pt2_buf{b}", a, [P, 4, 2, P]) for b, a in enumerate((PA + 54 * KB, SCR + 12 * KB))]
        mla = [{"s_free": [], "pt_free": [], "out": [], "out_free": [lat_ready]} for _ in range(NB)]

        def attention_mla(b):
            scale = (NOPE + ROPE) ** -0.5
            for g in range(H2 // 4):
                def score(j, ps, g=g):
                    hh = 4 * g + j
                    at_p = slice(ROPE * (hh % 2), ROPE * (hh % 2) + ROPE)
                    tok = slice(b * P, (b + 1) * P)
                    pe.quiet(lambda e: e.matmul(ps, qn_cols[:, hh, tok], kn_cols[:, hh, :], start=True, stop=False))
                    return lambda e: e.matmul(ps, qr_cols[at_p, hh // 2, tok], kr_cols[at_p, :],
                                              start=False, stop=True)

                def bias(sb, pair, ps, m, free):
                    return dve.do(lambda e: e.tensor_scalar(
                        sb[:, pair::2, :], ps[:].rearrange("p (j s) -> p j s", j=2),
                        scale, None, ALU.mult), m, free)

                yield from attention(score, bias, None,
                                     lambda j, kb, g=g: v2_rows[:, kb, 4 * g + j, :], VD,
                                     o2_rows[:, b, 4 * g:4 * g + 4, :], s2_buf[b], pt2_buf[b], mla[b], mla_ready)

        def take_dil(n, b, ps, m):
            which, part = n // 2, n % 2
            dst = (dq_rows, dk_rows)[which][:, b, 4 * part:4 * part + 4, :]
            flipped = (q2_flipped, kn_flipped)[which]
            assert len(flipped) == 4
            c, d = head_norm(ps.rearrange("p (h w) -> p h w", h=4), 4, 128, ("g_q_dil_2", "g_k_dil_2")[which],
                             dst, [m, flipped])
            dil_marks["qk"[which]][b].append(d)
            return [c]

        side.add(mla_flips(), rate=2)
        side.beside(gemm_rows(ws, h_hi, h_lo, h_ready, KT, 4, take_dil))
        side.finish()

        om_hi = at("om_hi", PA, [P, H2, S], F32R)
        om_lo = at("om_lo", PA + 8 * KB, [P, H2, S], F32R)
        mla_gone = [pe.mark()]
        dk_cols = at("dk_cols", PA + 32 * KB, [P, H2, S])
        dq_cols = at("dq_cols", PA + 40 * KB, [P, H2, S])
        g_cols = at("g_cols", PA + 16 * KB, [P, KT, S])
        dil_ready, om_ready = Ready(), Ready()
        for _ in flip_steps(dil_ready, lambda b, t: dq_rows[:, b, t, :], None, None, H2, dil_marks["q"],
                            free=mla_gone, plain=dq_cols):
            pass
        dist = at("dist", SCR + 8 * KB, [P, 2, 384])
        dist_sem = [sem("dist_in"), 0]
        dist_in = sp.dma(dist[:], A["dist"], dist_sem, dve.mark(), act.mark())
        dil = [{"s_free": mla[b]["s_free"], "pt_free": mla[b]["pt_free"], "out": [], "out_free": [om_ready]}
               for b in range(NB)]

        def dil_flips():
            yield from flip_steps(dil_ready, lambda b, t: dk_rows[:, b, t, :], None, None, H2, dil_marks["k"],
                                  free=mla_gone, plain=dk_cols)
            yield from flip_steps(om_ready, lambda b, t: o2_rows[:, b, t, :], om_hi, om_lo, H2,
                                  [mla[0]["out"], mla[1]["out"]], free=mla_gone)
            dil_ready.extend(dil_marks["v"])
            side.add(attention_dil(0))
            side.add(attention_dil(1), delay=2)

        def attention_dil(b):
            for g in range(H2 // 4):
                def score(j, ps, g=g):
                    hh = 4 * g + j
                    return lambda e: e.matmul(ps, dq_cols[:, hh, b * P:(b + 1) * P], dk_cols[:, hh, :],
                                              start=True, stop=True)

                def bias(sb, pair, ps, m, free, g=g):
                    cut = slice((1 - b) * P, (1 - b) * P + S)
                    for j in (pair, pair + 2):
                        slope = 2.0 ** (-8.0 * (4 * g + j + 1) / H2)
                        k = dve.do(lambda e, j=j, slope=slope: e.scalar_tensor_tensor(
                            out=sb[:, j, :], in0=dist[:, 0, cut], scalar=-slope, in1=dist[:, 1, cut],
                            op0=ALU.mult, op1=ALU.add), free, dist_in)
                    return dve.do(lambda e: e.scalar_tensor_tensor(
                        out=sb[:, pair::2, :], in0=ps[:].rearrange("p (j s) -> p j s", j=2),
                        scalar=128 ** -0.5, in1=sb[:, pair::2, :], op0=ALU.mult, op1=ALU.add), m, k)

                yield from attention(score, bias, None,
                                     lambda j, kb, g=g: dv_rows[:, kb, 4 * g + j, :], 128,
                                     o2_rows[:, b, 4 * g:4 * g + 4, :], s2_buf[b], pt2_buf[b], dil[b], dil_ready)

        def take_g0(n, ps, m):
            if n == H2:
                assert len(dil_ready) >= 8
            m = act.do(lambda e: e.activation(g_cols[:, n, :], ps, ACT.Identity, bias=col("b_gate_2", n)),
                       m, list(dil_ready))
            g0_marks.append(m)
            return [m]

        def take_ya(n, ps, m):
            m = dve.do(lambda e: e.tensor_tensor(g_cols[:, n, :], ps, g_cols[:, n, :], ALU.mult), m, g0_sig)
            z_marks[n] = m
            return [m]

        g0_marks, z_marks, g0_sig = [], {}, []
        side.add(dil_flips(), rate=2)
        side.beside(gemm_cols(ws, h_hi, h_lo, h_ready, KT, KT, take_g0))
        g0_sig.append(act.do(lambda e: e.activation(g_cols[:], g_cols[:], ACT.Sigmoid), g0_marks))
        side.beside(gemm_cols(ws, om_hi, om_lo, om_ready, H2, KT, take_ya))
        side.finish()

        od_hi = at("od_hi", PA + 32 * KB, [P, H2, S], F32R)
        od_lo = at("od_lo", PA + 40 * KB, [P, H2, S], F32R)
        att_gone = [pe.mark()]
        od_ready = Ready()
        side.add(flip_steps(od_ready, lambda b, t: o2_rows[:, b, t, :], od_hi, od_lo, H2,
                            [dil[0]["out"], dil[1]["out"]], free=att_gone))
        g1_cols = at("g1_cols", SCR + 8 * KB, [P, KT, S])
        g1_marks, z_ready = [], Ready()

        def take_g1(n, ps, m):
            g1_marks.append(act.do(lambda e: e.activation(g1_cols[:, n, :], ps, ACT.Sigmoid,
                                                          bias=col("b_gate_2", KT + n)), m, att_gone, dil_read))
            return [g1_marks[n]]

        def take_yb(n, ps, m):
            m = dve.do(lambda e: e.tensor_tensor(g1_cols[:, n, :], ps, g1_cols[:, n, :], ALU.mult), m, g1_marks[n])
            k = dve.do(lambda e: e.tensor_tensor(g_cols[:, n, :], g_cols[:, n, :], g1_cols[:, n, :], ALU.add),
                       m, z_marks[n])
            a = act.do(lambda e: e.activation(h_hi[:, n, :], g_cols[:, n, :], ACT.Copy), k, h_free)
            z_ready.put(n // 4, dve.do(lambda e: e.tensor_tensor(
                h_lo[:, n, :], g_cols[:, n, :], h_hi[:, n, :].bitcast(F32), ALU.subtract), a, h_free))
            return [m]

        dil_read = [dve.mark()]
        side.beside(gemm_cols(ws, h_hi, h_lo, h_ready, KT, KT, take_g1))
        side.finish()
        h_free = [pe.mark()]
        for _ in gemm_cols(ws, od_hi, od_lo, od_ready, H2, KT, take_yb):
            pass
        gone = [act.mark(), dve.mark(), pe.mark()]
        gain = load_gain("g_ffn_2", gone)
        sums, squared = [columns(4) for _ in range(NB)], [[], []]
        for _ in gemm_rows(ws, h_hi, h_lo, z_ready, KT, D // BANK, add_and_square(sums, squared, gone)):
            pass

        h_free = [pe.mark()]
        gone = [pe.mark(), dve.mark(), act.mark()]
        f_ready = Ready()
        norm_to_columns(sums, squared, gain, f_ready, h_hi, h_lo, free=h_free)
        hid_hi = at("hid_hi", PA, [P, FF_PARTS[0], S], F32R)
        hid_lo = at("hid_lo", PA + 24 * KB, [P, FF_PARTS[0], S], F32R)
        g_tmp = [at(f"silu_tmp{i}", PA + 48 * KB + KB * i, [P, S]) for i in range(4)]
        hid_free = gone
        g_free = [[gone] for _ in g_tmp]
        n_g = [0]
        out_sem = [sem("out_done"), 0]
        for part, tiles in enumerate(FF_PARTS):
            hid_ready, silu_marks = Ready(), {}

            def take_gu(n, ps, m):
                i, s = n // 2, (n // 2) % 4
                if n % 2 == 0:
                    silu_marks[i] = act.do(lambda e: e.activation(g_tmp[s][:], ps, ACT.Silu), m, g_free[s])
                    return [silu_marks[i]]
                d = dve.do(lambda e: e.tensor_tensor(g_tmp[s][:], ps, g_tmp[s][:], ALU.mult), m, silu_marks[i])
                a = act.do(lambda e: e.activation(hid_hi[:, i, :], g_tmp[s][:], ACT.Copy), d, hid_free)
                k = dve.do(lambda e: e.tensor_tensor(hid_lo[:, i, :], g_tmp[s][:], hid_hi[:, i, :].bitcast(F32),
                                                     ALU.subtract), a, hid_free)
                g_free[s] = [a, k]
                hid_ready.put(i // 4, k)
                return [d]

            for _ in gemm_cols(ws, h_hi, h_lo, f_ready, KT, 2 * tiles, take_gu):
                pass

            def to_x(n, b, ps, m):
                cut = slice(n * BANK, (n + 1) * BANK)
                m = dve.do(lambda e: e.tensor_tensor(x[:, b, cut], ps, x[:, b, cut], ALU.add), m)
                if part == len(FF_PARTS) - 1:
                    sp.dma(out[b * P:(b + 1) * P, cut], x[:, b, cut], out_sem, m)
                return [m]

            for _ in gemm_rows(ws, hid_hi, hid_lo, hid_ready, tiles, D // BANK, to_x):
                pass
            hid_free = [pe.mark()]
        sp.wait((out_sem[0], out_sem[1]))

        block = ctx.enter_context(nc.Block())

        @block.sync
        def _(e):
            sp.play(e)

        @block.scalar
        def _(e):
            act.play(e)

        @block.vector
        def _(e):
            dve.play(e)

        @block.gpsimd
        def _(e):
            pool.play(e)

        @block.tensor
        def _(e):
            pe.play(e)


def chunks_rows(w, width=BANK):
    k, n = w.shape
    per = WCH // width
    kt = k // P
    per = min(per, kt)
    w = w.reshape(kt // per, per, P, n // width, width).transpose(3, 0, 2, 1, 4)
    return np.ascontiguousarray(w).reshape(-1, P, per * width)


def chunks_cols(w):
    k, n = w.shape
    kt = k // P
    per = WCH // (P * kt)
    w = w.reshape(kt, P, n // (P * per), per, P).transpose(2, 1, 3, 0, 4)
    return np.ascontiguousarray(w).reshape(-1, P, WCH)


def columns_of(v):
    return np.ascontiguousarray(v.reshape(-1, P).T)


def layout(i):
    f = np.float32
    c = {}
    x = i["x"].reshape(NB, P, D)
    c["x"] = np.ascontiguousarray(x.transpose(1, 0, 2))
    c["ident"] = np.eye(P, dtype=f)
    col = {n: columns_of(i[n][0]) for n, _ in COLS}
    c["cols"] = np.ascontiguousarray(np.concatenate([col[n] for n, _ in COLS], axis=1))
    row = {n: i[n][0] for n, _ in ROWS if n != "iota16"}
    row["iota16"] = np.arange(TOPK, dtype=f)
    c["rows"] = np.ascontiguousarray(np.broadcast_to(np.concatenate([row[n] for n, _ in ROWS]), (P, N_ROWS)))

    def every_partition(v):
        return np.ascontiguousarray(np.broadcast_to(v, (P, D)))

    for n in ("g_mix", "g_ffn", "g_mix_2", "g_ffn_2"):
        c[n] = every_partition(i[n][0])
    c["g_final"] = every_partition(i["g_final"])
    c["g_attn_out"] = np.ascontiguousarray(np.broadcast_to(i["g_attn_out"][0], (P, AW)))
    c["g_lat"] = np.ascontiguousarray(np.broadcast_to(
        np.concatenate([i["g_cq_2"][0], i["g_ckv_2"][0]]), (P, 2 * QL)))

    pos = np.arange(S, dtype=f)[:, None]
    def table(inv):
        ang = pos * inv[None, :]
        cos, sin = np.cos(ang).astype(f), np.sin(ang).astype(f)
        t = np.stack([np.concatenate([cos, cos], 1), np.concatenate([-sin, sin], 1)], 1)
        return np.ascontiguousarray(t.reshape(NB, P, 2, 64).transpose(1, 0, 2, 3))
    c["rope1"] = table((f(10000.0) ** (-np.arange(32, dtype=f) / f(32))).astype(f))
    c["rope2"] = table((f(10000.0) ** (-np.arange(0, 64, 2, dtype=f) / f(64))).astype(f))
    delta = np.arange(384)[None, :] - P - np.arange(P)[:, None]
    c["window"] = np.where(np.abs(delta) <= 128, 0.0, NEG).astype(f)
    count = (np.abs(delta) <= 64).astype(int) + (delta % 4 == 0) + (delta % 16 == 0)
    c["dist"] = np.ascontiguousarray(np.stack(
        [np.abs(delta).astype(f), np.where(count > 0, np.log(np.maximum(count, 1)), NEG).astype(f)], 1))

    w = i["w_in"][0]
    c["w1_qkv"] = chunks_rows(w[:, :1536])
    c["w1_gate"] = chunks_cols(w[:, 1536:2560])
    c["w1_rec"] = chunks_cols(w[:, 2560:3584])
    lru = np.zeros((LT, P, 4, P), f)
    for k, n in enumerate(("fwd_wa", "fwd_wx", "bwd_wa", "bwd_wx")):
        a = i[n][0]
        for t in range(LT):
            lru[t, 0:64, k, 0:64] = a[2 * t]
            lru[t, 64:128, k, 64:128] = a[2 * t + 1]
    c["lru_w"] = lru
    c["w1_out"] = chunks_rows(i["w_out"][0])
    c["w1_pq"] = chunks_cols(i["w_pq"][0])
    sk = np.stack([i["sub_k1"][0], i["sub_k2"][0]], 1)
    c["sub_k"] = np.ascontiguousarray(sk.reshape(2 * PH, N_KEYS, P).transpose(2, 0, 1))
    c["u_emb"] = i["u_emb"][0]
    c["v_emb"] = i["v_emb"][0]

    w = i["w_in_2"][0]
    c["w2_lat"] = chunks_rows(w[:, 0:1024])
    kr = w[:, 1024:1088].reshape(KT, P, ROPE).transpose(1, 0, 2)
    c["w2_kr"] = np.ascontiguousarray(kr).reshape(1, P, KT * ROPE)
    c["w2_dil"] = chunks_rows(w[:, 1088:4160])
    c["w2_gate"] = chunks_cols(w[:, 4160:])
    uq = i["w_uq_2"][0].reshape(QL, H2, NOPE + ROPE)
    c["w2_uq"] = chunks_rows(np.concatenate([uq[:, :, :NOPE].reshape(QL, -1), uq[:, :, NOPE:].reshape(QL, -1)], 1))
    ukv = i["w_ukv_2"][0].reshape(QL, H2, NOPE + VD)
    c["w2_ukv"] = chunks_rows(np.concatenate([ukv[:, :, :NOPE].reshape(QL, -1), ukv[:, :, NOPE:].reshape(QL, -1)], 1))
    c["w2_omla"] = chunks_cols(i["w_o_mla_2"][0])
    c["w2_odil"] = chunks_cols(i["w_o_dil_2"][0])
    c["w2_o"] = chunks_rows(i["w_o_2"][0])
    gu = i["w_gate_up_2"][0].reshape(D, 2, FT, P).transpose(0, 2, 1, 3).reshape(D, 2 * FF)
    c["w2_gu"] = chunks_cols(gu)
    c["w2_down"] = chunks_rows(i["w_down_2"][0])
    return {k: np.ascontiguousarray(v) for k, v in c.items()}


def program(nc, arrays):
    A = {n: nc.dram_tensor(f"in_{n}", a.shape, F32, kind="ExternalInput").ap() for n, a in arrays.items()}
    out = nc.dram_tensor("out", (S, D), F32, kind="ExternalOutput").ap()
    build(nc, A, out)


def kernel(**inputs):
    import concourse.bacc as bacc
    from concourse.bass_utils import run_bass_kernel_spmd

    arrays = layout({k: np.asarray(v) for k, v in inputs.items()})
    nc = bacc.Bacc("TRN2", target_bir_lowering=False, num_devices=1)
    program(nc, arrays)
    r = run_bass_kernel_spmd(nc, [{f"in_{n}": a for n, a in arrays.items()}], core_ids=[0])
    return r.results[0]["out"].reshape(1, S, D)
```

```python
from contextlib import ExitStack
import math

import numpy as np
import concourse.bass as bass
from concourse import mybir

F32 = mybir.dt.float32
F32R = mybir.dt.float32r
U32 = mybir.dt.uint32
ALU = mybir.AluOpType
ACT = mybir.ActivationFunctionType
AX = mybir.AxisListType

P = 128
S = 256
NB = S // P
D = 2048
KT = D // P
WCH = 2048
BANK = 512

HD = 64
NQ, NKV = 16, 4
AW = NQ * HD
LW = 1024
LT = LW // P
N_KEYS = 128
PH = 8
TOPK = 16
NE = PH * TOPK
PARTS = 8
PT = N_KEYS // PARTS
NOPE, ROPE, VD = 128, 64, 128
H2 = 8
QL = 512
QLT = QL // P
FF = 5632
FT = FF // P
FF_PARTS = (24, 20)
LATENT_ORDER = "dqqdqkdkkdk"
EPS = 1e-6
NEG = -1e30

COLS = [("conv_w", 4 * LT), ("conv_b", LT), ("fwd_ba", LT), ("fwd_bx", LT), ("fwd_lam", LT),
        ("bwd_ba", LT), ("bwd_bx", LT), ("bwd_lam", LT), ("g_lru_out", LT), ("b_gate_2", 2 * KT)]
ROWS = [("sink", NQ), ("g_q_nope_2", NOPE), ("g_q_rope_2", ROPE), ("g_k_nope_2", NOPE),
        ("g_k_rope_2", ROPE), ("g_q_dil_2", 128), ("g_k_dil_2", 128), ("iota", N_KEYS)]


def offsets(table):
    at, out = 0, {}
    for name, n in table:
        out[name] = (at, n)
        at += n
    return out, at


COL_AT, N_COLS = offsets(COLS)
ROW_AT, N_ROWS = offsets(ROWS)


class Engine:

    def __init__(self, sem, chained=False):
        self.sem, self.count, self.steps, self.met = sem, 0, [], {}
        self.chained = chained

    def wait(self, *marks):
        for m in marks:
            if m is None:
                continue
            if isinstance(m, list):
                self.wait(*m)
                continue
            sem, value = m
            if self.met.get(sem.name, 0) < value:
                self.met[sem.name] = value
                self.steps.append(lambda e, sem=sem, value=value: e.wait_ge(sem, value))

    def do(self, fn, *after):
        self.wait(*after)
        if self.chained and self.count:
            self.wait((self.sem, self.count))
        self.count += 1
        self.steps.append(lambda e: fn(e).then_inc(self.sem, 1))
        return (self.sem, self.count)

    def quiet(self, fn, *after):
        self.wait(*after)
        self.steps.append(fn)

    def mark(self):
        return (self.sem, self.count)

    def dma(self, out, in_, counter, *after):
        self.wait(*after)
        counter[1] += 16
        self.steps.append(lambda e: e.dma_start(out, in_).then_inc(counter[0], 16))
        return (counter[0], counter[1])

    def play(self, e):
        for step in self.steps:
            step(e)


class Side:

    def __init__(self):
        self.live = []

    def add(self, stage, rate=1, delay=0):
        self.live.append([stage, rate, delay])

    def step(self):
        for entry in list(self.live):
            if entry[2]:
                entry[2] -= 1
                continue
            for _ in range(entry[1]):
                if next(entry[0], "end") == "end":
                    self.live.remove(entry)
                    break

    def beside(self, main):
        for _ in main:
            self.step()

    def finish(self):
        while self.live:
            self.step()


class Ready(list):

    def __init__(self):
        self.groups = {}

    def put(self, group, mark):
        self.append(mark)
        self.groups.setdefault(group, []).append(mark)

    def of(self, tile):
        return self.groups[tile // 4]


def build(nc, A, G_dram, out):
    ctx = ExitStack()
    with ctx:
        def sem(name):
            return ctx.enter_context(nc.semaphore(name))

        pe, sp = Engine(sem("pe_done")), Engine(None)
        act, dve, pool = (Engine(sem(n), chained=True) for n in ("act_done", "dve_done", "pool_done"))

        base = (nc.sbuf_base + 63) // 64 * 64
        used = {}

        def at(name, offset, shape, dt=F32):
            size = 4 * int(np.prod(shape[1:]))
            used[name] = (offset, offset + size)
            assert base + offset + size <= nc.sbuf_usable_end, (name, offset, size)
            return nc.alloc_sbuf_tensor_at(name, shape, dt, offset=base + offset)

        KB = 1024
        x = at("x", 0, [P, NB, D])
        o = 16 * KB
        ident = at("ident", o, [P, P]); o += 4 * P
        cols = at("cols", o, [P, N_COLS]); o += 4 * N_COLS
        rows = at("rows", o, [P, N_ROWS]); o += 4 * N_ROWS
        rope_t = at("rope_t", o, [P, NB, 2, 64]); o += 4 * NB * 128
        small = at("small", o, [P, 640]); o += 4 * 640
        SCR = (o + 63) // 64 * 64
        HHL = SCR + 24 * KB
        WR = HHL + 32 * KB
        PH0 = WR + 64 * KB
        xn = at("xn", SCR, [P, NB, D])
        g_row = at("g_row", SCR + 16 * KB, [P, D])
        h_hi = at("h_hi", HHL, [P, KT, S], F32R)
        h_lo = at("h_lo", HHL + 16 * KB, [P, KT, S], F32R)
        N_RAW, N_SPLIT = 2, 3
        w_raw = [at(f"w_raw{i}", WR + 8 * KB * i, [P, WCH]) for i in range(N_RAW)]
        w_hi = [at(f"w_hi{i}", WR + 8 * KB * (N_RAW + i), [P, WCH], F32R) for i in range(N_SPLIT)]
        w_lo = [at(f"w_lo{i}", WR + 8 * KB * (N_RAW + N_SPLIT + i), [P, WCH], F32R) for i in range(N_SPLIT)]

        def col(name, i=0):
            a = COL_AT[name][0] + i
            return cols[:, a:a + 1]

        def row(name):
            a, n = ROW_AT[name]
            return rows[:, a:a + n]

        small_at = [0]

        def columns(n):
            a = small_at[0]
            small_at[0] += n
            assert small_at[0] <= 640, small_at
            return small[:, a:a + n]

        psum = [ctx.enter_context(nc.psum_tensor(f"bank{i}", [P, BANK], F32)) for i in range(8)]
        bank_free = [[] for _ in range(8)]
        turn = {"main": 0, "side": 0}

        def take(kind, n=None):
            for _ in range(4):
                i = turn[kind] % 4 + (0 if kind == "main" else 4)
                turn[kind] += 1
                if bank_free[i] is not None:
                    return i
            assert False, "all banks are held"

        def pe_wait_bank(i):
            assert bank_free[i] is not None
            pe.wait(bank_free[i])
            bank_free[i] = None

        const_sem = [sem("consts"), 0]
        x_sem = [[sem(f"x_in{b}"), 0] for b in range(NB)]
        gain_sem = [sem("gains"), 0]
        x_in = [sp.dma(x[:, b, :], A["x"][:, b, :], x_sem[b]) for b in range(NB)]

        def load_gain(name, *after):
            return sp.dma(g_row[:], A[name], gain_sem, *after)

        class Weights:
            raw_sem = [[sem(f"w_raw_in{i}"), 0] for i in range(N_RAW)]

            def __init__(self, chunks):
                self.chunks, self.n_load, self.n_split, self.n_used = chunks, 0, 0, 0
                self.raw_free = [[] for _ in range(N_RAW)]
                self.split_free = [[] for _ in range(N_SPLIT)]
                self.loaded, self.ready = {}, {}

            def load(self):
                i = self.n_load
                if i >= len(self.chunks):
                    return
                self.n_load += 1
                s = i % N_RAW
                src = self.chunks[i]
                n = src.shape[-1]
                self.loaded[i] = sp.dma(w_raw[s][:, 0:n], src, self.raw_sem[s], self.raw_free[s])

            def split(self):
                i = self.n_split
                if i >= len(self.chunks):
                    return
                while self.n_load <= i:
                    self.load()
                self.n_split += 1
                s, r, n = i % N_SPLIT, i % N_RAW, self.chunks[i].shape[-1]
                hi, lo, raw = w_hi[s][:, 0:n], w_lo[s][:, 0:n], w_raw[r][:, 0:n]
                a = act.do(lambda e: e.activation(hi, raw, ACT.Copy), self.loaded[i], self.split_free[s])
                b = dve.do(lambda e: e.tensor_tensor(lo, raw, hi.bitcast(F32), ALU.subtract),
                           self.loaded[i], a, self.split_free[s])
                self.raw_free[r] = [a, b]
                self.ready[i] = b
                self.load()

            def next(self):
                i = self.n_used
                self.n_used += 1
                while self.n_split < min(i + N_SPLIT, len(self.chunks)):
                    self.split()
                self.now = i % N_SPLIT
                return w_hi[self.now], w_lo[self.now], self.ready[i]

            def used(self, mark):
                self.split_free[self.now] = [mark]

        def three(psum_ap, st, mv, first, last):
            pe.quiet(lambda e: e.matmul(psum_ap, st[0], mv[0], start=first, stop=False))
            pe.quiet(lambda e: e.matmul(psum_ap, st[0], mv[1], start=False, stop=False))
            return lambda e: e.matmul(psum_ap, st[1], mv[0], start=False, stop=last)

        def gemm_rows(ws, a_hi, a_lo, ready, tiles, n_out, consume, width=BANK, kind="main"):
            per = WCH // width
            for n in range(n_out):
                banks = [take(kind) for _ in range(NB)]
                for b in banks:
                    pe_wait_bank(b)
                c0 = 0
                while c0 < tiles:
                    k_here = min(per, tiles - c0)
                    hi, lo, split = ws.next()
                    pe.wait(split)
                    for b in range(NB):
                        for k in range(k_here):
                            t = c0 + k
                            pe.wait(ready.of(t))
                            last = t == tiles - 1
                            cut = slice(k * width, (k + 1) * width)
                            tok = slice(b * P, (b + 1) * P)
                            fin = three(psum[banks[b]][:, 0:width], (a_hi[:, t, tok], a_lo[:, t, tok]),
                                        (hi[:, cut], lo[:, cut]), t == 0, last)
                            if k == k_here - 1 and (b == NB - 1 or last):
                                mark = pe.do(fin)
                            else:
                                pe.quiet(fin)
                            if last:
                                done = mark
                                bank_free[banks[b]] = consume(n, b, psum[banks[b]][:, 0:width], done)
                    ws.used(mark)
                    c0 += k_here
                    yield

        def gemm_cols(ws, a_hi, a_lo, ready, tiles, n_out, consume):
            per = WCH // (P * tiles)
            for n in range(n_out):
                if n % per == 0:
                    hi, lo, split = ws.next()
                b = take("main")
                pe_wait_bank(b)
                pe.wait(split)
                for t in range(tiles):
                    pe.wait(ready.of(t))
                    cut = slice(((n % per) * tiles + t) * P, ((n % per) * tiles + t + 1) * P)
                    fin = three(psum[b][:, 0:S], (hi[:, cut], lo[:, cut]), (a_hi[:, t, :], a_lo[:, t, :]),
                                t == 0, t == tiles - 1)
                    if t == tiles - 1:
                        mark = pe.do(fin)
                    else:
                        pe.quiet(fin)
                if n % per == per - 1 or n == n_out - 1:
                    ws.used(mark)
                bank_free[b] = consume(n, psum[b][:, 0:S], mark)
                yield

        def power_mean(ss, n, width, *after):
            v, half, r = columns(n), columns(n), columns(n)
            m = dve.do(lambda e: e.tensor_scalar(v, ss, 1.0 / width, EPS, ALU.mult, ALU.add), *after)
            k = pool.do(lambda e: e.memset(half, -0.5))
            return r, pool.do(lambda e: e.tensor_tensor(r, v, half, ALU.pow), m, k)

        def norm_rows(src, dst, gain, width, *after, blocks=range(NB)):
            marks = []
            for b in blocks:
                ss = columns(1)
                m = act.do(lambda e, b=b, ss=ss: e.activation(dst(b), src(b), ACT.Square, accum_out=ss), *after)
                r, m = power_mean(ss, 1, width, m)
                marks.append(dve.do(lambda e, b=b, r=r: e.scalar_tensor_tensor(
                    out=dst(b), in0=src(b), scalar=r, in1=gain, op0=ALU.mult, op1=ALU.mult), m))
            return marks

        QUARTERS = [slice(q * BANK, (q + 1) * BANK) for q in range(D // BANK)]

        def square_of(b, q, sums, *after):
            cut = QUARTERS[q]
            return act.do(lambda e: e.activation(xn[:, b, cut], x[:, b, cut], ACT.Square,
                                                 accum_out=sums[:, q:q + 1]), *after)

        def norm_to_columns(sums, squared, gain_in, out_marks, hi, lo, *after, free=None):
            scale = {}
            for b in range(NB):
                ss = columns(1)
                m = dve.do(lambda e, ss=ss, b=b: e.tensor_reduce(ss, sums[b], AX.X, ALU.add), squared[b])
                scale[b] = power_mean(ss, 1, D, m)
            return rows_to_columns(scale, [gain_in, *after], out_marks, hi, lo, free=free)

        def rows_to_columns(scale, after, out_marks, hi, lo, before=None, free=None):
            rows_of = [{}, {}]

            def make_rows(q):
                cut = QUARTERS[q]
                for b in range(NB):
                    r, m = scale[b]
                    m = [m, before(b, q) if before else None]
                    rows_of[b][q] = dve.do(lambda e, b=b, r=r: e.scalar_tensor_tensor(
                        out=xn[:, b, cut], in0=x[:, b, cut], scalar=r, in1=g_row[:, cut],
                        op0=ALU.mult, op1=ALU.mult), m, after)

            flips = flip_steps(out_marks, lambda b, t: xn[:, b, t * P:(t + 1) * P], hi, lo, KT, rows_of, free=free)
            make_rows(0)
            for q in range(len(QUARTERS)):
                if q + 1 < len(QUARTERS):
                    make_rows(q + 1)
                for _ in range(NB):
                    next(flips)
            next(flips, None)
            return [rows_of[b][q] for b in range(NB) for q in rows_of[b]]

        def flip_steps(out_marks, src, hi, lo, tiles, marks, free=None, plain=None, blocks=range(NB), kind="side",
                       first=0, last=None):
            for t0 in range(first, tiles if last is None else last, 4):
                for b in blocks:
                    n = min(4, tiles - t0)
                    i = take(kind)
                    pe_wait_bank(i)
                    pe.wait(marks[b][t0 // 4] if isinstance(marks[b], dict) else marks[b])
                    for k in range(n):
                        fn = lambda e, k=k, i=i, t0=t0, b=b: e.transpose(
                            psum[i][:, k * P:(k + 1) * P], src(b, t0 + k), ident[:])
                        m = pe.do(fn) if k == n - 1 else pe.quiet(fn)
                    got = psum[i][:, 0:n * P].rearrange("p (k q) -> p k q", q=P)
                    tok = slice(b * P, (b + 1) * P)
                    if plain is not None:
                        a = act.do(lambda e, got=got, t0=t0, n=n, tok=tok: e.activation(
                            plain[:, t0:t0 + n, tok], got, ACT.Copy), m, free)
                        bank_free[i] = [a]
                        out_marks.put(t0 // 4, a)
                        yield
                        continue
                    a = act.do(lambda e, got=got, t0=t0, n=n, tok=tok: e.activation(
                        hi[:, t0:t0 + n, tok], got, ACT.Copy), m, free)
                    d = dve.do(lambda e, got=got, t0=t0, n=n, tok=tok: e.tensor_tensor(
                        lo[:, t0:t0 + n, tok], got, hi[:, t0:t0 + n, tok].bitcast(F32), ALU.subtract), a)
                    bank_free[i] = [a, d]
                    out_marks.put(t0 // 4, d)
                    yield

        def attention(score, bias, sink, value, dv, dst, sbuf_s, sbuf_pt, state, ready):
            pe.wait(ready)
            halves = []
            for pair in range(2):
                i = take("side")
                pe_wait_bank(i)
                for j in (pair, pair + 2):
                    fn = score(j, psum[i][:, (j // 2) * S:(j // 2 + 1) * S])
                    m = pe.do(fn) if j > 1 else pe.quiet(fn)
                halves.append((i, m))
            got = []
            for pair, (i, m) in enumerate(halves):
                d = bias(sbuf_s, pair, psum[i], m, state["s_free"])
                bank_free[i] = [d]
                got.append(d)
            top, neg, tot, rec = columns(4), columns(4), columns(4), columns(4)
            m = dve.do(lambda e: e.tensor_reduce(top, sbuf_s[:], AX.X, ALU.max), got)
            if sink is not None:
                top2 = columns(4)
                m = dve.do(lambda e: e.tensor_tensor(top2, top, sink, ALU.max), m)
            else:
                top2 = top
            m = dve.do(lambda e: e.tensor_scalar(neg, top2, -1.0, None, ALU.mult), m)
            if sink is not None:
                away, ex, tot2 = columns(4), columns(4), columns(4)
                m = dve.do(lambda e: e.tensor_tensor(away, sink, neg, ALU.add), m)
            yield
            es = None
            for j in range(4):
                es = act.do(lambda e, j=j: e.activation(sbuf_s[:, j, :], sbuf_s[:, j, :], ACT.Exp,
                                                        bias=neg[:, j:j + 1], accum_out=tot[:, j:j + 1]), m)
            if sink is not None:
                es2 = act.do(lambda e: e.activation(ex, away, ACT.Exp), m)
            yield
            copies = []
            for pair in range(2):
                i = take("side")
                pe_wait_bank(i)
                pe.wait(es)
                for k in range(4):
                    j, kb = 2 * pair + k // 2, k % 2
                    fn = lambda e, k=k, j=j, kb=kb, i=i: e.transpose(
                        psum[i][:, k * P:(k + 1) * P], sbuf_s[:, j, kb * P:(kb + 1) * P], ident[:])
                    m = pe.do(fn) if k == 3 else pe.quiet(fn)
                dst_pt = sbuf_pt[:, 2 * pair:2 * pair + 2, :, :].rearrange("p j k q -> p (j k q)")
                if pair == 0:
                    c = act.do(lambda e, i=i, d=dst_pt: e.activation(d, psum[i][:], ACT.Copy), m, state["pt_free"])
                else:
                    c = dve.do(lambda e, i=i, d=dst_pt: e.tensor_copy(d, psum[i][:]), m, state["pt_free"])
                bank_free[i] = [c]
                copies.append(c)
            state["s_free"] = [m]
            yield
            if sink is not None:
                inv = dve.do(lambda e: e.tensor_tensor(tot2, tot, ex, ALU.add), es2, es)
            else:
                tot2, inv = tot, es
            inv = dve.do(lambda e: e.reciprocal(rec, tot2), inv)
            i = take("side")
            pe_wait_bank(i)
            pe.wait(copies)
            for j in range(4):
                for kb in range(2):
                    fn = lambda e, j=j, kb=kb, i=i: e.matmul(psum[i][:, j * dv:(j + 1) * dv], sbuf_pt[:, j, kb, :],
                                                        value(j, kb), start=kb == 0, stop=kb == 1)
                    m = pe.do(fn) if (j, kb) == (3, 1) else pe.quiet(fn)
            state["pt_free"] = [m]
            o_ps = psum[i][:, 0:4 * dv].rearrange("p (j d) -> p j d", j=4)
            d = dve.do(lambda e: e.tensor_tensor(dst, o_ps, rec.unsqueeze(2).broadcast_to([P, 4, dv]), ALU.mult),
                       m, inv, state.get("out_free"))
            bank_free[i] = [d]
            state["out"].append(d)
            yield

        def rope_rows(src, dst, heads, b, tmp, ready, bank_mark=None):
            cos = rope_t[:, b, 0, :].unsqueeze(1).broadcast_to([P, heads, 64])
            sin = rope_t[:, b, 1, :].unsqueeze(1).broadcast_to([P, heads, 64])
            t0, t1 = tmp
            a = dve.do(lambda e: e.tensor_tensor(t0, src, cos, ALU.mult), ready)
            dve.do(lambda e: e.tensor_tensor(t1[:, :, 0:32], src[:, :, 32:64], sin[:, :, 0:32], ALU.mult), ready)
            c = dve.do(lambda e: e.tensor_tensor(t1[:, :, 32:64], src[:, :, 0:32], sin[:, :, 32:64], ALU.mult))
            return c, dve.do(lambda e: e.tensor_tensor(dst, t0, t1, ALU.add), a, c)

        o = PH0
        q_rows = at("q_rows", o, [P, NB, AW])
        k_rows = at("k_rows", o + 8 * KB, [P, NB, NKV, 2, HD])
        v_rows = at("v_rows", o + 12 * KB, [P, NB, NKV, HD])
        q_cols = at("q_cols", o + 14 * KB, [P, NQ // 2, S])
        k_cols = at("k_cols", o + 22 * KB, [P, NKV, S])
        s_buf = [at(f"s_buf{b}", a, [P, 4, S]) for b, a in enumerate((o + 26 * KB, SCR + 16 * KB))]
        pt_buf = [at(f"pt_buf{b}", a, [P, 4, 2, P]) for b, a in enumerate((o + 30 * KB, SCR + 20 * KB))]
        rope_tmp = [at(f"rope_tmp{i}", o + 50 * KB + 2 * KB * i, [P, 8, 64]) for i in range(2)]
        c_cols = at("c_cols", o + 34 * KB, [P, LT, S])
        h_sum = at("h_sum", o + 42 * KB, [P, LT, S])
        gate_c = at("gate_c", o + 50 * KB, [P, LT, S])
        window = at("window", o + 58 * KB, [P, 384])
        lru_w = [at(f"lru_w{i}", o + 59 * KB + 512 + 2 * KB * i, [P, 4, P]) for i in range(2)]
        sp_sm = at("softplus", o + 63 * KB + 512, [P, 8, LT])
        half = [at(f"lru_half{i}", SCR + 4 * KB * i, [P, LT // 2, S]) for i in range(4)]

        win_sem = [sem("window_in"), 0]
        out_chunks = [A["w1_out"][4 * n + 2 * part + c] for part in (1, 0) for n in range(4) for c in range(2)]

        def u_part(p):
            return [A["u_cols"][PT * p + i] for i in range(PT)]

        def v_part(p):
            return [A["v_rows"][n * (N_KEYS // 4) + (PT // 4) * p + i] for n in range(4) for i in range(PT // 4)]

        expert_chunks = u_part(0) + u_part(1)
        for p in range(PARTS):
            expert_chunks += (u_part(p + 2) if p + 2 < PARTS else []) + v_part(p)
        at_i = {"d": 20, "q": 0, "k": 0}
        latent_chunks = []
        for kind in LATENT_ORDER:
            latent_chunks.append(A[{"d": "w2_dil", "q": "w2_uq", "k": "w2_ukv"}[kind]][at_i[kind]])
            at_i[kind] += 1
        ws = Weights([A["w1_rec"][i] for i in range(8)] + [A["w1_qkv"][i] for i in (*range(8, 12), *range(8))]
                     + [A["w1_gate"][i] for i in range(8)] + out_chunks
                     + [A["w1_pq"][i] for i in range(16)] + expert_chunks
                     + [A["w2_lat"][i] for i in range(8)] + [A["w2_kr"][0]]
                     + [A["w2_dil"][i] for i in range(16, 20)] + latent_chunks
                     + [A["w2_dil"][i] for i in range(16)]
                     + [A["w2_gate"][i] for i in range(16)] + [A["w2_omla"][i] for i in range(8)]
                     + [A["w2_gate"][i] for i in range(16, 32)] + [A["w2_odil"][i] for i in range(8)]
                     + [A["w2_o"][i] for i in range(16)]
                     + [c for p0, np_ in ((0, FF_PARTS[0]), (FF_PARTS[0], FF_PARTS[1]))
                        for c in ([A["w2_gu"][2 * (p0 + i) + g] for i in range(np_) for g in range(2)]
                                  + [A["w2_down"][n * (FT // 4) + p0 // 4 + i]
                                     for n in range(4) for i in range(np_ // 4)])])
        gain = load_gain("g_mix")
        ident_sem = [sem("ident_in"), 0]
        ident_in = sp.dma(ident[:], A["ident"], ident_sem)
        for _ in range(N_RAW):
            ws.load()
        for t, name in ((cols, "cols"), (rows, "rows"), (rope_t, "rope1")):
            sp.dma(t[:], A[name], const_sem)
        consts_in = (const_sem[0], const_sem[1])
        win_in = sp.dma(window[:], A["window"], win_sem)
        first_sums, h_ready = [columns(1) for _ in range(NB)], Ready()
        m0 = act.do(lambda e: e.activation(xn[:, 0, :], x[:, 0, :], ACT.Square, accum_out=first_sums[0]), x_in[0])
        m1 = dve.do(lambda e: e.tensor_tensor_reduce(
            out=xn[:, 1, :], in0=x[:, 1, :], in1=x[:, 1, :], scale=1.0, scalar=0.0,
            op0=ALU.mult, op1=ALU.add, accum_out=first_sums[1]), x_in[1])
        norm_to_columns(first_sums, [m0, m1], [gain, ident_in], h_ready, h_hi, h_lo)
        act.wait(consts_in)
        dve.wait(consts_in)

        side = Side()
        rec_marks = []

        def take_rec(n, ps, m):
            def tap(w):
                return col("conv_w", w * LT + n)
            c = c_cols[:, n, :]
            m = act.do(lambda e: e.activation(c, ps, ACT.Identity, bias=col("conv_b", n), scale=tap(2)), m)
            for w, out_at, in_at in ((0, slice(2, S), slice(0, S - 2)), (1, slice(1, S), slice(0, S - 1)),
                                     (3, slice(0, S - 1), slice(1, S))):
                m = dve.do(lambda e, w=w, o_=out_at, i_=in_at: e.scalar_tensor_tensor(
                    out=c[:, o_], in0=ps[:, i_], scalar=tap(w), in1=c[:, o_], op0=ALU.mult, op1=ALU.add), m)
            rec_marks.append(m)
            return [m]

        lru_w_sem = [[sem(f"lru_w_in{i}"), 0] for i in range(2)]
        lru_done = []

        def softplus(d):
            lam = cols[:, COL_AT[("fwd_lam", "bwd_lam")[d]][0]:][:, 0:LT]
            t = [sp_sm[:, 4 * d + i, :] for i in range(4)]
            m = act.do(lambda e: e.activation(t[0], lam, ACT.Abs), consts_in)
            m = act.do(lambda e: e.activation(t[0], t[0], ACT.Exp, scale=-1.0), m)
            m = dve.do(lambda e: e.tensor_scalar(t[0], t[0], 1.0, None, ALU.add), m)
            m = act.do(lambda e: e.activation(t[0], t[0], ACT.Ln), m)
            n = dve.do(lambda e: e.tensor_scalar(t[1], lam, -1.0, 0.0, ALU.mult, ALU.max), consts_in)
            m = dve.do(lambda e: e.tensor_tensor(t[1], t[1], t[0], ALU.add), m, n)
            k = dve.do(lambda e: e.tensor_scalar(t[2], t[1], 8.0, None, ALU.mult), m)
            m = dve.do(lambda e: e.tensor_scalar(t[3], t[1], -8.0, None, ALU.mult), m)
            return t[2], t[3], [k, m]

        def recurrence():
            R, I, T, Q = [h[:] for h in half]
            rounds = [(d, part) for part in range(2) for d in range(2)]
            order = [(d, n) for d, part in rounds for n in range(part * LT // 2, (part + 1) * LT // 2)]
            soft, w_free, w_next, banks = {}, [[], []], {}, {}

            def load_w(k):
                if k < len(order):
                    w_next[k] = sp.dma(lru_w[k % 2][:], A["lru_w"][order[k][1]], lru_w_sem[k % 2], w_free[k % 2])

            def products(k):
                d, n = order[k]
                s, i = k % 2, take("side")
                pe_wait_bank(i)
                pe.wait(w_next[k], rec_marks[n])
                for h in range(2):
                    fn = lambda e, h=h, w=2 * d + h: e.matmul(
                        psum[i][:, h * S:(h + 1) * S], lru_w[s][:, w, :], c_cols[:, n, :], start=True, stop=True)
                    m = pe.do(fn) if h else pe.quiet(fn)
                w_free[s] = [m]
                load_w(k + 2)
                banks[k] = (i, m)

            def gates_of_tile(k, free):
                d, n = order[k]
                i, m = banks[k]
                ba, bx = (("fwd_ba", "fwd_bx"), ("bwd_ba", "bwd_bx"))[d]
                act.do(lambda e: e.activation(R[:, k % 4, :], psum[i][:, 0:S], ACT.Sigmoid, bias=col(ba, n)), m, free)
                a = act.do(lambda e: e.activation(I[:, k % 4, :], psum[i][:, S:2 * S], ACT.Sigmoid, bias=col(bx, n)), m)
                bank_free[i] = [a]
                return a

            load_w(0)
            load_w(1)
            soft = [softplus(d) for d in range(2)]
            for k in range(2):
                products(k)
            yield
            free = h_ready
            for r, (d, part) in enumerate(rounds):
                s_pos, s_neg, sp_done = soft[d]
                k0, t0 = 4 * r, part * LT // 2
                for k in (k0, k0 + 1):
                    gates_of_tile(k, free)
                for k in (k0 + 2, k0 + 3):
                    products(k)
                yield
                for k in (k0 + 2, k0 + 3):
                    m_i = gates_of_tile(k, free)
                for k in range(4):
                    m_t = act.do(lambda e, k=k, s=s_pos[:, t0 + k:t0 + k + 1]: e.activation(
                        T[:, k, :], R[:, k, :], ACT.Tanh, scale=s), sp_done, m_i, free)
                for k in range(4):
                    m_a = act.do(lambda e, k=k, s=s_neg[:, t0 + k:t0 + k + 1]: e.activation(
                        R[:, k, :], R[:, k, :], ACT.Exp, scale=s), m_t)
                yield
                m = dve.do(lambda e: e.tensor_scalar(Q, T, 1.0, None, ALU.add), m_t, free)
                m = dve.do(lambda e: e.reciprocal(Q, Q), m)
                m_q = dve.do(lambda e: e.tensor_tensor(T, T, Q, ALU.mult), m)
                m_c = pool.do(lambda e, t0=t0: e.tensor_tensor(I, I, c_cols[:, t0:t0 + LT // 2, :], ALU.mult), m_i)
                yield
                m_s = act.do(lambda e: e.activation(T, T, ACT.Sqrt, scale=2.0), m_q)
                yield
                m = dve.do(lambda e: e.tensor_tensor(I, I, T, ALU.mult), m_c, m_s)
                for k in range(4):
                    if d == 0:
                        f = dve.do(lambda e, k=k, t0=t0: e.tensor_tensor_scan(
                            h_sum[:, t0 + k, :], R[:, k, :], I[:, k, :], 0.0, ALU.mult, ALU.add), m, m_a)
                    else:
                        f = dve.do(lambda e, k=k: e.tensor_tensor_scan(
                            Q[:, k, ::-1], R[:, k, ::-1], I[:, k, ::-1], 0.0, ALU.mult, ALU.add), m, m_a)
                if d == 1:
                    f = dve.do(lambda e, t0=t0: e.tensor_tensor(
                        h_sum[:, t0:t0 + LT // 2, :], h_sum[:, t0:t0 + LT // 2, :], Q, ALU.add), f)
                free = [f]
                lru_done.append(f)
                if r + 1 < len(rounds):
                    for k in (k0 + 4, k0 + 5):
                        products(k)
                yield

        qkv_marks = {"q": [[], []], "k": [[], []], "v": []}

        def take_qkv(n, b, ps, m):
            n = n - 1
            if n >= 0:
                src = ps.rearrange("p (h d) -> p h d", d=HD)
                dst = q_rows[:, b, n * 512:(n + 1) * 512].rearrange("p (h d) -> p h d", d=HD)
                c, r = rope_rows(src, dst, 8, b, [t[:] for t in rope_tmp], m)
                qkv_marks["q"][b].append(r)
                return [c]
            src = ps[:, 0:256].rearrange("p (h d) -> p h d", d=HD)
            c, r = rope_rows(src, k_rows[:, b, :, 0, :], NKV, b, [t[:, 0:NKV, :] for t in rope_tmp], m)
            r2 = act.do(lambda e: e.activation(k_rows[:, b, :, 1, :], k_rows[:, b, :, 0, :], ACT.Copy), r)
            qkv_marks["k"][b].append(r2)
            v = act.do(lambda e: e.activation(v_rows[:, b, :, :].rearrange("p h d -> p (h d)"), ps[:, 256:512],
                                              ACT.Copy), m)
            qkv_marks["v"].append(v)
            return [c, v]

        att = [{"s_free": h_ready, "pt_free": h_ready, "out": []} for _ in range(NB)]
        k_ready, q_ready = Ready(), Ready()

        def attention_1(b):
            for g in range(NKV):
                att[b]["out_free"] = list(q_ready.of(2 * g))
                def score(j, ps, g=g):
                    hh = 4 * g + j
                    at_p = slice(HD * (hh % 2), HD * (hh % 2) + HD)
                    return lambda e: e.matmul(ps, q_cols[at_p, hh // 2, b * P:(b + 1) * P],
                                              k_cols[at_p, g, :], start=True, stop=True)

                def bias(sb, pair, ps, m, free):
                    mask = window[:, (1 - b) * P:(1 - b) * P + S].unsqueeze(1).broadcast_to([P, 2, S])
                    return dve.do(lambda e: e.scalar_tensor_tensor(
                        out=sb[:, pair::2, :], in0=ps[:].rearrange("p (j s) -> p j s", j=2),
                        scalar=HD ** -0.5, in1=mask, op0=ALU.mult, op1=ALU.add), m, free, win_in)

                yield from attention(
                    score, bias, row("sink")[:, 4 * g:4 * g + 4],
                    lambda j, kb, g=g: v_rows[:, kb, g, :], HD,
                    q_rows[:, b, 256 * g:256 * g + 256].rearrange("p (j d) -> p j d", j=4),
                    s_buf[b], pt_buf[b], att[b], [k_ready, q_ready.of(2 * g), qkv_marks["v"], win_in])

        def take_gate(n, ps, m):
            m = act.do(lambda e: e.activation(gate_c[:, n, :], ps, ACT.Copy), m, rope_gone)
            gate_marks.append(m)
            return [m]

        gate_marks = []
        side.add(recurrence(), delay=4)
        side.beside(gemm_cols(ws, h_hi, h_lo, h_ready, KT, LT, take_rec))

        def flip_k():
            return flip_steps(k_ready, lambda b, t: k_rows[:, b, t, :, :].rearrange("p a d -> p (a d)"), None,
                              None, NKV, qkv_marks["k"], plain=k_cols)

        def flip_q(part):
            marks = [[qkv_marks["q"][b][part]] for b in range(NB)]
            yield from flip_steps(q_ready, lambda b, t: q_rows[:, b, t * P:(t + 1) * P], None, None, NQ // 2,
                                  marks, plain=q_cols, first=4 * part, last=4 * part + 4)

        step = 0
        for _ in gemm_rows(ws, h_hi, h_lo, h_ready, KT, 3, take_qkv):
            step += 1
            if step == 5:
                side.add(flip_k())
            if step == 9:
                side.add(flip_q(0), rate=2)
            if step == 10:
                side.add(attention_1(0))
                side.add(attention_1(1), delay=1)
            side.step()
        rope_gone = [dve.mark()]
        side.add(flip_q(1), delay=1)
        side.beside(gemm_cols(ws, h_hi, h_lo, h_ready, KT, LT, take_gate))
        h_free = [pe.mark()]
        while len(lru_done) < 4:
            side.step()

        T0 = AW // P
        ylru = gate_c
        m = act.do(lambda e: e.activation(gate_c[:], gate_c[:], ACT.Gelu_apprx_tanh), gate_marks)
        m = dve.do(lambda e: e.tensor_tensor(ylru[:], gate_c[:], h_sum[:], ALU.mult), lru_done, m)
        m2 = act.do(lambda e: e.activation(h_sum[:], ylru[:], ACT.Square), m)
        ones = at("ones", o + 34 * KB, [P, P])
        rs_bc = at("rs_bc", o + 35 * KB, [P, S])
        k = pool.do(lambda e: e.memset(ones[:], 1.0), lru_done)
        i = take("side")
        pe_wait_bank(i)
        pe.wait(m2, k)
        for t in range(LT):
            fn = lambda e, t=t, i=i: e.matmul(psum[i][:, 0:S], ones[:], h_sum[:, t, :], start=t == 0, stop=t == LT - 1)
            m3 = pe.do(fn) if t == LT - 1 else pe.quiet(fn)
        m = dve.do(lambda e, i=i: e.tensor_scalar(rs_bc[:], psum[i][:, 0:S], 1.0 / LW, EPS, ALU.mult, ALU.add), m3, k)
        bank_free[i] = [m]
        m = act.do(lambda e: e.activation(rs_bc[:], rs_bc[:], ACT.Sqrt), m)
        m = dve.do(lambda e: e.reciprocal(rs_bc[:], rs_bc[:]), m)
        side.step()
        ylru_ready = Ready()
        for t4 in (0, 4):
            for t in range(t4, t4 + 4):
                m1 = dve.do(lambda e, t=t: e.scalar_tensor_tensor(
                    out=ylru[:, t, :], in0=ylru[:, t, :], scalar=col("g_lru_out", t), in1=rs_bc[:],
                    op0=ALU.mult, op1=ALU.mult), m, m2)
            part, to = slice(t4, t4 + 4), slice(T0 + t4, T0 + t4 + 4)
            a = act.do(lambda e, part=part, to=to: e.activation(h_hi[:, to, :], ylru[:, part, :], ACT.Copy), m1, h_free)
            d = dve.do(lambda e, part=part, to=to: e.tensor_tensor(
                h_lo[:, to, :], ylru[:, part, :], h_hi[:, to, :].bitcast(F32), ALU.subtract), a, h_free)
            ylru_ready.put(t4 // 4, d)

        def add_to_x(n, b, ps, m):
            return [dve.do(lambda e: e.tensor_tensor(x[:, b, QUARTERS[n]], ps, x[:, b, QUARTERS[n]], ALU.add), m)]

        def add_and_square(sums, squared, *after):
            def consume(n, b, ps, m):
                m = add_to_x(n, b, ps, m)
                squared[b].append(square_of(b, n, sums[b], m, *after))
                return m
            return consume

        g_att = at("g_att", o + 36 * KB, [P, AW])
        y_rows = at("y_rows", SCR, [P, NB, AW])
        g_att_in = sp.dma(g_att[:], A["g_attn_out"], gain_sem, lru_done)
        y_ready = Ready()

        def finish_attention(b):
            while len(att[b]["out"]) < NKV:
                yield
            m = norm_rows(lambda b: q_rows[:, b, :], lambda b: y_rows[:, b, :], g_att[:], AW,
                          att[b]["out"], g_att_in, lru_done, blocks=(b,))
            yield
            yield from flip_steps(y_ready, lambda b, t: y_rows[:, b, t * P:(t + 1) * P], h_hi, h_lo, T0, {b: m},
                                  free=h_free, blocks=(b,))

        for b in range(NB):
            side.add(finish_attention(b))
        side.beside(gemm_rows(ws, h_hi[:, T0:KT, :], h_lo[:, T0:KT, :], ylru_ready, LT, D // BANK, add_to_x))
        side.finish()
        gone = [dve.mark(), act.mark(), pe.mark(), pool.mark()]
        gain = load_gain("g_ffn", gone)
        sums, squared = [columns(4) for _ in range(NB)], [[], []]
        for _ in gemm_rows(ws, h_hi, h_lo, y_ready, T0, D // BANK, add_and_square(sums, squared, gone)):
            pass

        h_free = [pe.mark()]
        f_ready = Ready()
        xn_rows = norm_to_columns(sums, squared, gain, f_ready, h_hi, h_lo, free=h_free)
        gone = [gone, h_free]
        acts_free = [gone, gone]

        hid_e = [at("hid_e_hi", PH0, [P, PT, S], F32R), at("hid_e_lo", PH0 + 16 * KB, [P, PT, S], F32R)]
        acts = [at(f"acts{i}", PH0 + (32 + 16 * i) * KB, [P, PT, S]) for i in range(2)]
        g_part = at("g_part", SCR, [P, S, PT])
        o = PH0
        sub_k = at("sub_k", o, [P, 2 * PH, N_KEYS])
        scores1 = at("scores1", o + 8 * KB, [P, 2 * PH, N_KEYS])
        scores0 = at("scores0", o + 16 * KB, [P, 2, N_KEYS])
        qp = [at(f"qp{i}", o + 17 * KB + KB * i, [P, S]) for i in range(2)]
        o += 19 * KB
        val = at("val", o, [P, NB, 2 * PH, TOPK])
        idx = at("idx", o + 2 * KB, [P, NB, 2 * PH, TOPK], U32)
        cand = at("cand", o + 4 * KB, [P, TOPK, TOPK])
        eq = at("eq", PH0 + 56 * KB, [P, PH, TOPK, TOPK])
        best = at("best", o + 6 * KB, [P, NB, PH, TOPK])
        pos = at("pos", o + 7 * KB, [P, NB, PH, TOPK], U32)
        half_u = [at(f"half_u{i}", o + (8 - 3 * i) * KB, [P, PH, TOPK], U32) for i in range(2)]
        picked = at("picked", o + 9 * KB, [P, NB, 3, NE])
        by_choice = at("by_choice", PH0 + 16 * KB, [P, 3, S])
        N_HOT = 16
        hot1 = [at(f"hot1_{i}", PH0 + 512 * i, [P, N_KEYS]) for i in range(N_HOT)]
        hot2 = [at(f"hot2_{i}", SCR + 16 * KB + 512 * i, [P, N_KEYS]) for i in range(N_HOT)]
        stage = [at(f"g_stage{i}", SCR + 8 * KB * i, [P, PARTS, PT, PT]) for i in range(2)]
        subk_sem = [sem("sub_k_in"), 0]
        subk_in = sp.dma(sub_k[:], A["sub_k"], subk_sem, gone)
        score_marks = {}

        def top16(values, src, indices, after):
            m = dve.do(lambda e: e.max(values[:, 0:8], src), after)
            m = dve.do(lambda e: e.max_index(indices[:, 0:8], values[:, 0:8], src), m)
            m = dve.do(lambda e: e.match_replace(src, values[:, 0:8], src, -3e38), m)
            m = dve.do(lambda e: e.max(values[:, 8:16], src), m)
            return dve.do(lambda e: e.max_index(indices[:, 8:16], values[:, 8:16], src), m)

        def route_half(b, n):
            src = scores0[:, n % 2, :] if b == 0 else scores1[:, n, :]
            return top16(val[:, b, n, :], src, idx[:, b, n, :], [score_marks[n], gone])

        def route_head(b, h):
            m = dve.do(lambda e: e.tensor_tensor(
                cand[:], val[:, b, 2 * h, :].unsqueeze(2).broadcast_to([P, TOPK, TOPK]),
                val[:, b, 2 * h + 1, :].unsqueeze(1).broadcast_to([P, TOPK, TOPK]), ALU.add))
            best_of[b].append(top16(best[:, b, h, :], cand[:].rearrange("p a b -> p (a b)"), pos[:, b, h, :], [m]))

        def pick_choices(b):
            g = picked[:, b, 2, :].rearrange("p (h k) -> p h k", h=PH)
            tot, rec = columns(PH), columns(PH)
            m0 = best_of[b]
            k = dve.do(lambda e: e.tensor_tensor(
                g, best[:, b, :, :], best[:, b, :, 0:1].broadcast_to([P, PH, TOPK]), ALU.subtract), m0)
            k = act.do(lambda e: e.activation(g, g, ACT.Exp), k)
            m1 = dve.do(lambda e: e.tensor_scalar(half_u[0][:], pos[:, b, :, :], 4, None, ALU.logical_shift_right))
            m2 = dve.do(lambda e: e.tensor_scalar(half_u[1][:], pos[:, b, :, :], 15, None, ALU.bitwise_and))
            yield
            iota = row("iota")[:, 0:TOPK].unsqueeze(1).broadcast_to([P, TOPK, TOPK])
            for i in range(2):
                for h in range(PH):
                    m = dve.do(lambda e, i=i, h=h: e.tensor_tensor(
                        eq[:, h, :, :], half_u[i][:, h, :].unsqueeze(2).broadcast_to([P, TOPK, TOPK]), iota,
                        ALU.is_equal), m1, m2)
                    if h % 4 == 3:
                        yield
                for h in range(PH):
                    m = dve.do(lambda e, i=i, h=h: e.tensor_tensor(
                        eq[:, h, :, :], eq[:, h, :, :],
                        idx[:, b, 2 * h + i:2 * h + i + 1, :].broadcast_to([P, TOPK, TOPK]), ALU.mult))
                    if h % 4 == 3:
                        yield
                m = dve.do(lambda e, i=i: e.tensor_reduce(
                    picked[:, b, i, :].rearrange("p (h k) -> p h k", h=PH), eq[:], AX.X, ALU.add))
                yield
            m = dve.do(lambda e: e.tensor_reduce(tot, g, AX.X, ALU.add), k)
            m = dve.do(lambda e: e.reciprocal(rec, tot))
            picked_of[b].append(dve.do(lambda e: e.tensor_tensor(
                g, g, rec.unsqueeze(2).broadcast_to([P, PH, TOPK]), ALU.mult)))
            yield

        best_of, g_first = [[], []], []
        picked_of = [[], []]
        qp_free = [[gone], [gone]]

        q_in, routed0 = {}, {}

        def take_pq(n, ps, m):
            q_in[n] = act.do(lambda e: e.activation(qp[n % 2][:], ps, ACT.Copy), m, qp_free[n % 2])
            return [q_in[n]]

        def score_half(n):
            q, i = qp[n % 2], take("side")
            pe_wait_bank(i)
            pe.wait(q_in[n], subk_in)
            for b in range(NB):
                fn = lambda e, b=b: e.matmul(psum[i][:, b * P:(b + 1) * P], q[:, b * P:(b + 1) * P],
                                             sub_k[:, n, :], start=True, stop=True)
                k = pe.do(fn) if b else pe.quiet(fn)
            qp_free[n % 2] = [k]
            act.do(lambda e: e.activation(scores0[:, n % 2, :], psum[i][:, 0:P], ACT.Copy), k, gone,
                   routed0.get(n - 2))
            c = act.do(lambda e: e.activation(scores1[:, n, :], psum[i][:, P:2 * P], ACT.Copy), k, gone)
            bank_free[i] = [c]
            score_marks[n] = c

        def route_0(n):
            routed0[n] = route_half(0, n)
            if n % 2:
                route_head(0, n // 2)

        for n, _ in enumerate(gemm_cols(ws, h_hi, h_lo, f_ready, KT, 2 * PH, take_pq)):
            if n > 0:
                score_half(n - 1)
            if n > 1:
                route_0(n - 2)
        score_half(2 * PH - 1)
        route_0(2 * PH - 2)
        route_0(2 * PH - 1)
        scored = pe.mark()

        g_out_sem = [[sem(f"g_out{i}"), 0] for i in range(2)]
        xn_gone, turned = f_ready, {}
        stage_free = [[xn_gone], [xn_gone]]
        g_written, hot_free = [], [[xn_rows, scored] for _ in hot1]

        def turn_choices(b):
            i = take("side")
            pe_wait_bank(i)
            pe.wait(picked_of[b])
            for k in range(3):
                fn = lambda e, k=k: e.transpose(psum[i][:, k * P:(k + 1) * P], picked[:, b, k, :], ident[:])
                m = pe.do(fn) if k == 2 else pe.quiet(fn)
            turned[b] = act.do(lambda e: e.activation(
                by_choice[:, :, b * P:(b + 1) * P], psum[i][:, 0:3 * P].rearrange("p (k q) -> p k q", q=P),
                ACT.Copy), m, scored, list(routed0.values()))
            bank_free[i] = [turned[b]]

        def build_g(b):
            turn_choices(b)
            yield
            iota, hots = row("iota"), {}

            def make_hots(t):
                h = t % N_HOT
                m1 = dve.do(lambda e: e.tensor_scalar(
                    hot1[h][:], iota, by_choice[:, 0, t:t + 1], by_choice[:, 2, t:t + 1],
                    ALU.is_equal, ALU.mult), turned[b], hot_free[h])
                engine = dve if b == 1 and t % 2 else pool
                m2 = engine.do(lambda e: e.tensor_scalar(
                    hot2[h][:], iota, by_choice[:, 1, t:t + 1], None, ALU.is_equal), turned[b], hot_free[h])
                hots[t] = [m1, m2]

            def product(t4):
                i, s, at_t = take("side"), t4 // PT % 2, t4 % PT
                pe_wait_bank(i)
                pe.wait(hots[t4 + 2], hots[t4 + 3])
                for k in range(4):
                    h = (t4 + k) % N_HOT
                    fn = lambda e, h=h, k=k: e.matmul(
                        psum[i][:, k * P:(k + 1) * P], hot2[h][:], hot1[h][:], start=True, stop=True)
                    m = pe.do(fn) if k == 3 else pe.quiet(fn)
                for k in range(4):
                    hot_free[(t4 + k) % N_HOT] = [m]
                a = act.do(lambda e: e.activation(
                    stage[s][:, :, at_t:at_t + 4, :].rearrange("p a t j -> p t a j"),
                    psum[i][:].rearrange("p (t a j) -> p t a j", t=4, a=PARTS), ACT.Copy), m, stage_free[s])
                bank_free[i] = [a]
                if at_t + 4 == PT:
                    t0 = t4 + 4 - PT
                    w = sp.dma(G_dram[:, :, t0:t0 + PT, :].rearrange("a p t j -> p a t j"), stage[s][:],
                               g_out_sem[s], a)
                    stage_free[s] = [w]
                    g_written.append(w)

            for step in range(P // 8 + 1):
                t = b * P + 8 * step
                if step:
                    product(t - 8)
                    product(t - 4)
                if step < P // 8:
                    for k in range(8):
                        make_hots(t + k)
                yield

        def both_g():
            yield from build_g(0)
            while not picked_of[1]:
                yield
            for i, _ in enumerate(build_g(1)):
                if i % 2:
                    yield
            g_first.append(load_g(0, g_written))

        def choices():
            yield from pick_choices(0)
            side.add(both_g(), delay=1)
            for h in range(PH):
                for n in (2 * h, 2 * h + 1):
                    route_half(1, n)
                    yield
                route_head(1, h)
                yield
            yield from pick_choices(1)

        ROUTE_RATE = 2
        g_in_sem = [sem("g_in"), 0]
        acts_done = [[], []]

        def load_g(p, *after):
            return sp.dma(g_part[:].rearrange("p t j -> p (t j)"),
                          G_dram[p].rearrange("p t j -> p (t j)"), g_in_sem, *after)

        def gate_steps(p, g_in, dst, free):
            a_p = acts[p % 2]
            for g in range(PT // 4):
                t4 = slice(4 * g, 4 * g + 4)
                m = dve.do(lambda e, t4=t4: e.tensor_tensor(
                    a_p[:, t4, :], a_p[:, t4, :], g_part[:, :, t4].rearrange("p t j -> p j t"), ALU.mult),
                    g_in, acts_done[p % 2])
                a = act.do(lambda e, t4=t4: e.activation(dst[0][:, t4, :], a_p[:, t4, :], ACT.Copy), m, free)
                d = dve.do(lambda e, t4=t4: e.tensor_tensor(
                    dst[1][:, t4, :], a_p[:, t4, :], dst[0][:, t4, :].bitcast(F32), ALU.subtract), a, free)
                gated[p].put(g, d)
                g_read[p] = m
                acts_free[p % 2] = [a, d]
                yield

        gated, g_read = {p: Ready() for p in range(PARTS)}, {}

        def u_products(p, gating):
            def take_u(n, ps, m):
                if p == 1 and n >= PT // 2:
                    assert picked_of[1]
                    acts_free[1] = [gone, picked_of[1]]
                m = act.do(lambda e: e.activation(acts[p % 2][:, n, :], ps, ACT.Gelu_apprx_tanh), m,
                           acts_free[p % 2])
                acts_done[p % 2].append(m)
                return [m]

            next(gating, None)
            acts_done[p % 2] = []
            for n, _ in enumerate(gemm_cols(ws, h_hi, h_lo, f_ready, KT, PT, take_u)):
                side.step()
                if n % 4 == 3:
                    next(gating, None)

        side.add(choices(), rate=ROUTE_RATE)
        u_products(0, iter(()))
        u_products(1, iter(()))
        side.finish()
        g_in = g_first[0]
        routing_gone = [pe.mark(), act.mark(), dve.mark(), pool.mark()]

        gf_row = at("gf_row", PH0 + 32 * KB, [P, D])
        junk = at("junk", PH0 + 40 * KB, [P, BANK])
        gf_sem = [sem("g_final_in"), 0]
        gain_next = load_gain("g_mix_2", routing_gone)
        sx, sy = [columns(4) for _ in range(NB)], [columns(4) for _ in range(NB)]
        squared = [[], []]

        def take_v(n, b, ps, m):
            return add_to_x(n, b, ps, m)

        def take_last_v(n, b, ps, m):
            cut = QUARTERS[n]
            added = add_to_x(n, b, ps, m)
            m = square_of(b, n, sx[b], added, g_read[PARTS - 1])
            m = dve.do(lambda e: e.tensor_tensor(x[:, b, cut], x[:, b, cut], gf_row[:, cut], ALU.mult), m, gf_in)
            squared[b].append(act.do(lambda e: e.activation(junk[:], x[:, b, cut], ACT.Square,
                                                            accum_out=sy[b][:, n:n + 1]), m, junk_free))
            return added

        hid_of = [hid_e] * PARTS
        hid_of[PARTS - 2] = [h_hi, h_lo]
        hid_free = routing_gone
        gating = gate_steps(0, g_in, hid_of[0], hid_free)
        for p in range(PARTS):
            if p + 2 < PARTS:
                u_products(p + 2, gating)
                for _ in gating:
                    pass
            u_end, v_before = pe.mark(), hid_free
            if p + 1 < PARTS:
                g_in = load_g(p + 1, g_read[p])
            if p + 3 == PARTS:
                side.add(gate_steps(p + 1, g_in, hid_of[p + 1], u_end))
            elif p + 2 == PARTS:
                side.add(gate_steps(p + 1, g_in, hid_of[p + 1], v_before))
                junk_free = acts_free[0]
                gf_in = sp.dma(gf_row[:], A["g_final"], gf_sem, junk_free)
            side.beside(gemm_rows(ws, *hid_of[p], gated[p], PT, D // BANK, take_last_v if p + 1 == PARTS else take_v))
            side.finish()
            hid_free = [pe.mark()]
            if p + 3 < PARTS:
                gating = gate_steps(p + 1, g_in, hid_of[p + 1], hid_free)

        h_ready = Ready()
        scale, r1 = {}, []
        means = []
        for b in range(NB):
            tx, ty = columns(1), columns(1)
            m = dve.do(lambda e, b=b, tx=tx: e.tensor_reduce(tx, sx[b], AX.X, ALU.add), squared[b])
            r1.append(power_mean(tx, 1, D, m))
            means.append((ty, dve.do(lambda e, b=b, ty=ty: e.tensor_reduce(ty, sy[b], AX.X, ALU.add), squared[b])))
        for b in range(NB):
            (ty, m), (r, m1), ty_r = means[b], r1[b], columns(1)
            m = dve.do(lambda e, ty=ty, ty_r=ty_r, r=r: e.scalar_tensor_tensor(
                out=ty_r, in0=ty, scalar=r, in1=r, op0=ALU.mult, op1=ALU.mult), m, m1)
            scale[b] = power_mean(ty_r, 1, D, m)

        def renew_x(b, q):
            r, m = r1[b]
            cut = QUARTERS[q]
            return act.do(lambda e: e.activation(x[:, b, cut], x[:, b, cut], ACT.Copy, scale=r), m)

        rows_to_columns(scale, gain_next, h_ready, h_hi, h_lo, before=renew_x, free=[pe.mark()])

        everything = [pe.mark(), dve.mark(), act.mark()]
        for e in (act, dve, pool):
            e.wait(everything)
        small_at[0] = 0
        rope_in = sp.dma(rope_t[:], A["rope2"], const_sem, everything)

        PA = PH0
        lat_hi = at("lat_hi", PA, [P, 2 * QLT, S], F32R)
        lat_lo = at("lat_lo", PA + 8 * KB, [P, 2 * QLT, S], F32R)
        q2_rows = at("q2_rows", PA + 16 * KB, [P, NB, H2, NOPE])
        kn_rows = at("kn_rows", PA + 24 * KB, [P, NB, H2, NOPE])
        v2_rows = at("v2_rows", PA + 32 * KB, [P, NB, H2, VD])
        qr_rows = at("qr_rows", PA + 40 * KB, [P, NB, H2, ROPE])
        kr_cols = at("kr_cols", PA + 44 * KB, [P, S])
        kr_rows = at("kr_rows", PA + 45 * KB, [P, NB, 2, ROPE])
        qr_cols = at("qr_cols", PA + 46 * KB, [P, H2 // 2, S])
        g_lat = at("g_lat", PA + 58 * KB, [P, 2 * QL])
        lat_rows = at("lat_rows", SCR, [P, NB, 2, QL])
        sq_tmp = at("sq_tmp", SCR + 8 * KB, [P, BANK])
        nt_tmp = at("nt_tmp", SCR + 10 * KB, [P, BANK])
        rt_tmp = [at(f"rt_tmp{i}", SCR + 12 * KB + 2 * KB * i, [P, 8, 64]) for i in range(2)]
        dv_rows = at("dv_rows", SCR + 16 * KB, [P, NB, H2, 128])

        tmp_free = [h_ready]

        def head_norm(src, heads, width, gain_name, dst, ready):
            n = heads * width
            ss = columns(heads)
            if heads == 4:
                for h in range(heads):
                    a = act.do(lambda e, h=h: e.activation(sq_tmp[:, 0:width], src[:, h, :], ACT.Square,
                                                           accum_out=ss[:, h:h + 1]), ready, tmp_free[0])
                r, m = power_mean(ss, heads, width, a)
                for h in range(heads):
                    d = dve.do(lambda e, h=h: e.scalar_tensor_tensor(
                        out=dst[:, h, :], in0=src[:, h, :], scalar=r[:, h:h + 1], in1=row(gain_name),
                        op0=ALU.mult, op1=ALU.mult), m, a, ready)
                return d, d
            sq = sq_tmp[:, 0:n].rearrange("p (h w) -> p h w", h=heads)
            nt = nt_tmp[:, 0:n].rearrange("p (h w) -> p h w", h=heads)
            a = act.do(lambda e: e.activation(sq, src, ACT.Square), ready, tmp_free[0])
            m = dve.do(lambda e: e.tensor_reduce(ss, sq, AX.X, ALU.add), a)
            c = dve.do(lambda e: e.tensor_tensor(nt, src, row(gain_name).unsqueeze(1).broadcast_to(
                [P, heads, width]), ALU.mult), a, consts_in)
            r, m = power_mean(ss, heads, width, m)
            d = dve.do(lambda e: e.tensor_tensor(dst, nt, r.unsqueeze(2).broadcast_to([P, heads, width]),
                                                 ALU.mult), m, c)
            tmp_free[0] = [d]
            return c, d

        lat_marks = [[], []]

        def take_lat(n, b, ps, m):
            ss = columns(1)
            a = act.do(lambda e: e.activation(sq_tmp[:], ps, ACT.Square, accum_out=ss), m, tmp_free[0])
            r, k = power_mean(ss, 1, QL, a)
            d = dve.do(lambda e: e.scalar_tensor_tensor(
                out=lat_rows[:, b, n, :], in0=ps, scalar=r, in1=g_lat[:, n * QL:(n + 1) * QL],
                op0=ALU.mult, op1=ALU.mult), k, lat_gain)
            lat_marks[b].append(d)
            return [a, d]

        lat_gain = sp.dma(g_lat[:], A["g_lat"], gain_sem, everything)
        for _ in gemm_rows(ws, h_hi, h_lo, h_ready, KT, 2, take_lat):
            pass

        kr_marks = [[], []]

        def take_kr(n, b, ps, m):
            c, d = head_norm(ps.rearrange("p (h w) -> p h w", h=1), 1, ROPE, "g_k_rope_2",
                             kr_rows[:, b, 0:1, :], m)
            _, r = rope_rows(kr_rows[:, b, 0:1, :], kr_rows[:, b, 1:2, :], 1, b, [t[:, 0:1, :] for t in rt_tmp],
                             [d, rope_in])
            r = dve.do(lambda e: e.tensor_copy(kr_rows[:, b, 0:1, :], kr_rows[:, b, 1:2, :]), r)
            kr_marks[b].append(r)
            return [c]

        for _ in gemm_rows(ws, h_hi, h_lo, h_ready, KT, 1, take_kr, width=ROPE):
            pass

        dil_marks = {"q": [[], []], "k": [[], []], "v": []}

        def take_dv(n, b, ps, m):
            d = act.do(lambda e: e.activation(dv_rows[:, b, 4 * n:4 * n + 4, :].rearrange("p h w -> p (h w)"),
                                              ps, ACT.Copy), m, everything)
            dil_marks["v"].append(d)
            return [d]

        lat_ready, kr_ready = Ready(), Ready()
        side.add(flip_steps(lat_ready, lambda b, t: lat_rows[:, b, t // QLT, (t % QLT) * P:(t % QLT + 1) * P],
                            lat_hi, lat_lo, 2 * QLT, lat_marks, free=everything))
        side.add(flip_steps(kr_ready, lambda b, t: kr_rows[:, b, :, :].rearrange("p a d -> p (a d)"), None, None, 1,
                            kr_marks, free=everything, plain=kr_cols[:].unsqueeze(1)))
        dv_product = gemm_rows(ws, h_hi, h_lo, h_ready, KT, 2, take_dv)
        for _ in range(4):
            next(dv_product)
            side.step()
        side.finish()

        mla_marks = {"qn": [[], []], "qr": [[], []], "kn": [[], []], "v": []}

        def take_uq(n, b, ps, m):
            if n < 2:
                c, d = head_norm(ps.rearrange("p (h w) -> p h w", h=4), 4, NOPE, "g_q_nope_2",
                                 q2_rows[:, b, 4 * n:4 * n + 4, :], m)
                mla_marks["qn"][b].append(d)
                return [c]
            c, d = head_norm(ps.rearrange("p (h w) -> p h w", h=8), 8, ROPE, "g_q_rope_2", qr_rows[:, b, :, :], m)
            _, r = rope_rows(qr_rows[:, b, :, :], qr_rows[:, b, :, :], 8, b, [t[:] for t in rt_tmp], [d, rope_in])
            mla_marks["qr"][b].append(r)
            return [c]

        def take_ukv(n, b, ps, m):
            if n < 2:
                c, d = head_norm(ps.rearrange("p (h w) -> p h w", h=4), 4, NOPE, "g_k_nope_2",
                                 kn_rows[:, b, 4 * n:4 * n + 4, :], m)
                mla_marks["kn"][b].append(d)
                return [c]
            d = act.do(lambda e: e.activation(
                v2_rows[:, b, 4 * (n - 2):4 * (n - 2) + 4, :].rearrange("p h w -> p (h w)"), ps, ACT.Copy), m)
            mla_marks["v"].append(d)
            return [d]

        lat_ready_kv = Ready()
        for m in lat_ready:
            lat_ready_kv.put(0, m)
        uq = gemm_rows(ws, lat_hi[:, 0:QLT, :], lat_lo[:, 0:QLT, :], lat_ready, QLT, 3, take_uq, kind="side")
        ukv = gemm_rows(ws, lat_hi[:, QLT:2 * QLT, :], lat_lo[:, QLT:2 * QLT, :], lat_ready_kv, QLT, 4, take_ukv,
                        kind="side")
        for turn_of in LATENT_ORDER:
            next({"d": dv_product, "q": uq, "k": ukv}[turn_of], None)

        lat_gone = [pe.mark()]
        qn_cols = at("qn_cols", PA, [P, H2, S])
        kn_cols = at("kn_cols", PA + 8 * KB, [P, H2, S])
        mla_ready, q2_flipped, kn_flipped = Ready(), Ready(), Ready()

        def mla_flips():
            yield from flip_steps(q2_flipped, lambda b, t: q2_rows[:, b, t, :], None, None, H2, mla_marks["qn"],
                                  free=lat_gone, plain=qn_cols)
            yield from flip_steps(kn_flipped, lambda b, t: kn_rows[:, b, t, :], None, None, H2, mla_marks["kn"],
                                  free=lat_gone, plain=kn_cols)
            yield from flip_steps(mla_ready, lambda b, t: qr_rows[:, b, 2 * t:2 * t + 2, :].rearrange(
                "p a d -> p (a d)"), None, None, H2 // 2, mla_marks["qr"], plain=qr_cols)
            mla_ready.extend([q2_flipped, kn_flipped, kr_ready, mla_marks["v"]])
            side.add(attention_mla(0))
            side.add(attention_mla(1), delay=2)

        dq_rows = at("dq_rows", PA + 16 * KB, [P, NB, H2, 128])
        dk_rows = at("dk_rows", PA + 24 * KB, [P, NB, H2, 128])
        o2_rows = at("o2_rows", SCR, [P, NB, H2, VD])
        s2_buf = [at(f"s2_buf{b}", a, [P, 4, S]) for b, a in enumerate((PA + 50 * KB, PA + 58 * KB))]
        pt2_buf = [at(f"pt2_buf{b}", a, [P, 4, 2, P]) for b, a in enumerate((PA + 54 * KB, SCR + 12 * KB))]
        mla = [{"s_free": [], "pt_free": [], "out": [], "out_free": [lat_ready]} for _ in range(NB)]

        def attention_mla(b):
            scale = (NOPE + ROPE) ** -0.5
            for g in range(H2 // 4):
                def score(j, ps, g=g):
                    hh = 4 * g + j
                    at_p = slice(ROPE * (hh % 2), ROPE * (hh % 2) + ROPE)
                    tok = slice(b * P, (b + 1) * P)
                    pe.quiet(lambda e: e.matmul(ps, qn_cols[:, hh, tok], kn_cols[:, hh, :], start=True, stop=False))
                    return lambda e: e.matmul(ps, qr_cols[at_p, hh // 2, tok], kr_cols[at_p, :],
                                              start=False, stop=True)

                def bias(sb, pair, ps, m, free):
                    return dve.do(lambda e: e.tensor_scalar(
                        sb[:, pair::2, :], ps[:].rearrange("p (j s) -> p j s", j=2),
                        scale, None, ALU.mult), m, free)

                yield from attention(score, bias, None,
                                     lambda j, kb, g=g: v2_rows[:, kb, 4 * g + j, :], VD,
                                     o2_rows[:, b, 4 * g:4 * g + 4, :], s2_buf[b], pt2_buf[b], mla[b], mla_ready)

        def take_dil(n, b, ps, m):
            which, part = n // 2, n % 2
            dst = (dq_rows, dk_rows)[which][:, b, 4 * part:4 * part + 4, :]
            flipped = (q2_flipped, kn_flipped)[which]
            assert len(flipped) == 4
            c, d = head_norm(ps.rearrange("p (h w) -> p h w", h=4), 4, 128, ("g_q_dil_2", "g_k_dil_2")[which],
                             dst, [m, flipped])
            dil_marks["qk"[which]][b].append(d)
            return [c]

        side.add(mla_flips(), rate=2)
        side.beside(gemm_rows(ws, h_hi, h_lo, h_ready, KT, 4, take_dil))
        side.finish()

        om_hi = at("om_hi", PA, [P, H2, S], F32R)
        om_lo = at("om_lo", PA + 8 * KB, [P, H2, S], F32R)
        mla_gone = [pe.mark()]
        dk_cols = at("dk_cols", PA + 32 * KB, [P, H2, S])
        dq_cols = at("dq_cols", PA + 40 * KB, [P, H2, S])
        g_cols = at("g_cols", PA + 16 * KB, [P, KT, S])
        dil_ready, om_ready = Ready(), Ready()
        for _ in flip_steps(dil_ready, lambda b, t: dq_rows[:, b, t, :], None, None, H2, dil_marks["q"],
                            free=mla_gone, plain=dq_cols):
            pass
        dist = at("dist", SCR + 8 * KB, [P, 2, 384])
        dist_sem = [sem("dist_in"), 0]
        dist_in = sp.dma(dist[:], A["dist"], dist_sem, dve.mark(), act.mark())
        dil = [{"s_free": mla[b]["s_free"], "pt_free": mla[b]["pt_free"], "out": [], "out_free": [om_ready]}
               for b in range(NB)]

        def dil_flips():
            yield from flip_steps(dil_ready, lambda b, t: dk_rows[:, b, t, :], None, None, H2, dil_marks["k"],
                                  free=mla_gone, plain=dk_cols)
            yield from flip_steps(om_ready, lambda b, t: o2_rows[:, b, t, :], om_hi, om_lo, H2,
                                  [mla[0]["out"], mla[1]["out"]], free=mla_gone)
            dil_ready.extend(dil_marks["v"])
            side.add(attention_dil(0))
            side.add(attention_dil(1), delay=2)

        def attention_dil(b):
            for g in range(H2 // 4):
                def score(j, ps, g=g):
                    hh = 4 * g + j
                    return lambda e: e.matmul(ps, dq_cols[:, hh, b * P:(b + 1) * P], dk_cols[:, hh, :],
                                              start=True, stop=True)

                def bias(sb, pair, ps, m, free, g=g):
                    cut = slice((1 - b) * P, (1 - b) * P + S)
                    for j in (pair, pair + 2):
                        slope = 2.0 ** (-8.0 * (4 * g + j + 1) / H2)
                        k = dve.do(lambda e, j=j, slope=slope: e.scalar_tensor_tensor(
                            out=sb[:, j, :], in0=dist[:, 0, cut], scalar=-slope, in1=dist[:, 1, cut],
                            op0=ALU.mult, op1=ALU.add), free, dist_in)
                    return dve.do(lambda e: e.scalar_tensor_tensor(
                        out=sb[:, pair::2, :], in0=ps[:].rearrange("p (j s) -> p j s", j=2),
                        scalar=128 ** -0.5, in1=sb[:, pair::2, :], op0=ALU.mult, op1=ALU.add), m, k)

                yield from attention(score, bias, None,
                                     lambda j, kb, g=g: dv_rows[:, kb, 4 * g + j, :], 128,
                                     o2_rows[:, b, 4 * g:4 * g + 4, :], s2_buf[b], pt2_buf[b], dil[b], dil_ready)

        def take_g0(n, ps, m):
            if n == H2:
                assert len(dil_ready) >= 8
            m = act.do(lambda e: e.activation(g_cols[:, n, :], ps, ACT.Identity, bias=col("b_gate_2", n)),
                       m, list(dil_ready))
            g0_marks.append(m)
            return [m]

        def take_ya(n, ps, m):
            m = dve.do(lambda e: e.tensor_tensor(g_cols[:, n, :], ps, g_cols[:, n, :], ALU.mult), m, g0_sig)
            z_marks[n] = m
            return [m]

        g0_marks, z_marks, g0_sig = [], {}, []
        side.add(dil_flips(), rate=2)
        side.beside(gemm_cols(ws, h_hi, h_lo, h_ready, KT, KT, take_g0))
        g0_sig.append(act.do(lambda e: e.activation(g_cols[:], g_cols[:], ACT.Sigmoid), g0_marks))
        side.beside(gemm_cols(ws, om_hi, om_lo, om_ready, H2, KT, take_ya))
        side.finish()

        od_hi = at("od_hi", PA + 32 * KB, [P, H2, S], F32R)
        od_lo = at("od_lo", PA + 40 * KB, [P, H2, S], F32R)
        att_gone = [pe.mark()]
        od_ready = Ready()
        side.add(flip_steps(od_ready, lambda b, t: o2_rows[:, b, t, :], od_hi, od_lo, H2,
                            [dil[0]["out"], dil[1]["out"]], free=att_gone))
        g1_cols = at("g1_cols", SCR + 8 * KB, [P, KT, S])
        g1_marks, z_ready = [], Ready()

        def take_g1(n, ps, m):
            g1_marks.append(act.do(lambda e: e.activation(g1_cols[:, n, :], ps, ACT.Sigmoid,
                                                          bias=col("b_gate_2", KT + n)), m, att_gone, dil_read))
            return [g1_marks[n]]

        def take_yb(n, ps, m):
            m = dve.do(lambda e: e.tensor_tensor(g1_cols[:, n, :], ps, g1_cols[:, n, :], ALU.mult), m, g1_marks[n])
            k = dve.do(lambda e: e.tensor_tensor(g_cols[:, n, :], g_cols[:, n, :], g1_cols[:, n, :], ALU.add),
                       m, z_marks[n])
            a = act.do(lambda e: e.activation(h_hi[:, n, :], g_cols[:, n, :], ACT.Copy), k, h_free)
            z_ready.put(n // 4, dve.do(lambda e: e.tensor_tensor(
                h_lo[:, n, :], g_cols[:, n, :], h_hi[:, n, :].bitcast(F32), ALU.subtract), a, h_free))
            return [m]

        dil_read = [dve.mark()]
        side.beside(gemm_cols(ws, h_hi, h_lo, h_ready, KT, KT, take_g1))
        side.finish()
        h_free = [pe.mark()]
        for _ in gemm_cols(ws, od_hi, od_lo, od_ready, H2, KT, take_yb):
            pass
        gone = [act.mark(), dve.mark(), pe.mark()]
        gain = load_gain("g_ffn_2", gone)
        sums, squared = [columns(4) for _ in range(NB)], [[], []]
        for _ in gemm_rows(ws, h_hi, h_lo, z_ready, KT, D // BANK, add_and_square(sums, squared, gone)):
            pass

        h_free = [pe.mark()]
        gone = [pe.mark(), dve.mark(), act.mark()]
        f_ready = Ready()
        norm_to_columns(sums, squared, gain, f_ready, h_hi, h_lo, free=h_free)
        hid_hi = at("hid_hi", PA, [P, FF_PARTS[0], S], F32R)
        hid_lo = at("hid_lo", PA + 24 * KB, [P, FF_PARTS[0], S], F32R)
        g_tmp = [at(f"silu_tmp{i}", PA + 48 * KB + KB * i, [P, S]) for i in range(4)]
        hid_free = gone
        g_free = [[gone] for _ in g_tmp]
        out_sem = [sem("out_done"), 0]
        for part, tiles in enumerate(FF_PARTS):
            hid_ready, silu_marks = Ready(), {}

            def take_gu(n, ps, m):
                i, s = n // 2, (n // 2) % 4
                if n % 2 == 0:
                    silu_marks[i] = act.do(lambda e: e.activation(g_tmp[s][:], ps, ACT.Silu), m, g_free[s])
                    return [silu_marks[i]]
                d = dve.do(lambda e: e.tensor_tensor(g_tmp[s][:], ps, g_tmp[s][:], ALU.mult), m, silu_marks[i])
                a = act.do(lambda e: e.activation(hid_hi[:, i, :], g_tmp[s][:], ACT.Copy), d, hid_free)
                k = dve.do(lambda e: e.tensor_tensor(hid_lo[:, i, :], g_tmp[s][:], hid_hi[:, i, :].bitcast(F32),
                                                     ALU.subtract), a, hid_free)
                g_free[s] = [a, k]
                hid_ready.put(i // 4, k)
                return [d]

            for _ in gemm_cols(ws, h_hi, h_lo, f_ready, KT, 2 * tiles, take_gu):
                pass

            def to_x(n, b, ps, m):
                cut = slice(n * BANK, (n + 1) * BANK)
                m = dve.do(lambda e: e.tensor_tensor(x[:, b, cut], ps, x[:, b, cut], ALU.add), m)
                if part == len(FF_PARTS) - 1:
                    sp.dma(out[b * P:(b + 1) * P, cut], x[:, b, cut], out_sem, m)
                return [m]

            for _ in gemm_rows(ws, hid_hi, hid_lo, hid_ready, tiles, D // BANK, to_x):
                pass
            hid_free = [pe.mark()]
        sp.wait((out_sem[0], out_sem[1]))

        block = ctx.enter_context(nc.Block())

        @block.sync
        def _(e):
            sp.play(e)

        @block.scalar
        def _(e):
            act.play(e)

        @block.vector
        def _(e):
            dve.play(e)

        @block.gpsimd
        def _(e):
            pool.play(e)

        @block.tensor
        def _(e):
            pe.play(e)


def chunks_rows(w, width=BANK):
    k, n = w.shape
    per = WCH // width
    kt = k // P
    per = min(per, kt)
    w = w.reshape(kt // per, per, P, n // width, width).transpose(3, 0, 2, 1, 4)
    return np.ascontiguousarray(w).reshape(-1, P, per * width)


def chunks_cols(w):
    k, n = w.shape
    kt = k // P
    per = WCH // (P * kt)
    w = w.reshape(kt, P, n // (P * per), per, P).transpose(2, 1, 3, 0, 4)
    return np.ascontiguousarray(w).reshape(-1, P, WCH)


def columns_of(v):
    return np.ascontiguousarray(v.reshape(-1, P).T)


def layout(i):
    f = np.float32
    c = {}
    x = i["x"].reshape(NB, P, D)
    c["x"] = np.ascontiguousarray(x.transpose(1, 0, 2))
    c["ident"] = np.eye(P, dtype=f)
    col = {n: columns_of(i[n][0]) for n, _ in COLS}
    c["cols"] = np.ascontiguousarray(np.concatenate([col[n] for n, _ in COLS], axis=1))
    row = {n: i[n][0] for n, _ in ROWS if n != "iota"}
    row["iota"] = np.arange(N_KEYS, dtype=f)
    c["rows"] = np.ascontiguousarray(np.broadcast_to(np.concatenate([row[n] for n, _ in ROWS]), (P, N_ROWS)))

    def every_partition(v):
        return np.ascontiguousarray(np.broadcast_to(v, (P, D)))

    for n in ("g_mix", "g_ffn", "g_mix_2", "g_ffn_2"):
        c[n] = every_partition(i[n][0])
    c["g_final"] = every_partition(i["g_final"])
    c["g_attn_out"] = np.ascontiguousarray(np.broadcast_to(i["g_attn_out"][0], (P, AW)))
    c["g_lat"] = np.ascontiguousarray(np.broadcast_to(
        np.concatenate([i["g_cq_2"][0], i["g_ckv_2"][0]]), (P, 2 * QL)))

    pos = np.arange(S, dtype=f)[:, None]
    def table(inv):
        ang = pos * inv[None, :]
        cos, sin = np.cos(ang).astype(f), np.sin(ang).astype(f)
        t = np.stack([np.concatenate([cos, cos], 1), np.concatenate([-sin, sin], 1)], 1)
        return np.ascontiguousarray(t.reshape(NB, P, 2, 64).transpose(1, 0, 2, 3))
    c["rope1"] = table((f(10000.0) ** (-np.arange(32, dtype=f) / f(32))).astype(f))
    c["rope2"] = table((f(10000.0) ** (-np.arange(0, 64, 2, dtype=f) / f(64))).astype(f))
    delta = np.arange(384)[None, :] - P - np.arange(P)[:, None]
    c["window"] = np.where(np.abs(delta) <= 128, 0.0, NEG).astype(f)
    count = (np.abs(delta) <= 64).astype(int) + (delta % 4 == 0) + (delta % 16 == 0)
    c["dist"] = np.ascontiguousarray(np.stack(
        [np.abs(delta).astype(f), np.where(count > 0, np.log(np.maximum(count, 1)), NEG).astype(f)], 1))

    w = i["w_in"][0]
    c["w1_qkv"] = chunks_rows(w[:, :1536])
    c["w1_gate"] = chunks_cols(w[:, 1536:2560])
    c["w1_rec"] = chunks_cols(w[:, 2560:3584])
    lru = np.zeros((LT, P, 4, P), f)
    for k, n in enumerate(("fwd_wa", "fwd_wx", "bwd_wa", "bwd_wx")):
        a = i[n][0]
        for t in range(LT):
            lru[t, 0:64, k, 0:64] = a[2 * t]
            lru[t, 64:128, k, 64:128] = a[2 * t + 1]
    c["lru_w"] = lru
    c["w1_out"] = chunks_rows(i["w_out"][0])
    c["w1_pq"] = chunks_cols(i["w_pq"][0])
    sk = np.stack([i["sub_k1"][0], i["sub_k2"][0]], 1)
    c["sub_k"] = np.ascontiguousarray(sk.reshape(2 * PH, N_KEYS, P).transpose(2, 0, 1))
    c["u_cols"] = chunks_cols(i["u_emb"][0].T)
    c["v_rows"] = chunks_rows(i["v_emb"][0])

    w = i["w_in_2"][0]
    c["w2_lat"] = chunks_rows(w[:, 0:1024])
    kr = w[:, 1024:1088].reshape(KT, P, ROPE).transpose(1, 0, 2)
    c["w2_kr"] = np.ascontiguousarray(kr).reshape(1, P, KT * ROPE)
    c["w2_dil"] = chunks_rows(w[:, 1088:4160])
    c["w2_gate"] = chunks_cols(w[:, 4160:])
    uq = i["w_uq_2"][0].reshape(QL, H2, NOPE + ROPE)
    c["w2_uq"] = chunks_rows(np.concatenate([uq[:, :, :NOPE].reshape(QL, -1), uq[:, :, NOPE:].reshape(QL, -1)], 1))
    ukv = i["w_ukv_2"][0].reshape(QL, H2, NOPE + VD)
    c["w2_ukv"] = chunks_rows(np.concatenate([ukv[:, :, :NOPE].reshape(QL, -1), ukv[:, :, NOPE:].reshape(QL, -1)], 1))
    c["w2_omla"] = chunks_cols(i["w_o_mla_2"][0])
    c["w2_odil"] = chunks_cols(i["w_o_dil_2"][0])
    c["w2_o"] = chunks_rows(i["w_o_2"][0])
    gu = i["w_gate_up_2"][0].reshape(D, 2, FT, P).transpose(0, 2, 1, 3).reshape(D, 2 * FF)
    c["w2_gu"] = chunks_cols(gu)
    c["w2_down"] = chunks_rows(i["w_down_2"][0])
    return {k: np.ascontiguousarray(v) for k, v in c.items()}


def program(nc, arrays):
    A = {n: nc.dram_tensor(f"in_{n}", a.shape, F32, kind="ExternalInput").ap() for n, a in arrays.items()}
    out = nc.dram_tensor("out", (S, D), F32, kind="ExternalOutput").ap()
    g_dram = nc.dram_tensor("expert_gates", (PARTS, P, S, PT), F32, kind="Internal").ap()
    build(nc, A, g_dram, out)


def kernel(**inputs):
    import concourse.bacc as bacc
    from concourse.bass_utils import run_bass_kernel_spmd

    arrays = layout({k: np.asarray(v) for k, v in inputs.items()})
    nc = bacc.Bacc("TRN2", target_bir_lowering=False, num_devices=1)
    program(nc, arrays)
    r = run_bass_kernel_spmd(nc, [{f"in_{n}": a for n, a in arrays.items()}], core_ids=[0])
    return r.results[0]["out"].reshape(1, S, D)
```
